# Optimizing a Trainium2 kernel written in Bass

```python
import math
import jax, jax.numpy as jnp
from jax import lax
import numpy as np

D_MODEL = 1024
BATCH = 1
SEQ = 128
DEPTH = 2
DEC_BATCH = 1
DEC_SEQ = 256
PAST_LEN = 128

GRID_W = 64
HEAD_DIM = 64
N_Q_HEADS = 8
N_KV_HEADS = 2
Q_PER_KV = N_Q_HEADS // N_KV_HEADS
Q_W = N_Q_HEADS * HEAD_DIM
KV_W = N_KV_HEADS * HEAD_DIM
CONV_CH = D_MODEL // 2
CONV_K = 31
CONV_PAD = CONV_K // 2
MIX_WIDTH = Q_W + CONV_CH
IN_COLS = Q_W + 2 * KV_W + 2 * CONV_CH
AXIS_PAIRS = HEAD_DIM // 4
ROPE_THETA = 10000.0
Q_BLOCK = 128
N_EXPERTS = 16
N_GROUPS = 4
EXPERTS_PER_GROUP = N_EXPERTS // N_GROUPS
TOP_K = 2
D_FF_EXPERT = 512
EPS = 1e-6

kernel_name = 'hybrid_diffusion_attn_conformer_moe_step'

def rms_norm(x, g):
    xf = x.astype(jnp.float32)
    y = xf * lax.rsqrt(jnp.mean(xf * xf, axis=-1, keepdims=True) + EPS)
    return (y * g.astype(jnp.float32)).astype(x.dtype)

def layer_norm(x, g, b):
    xf = x.astype(jnp.float32)
    mu = jnp.mean(xf, axis=-1, keepdims=True)
    var = jnp.mean(jnp.square(xf - mu), axis=-1, keepdims=True)
    y = (xf - mu) * lax.rsqrt(var + EPS)
    return (y * g.astype(jnp.float32) + b.astype(jnp.float32)).astype(x.dtype)

def modulation(cvec, w_mod_l, b_mod_l):
    m = jax.nn.silu(cvec) @ w_mod_l + b_mod_l
    return m.reshape(cvec.shape[0], 6, D_MODEL)

def axial_rope_tables(n):
    rows = n // GRID_W
    r_idx, c_idx = jnp.meshgrid(jnp.arange(rows), jnp.arange(GRID_W), indexing='ij')
    r_idx = r_idx.reshape(-1).astype(jnp.float32)
    c_idx = c_idx.reshape(-1).astype(jnp.float32)
    freqs = ROPE_THETA ** (-jnp.arange(AXIS_PAIRS, dtype=jnp.float32) / AXIS_PAIRS)
    ang = jnp.stack([r_idx[:, None] * freqs, c_idx[:, None] * freqs], axis=1)
    return jnp.cos(ang), jnp.sin(ang)

def apply_rope(x, cos, sin):
    B, n, H, _ = x.shape
    xr = x.astype(jnp.float32).reshape(B, n, H, 2, 2, AXIS_PAIRS)
    x1, x2 = xr[..., 0, :], xr[..., 1, :]
    cb, sb = cos[None, :, None], sin[None, :, None]
    out = jnp.stack([x1 * cb - x2 * sb, x2 * cb + x1 * sb], axis=-2)
    return out.reshape(B, n, H, HEAD_DIM).astype(x.dtype)

def block_attention(q, k, v):
    B, Sq, _, _ = q.shape
    nb = Sq // Q_BLOCK
    scale = 1.0 / math.sqrt(HEAD_DIM)
    qb = q.reshape(B, nb, Q_BLOCK, N_KV_HEADS, Q_PER_KV, HEAD_DIM).swapaxes(0, 1)

    def one_block(qblk):
        s = jnp.einsum('bqhgd,bkhd->bhgqk', qblk, k, preferred_element_type=jnp.float32) * scale
        p = jax.nn.softmax(s, axis=-1).astype(v.dtype)
        return jnp.einsum('bhgqk,bkhd->bqhgd', p, v)

    o = lax.map(one_block, qb)
    return o.swapaxes(0, 1).reshape(B, Sq, Q_W)

def conv_module(u, dw_w, dw_b, ln_g, ln_b):
    a, b = jnp.split(u, 2, axis=-1)
    z = a * jax.nn.sigmoid(b)
    z = lax.conv_general_dilated(z, dw_w[:, None, :].astype(z.dtype), window_strides=(1,),
                                 padding=[(CONV_PAD, CONV_PAD)],
                                 dimension_numbers=('NWC', 'WIO', 'NWC'),
                                 feature_group_count=CONV_CH) + dw_b
    return jax.nn.silu(layer_norm(z, ln_g, ln_b))

def grouped_moe(h, w_router, b_router, w_gate, w_up, w_down):
    B, S, D = h.shape
    t = h.reshape(-1, D)
    T = t.shape[0]
    s = jax.nn.sigmoid((t @ w_router).astype(jnp.float32))
    sb = s + b_router.astype(jnp.float32)
    grp = sb.reshape(T, N_GROUPS, EXPERTS_PER_GROUP)
    gscore = lax.top_k(grp, 2)[0].sum(-1)
    gmask = jax.nn.one_hot(jnp.argmax(gscore, axis=-1), N_GROUPS, dtype=jnp.bool_)[:, :, None]
    masked = jnp.where(gmask, grp, -jnp.inf).reshape(T, N_EXPERTS)
    _, idx = lax.top_k(masked, TOP_K)
    w = jnp.take_along_axis(s, idx, axis=-1)
    w = w / jnp.sum(w, axis=-1, keepdims=True)
    gates = jnp.sum(jax.nn.one_hot(idx, N_EXPERTS, dtype=jnp.float32) * w[..., None], axis=1)
    hid = jax.nn.silu(jnp.einsum('td,edf->tef', t, w_gate)) * jnp.einsum('td,edf->tef', t, w_up)
    hid = hid * gates.astype(hid.dtype)[:, :, None]
    out = jnp.einsum('tef,efd->td', hid, w_down)
    return out.reshape(B, S, D)

def trunk_layer(x, mod, n1, n2, w_in, qg, kg, dw_w, dw_b, ln_g, ln_b, w_out,
                w_router, b_router, wg, wu, wd, rope=None, ctx_kv=None):
    sh1, sc1, g1, sh2, sc2, g2 = [mod[:, i][:, None, :] for i in range(6)]
    B, S, _ = x.shape
    h = rms_norm(x, n1) * (1.0 + sc1) + sh1
    proj = h @ w_in
    q, k, v, u = jnp.split(proj, [Q_W, Q_W + KV_W, Q_W + 2 * KV_W], axis=-1)
    q = rms_norm(q.reshape(B, S, N_Q_HEADS, HEAD_DIM), qg)
    k = rms_norm(k.reshape(B, S, N_KV_HEADS, HEAD_DIM), kg)
    v = v.reshape(B, S, N_KV_HEADS, HEAD_DIM)
    if rope is not None:
        q = apply_rope(q, rope[0], rope[1])
        k = apply_rope(k, rope[0], rope[1])
    if ctx_kv is not None:
        k_all = jnp.concatenate([ctx_kv[0].astype(k.dtype), k], axis=1)
        v_all = jnp.concatenate([ctx_kv[1].astype(v.dtype), v], axis=1)
    else:
        k_all, v_all = k, v
    attn = block_attention(q, k_all, v_all)
    conv = conv_module(u, dw_w, dw_b, ln_g, ln_b)
    x = x + g1 * (jnp.concatenate([attn, conv], axis=-1) @ w_out)
    h2 = rms_norm(x, n2) * (1.0 + sc2) + sh2
    x = x + g2 * grouped_moe(h2, w_router, b_router, wg, wu, wd)
    return x, k, v

def setup_inputs(seed: int = 0) -> dict:
    key = jax.random.key(seed)
    ks = jax.random.split(key, 24)
    f32 = jnp.float32
    nrm = lambda k, shape, s: jax.random.normal(k, shape, f32) * s
    return {
        'x_prompt': nrm(ks[0], (BATCH, SEQ, D_MODEL), 1.0),
        'x_sample': nrm(ks[1], (DEC_BATCH, DEC_SEQ, D_MODEL), 1.0),
        'cache_k': nrm(ks[2], (DEC_BATCH, DEPTH, PAST_LEN, N_KV_HEADS, HEAD_DIM), 1.0),
        'cache_v': nrm(ks[3], (DEC_BATCH, DEPTH, PAST_LEN, N_KV_HEADS, HEAD_DIM), 1.0),
        'c': nrm(ks[4], (DEC_BATCH, D_MODEL), 1.0),
        'c_ctx': nrm(ks[5], (D_MODEL,), 1.0),
        'w_mod': nrm(ks[6], (DEPTH, D_MODEL, 6 * D_MODEL), 0.5 * D_MODEL ** -0.5),
        'b_mod': nrm(ks[7], (DEPTH, 6 * D_MODEL), 0.02),
        'norm1_g': 1.0 + nrm(ks[8], (DEPTH, D_MODEL), 0.02),
        'norm2_g': 1.0 + nrm(ks[9], (DEPTH, D_MODEL), 0.02),
        'w_in': nrm(ks[10], (DEPTH, D_MODEL, IN_COLS), D_MODEL ** -0.5),
        'q_norm_g': 1.0 + nrm(ks[11], (DEPTH, HEAD_DIM), 0.02),
        'k_norm_g': 1.0 + nrm(ks[12], (DEPTH, HEAD_DIM), 0.02),
        'conv_dw_w': nrm(ks[13], (DEPTH, CONV_K, CONV_CH), CONV_K ** -0.5),
        'conv_dw_b': nrm(ks[14], (DEPTH, CONV_CH), 0.02),
        'conv_ln_g': 1.0 + nrm(ks[15], (DEPTH, CONV_CH), 0.02),
        'conv_ln_b': nrm(ks[16], (DEPTH, CONV_CH), 0.02),
        'w_out': nrm(ks[17], (DEPTH, MIX_WIDTH, D_MODEL), MIX_WIDTH ** -0.5),
        'w_router': nrm(ks[18], (D_MODEL, N_EXPERTS), D_MODEL ** -0.5),
        'b_router': nrm(ks[19], (N_EXPERTS,), 0.01),
        'w_gate': nrm(ks[20], (DEPTH, N_EXPERTS, D_MODEL, D_FF_EXPERT), D_MODEL ** -0.5),
        'w_up': nrm(ks[21], (DEPTH, N_EXPERTS, D_MODEL, D_FF_EXPERT), D_MODEL ** -0.5),
        'w_down': nrm(ks[22], (DEPTH, N_EXPERTS, D_FF_EXPERT, D_MODEL), D_FF_EXPERT ** -0.5),
    }

def reference(x_prompt, x_sample, cache_k, cache_v, c, c_ctx, w_mod, b_mod, norm1_g, norm2_g,
              w_in, q_norm_g, k_norm_g, conv_dw_w, conv_dw_b, conv_ln_g, conv_ln_b, w_out,
              w_router, b_router, w_gate, w_up, w_down):
    x = x_prompt
    ks_list, vs_list = [], []
    for l in range(DEPTH):
        mod = modulation(c_ctx[None, :], w_mod[l], b_mod[l])
        x, k, v = trunk_layer(x, mod, norm1_g[l], norm2_g[l], w_in[l], q_norm_g[l], k_norm_g[l],
                              conv_dw_w[l], conv_dw_b[l], conv_ln_g[l], conv_ln_b[l], w_out[l],
                              w_router, b_router, w_gate[l], w_up[l], w_down[l])
        ks_list.append(k)
        vs_list.append(v)
    y_prompt = x
    new_cache_k = jnp.stack(ks_list, axis=1)
    new_cache_v = jnp.stack(vs_list, axis=1)

    rope = axial_rope_tables(x_sample.shape[1])
    z = x_sample
    for l in range(DEPTH):
        mod = modulation(c, w_mod[l], b_mod[l])
        z, _, _ = trunk_layer(z, mod, norm1_g[l], norm2_g[l], w_in[l], q_norm_g[l], k_norm_g[l],
                              conv_dw_w[l], conv_dw_b[l], conv_ln_g[l], conv_ln_b[l], w_out[l],
                              w_router, b_router, w_gate[l], w_up[l], w_down[l],
                              rope=rope, ctx_kv=(cache_k[:, l], cache_v[:, l]))
    y_sample = z
    return (y_prompt, y_sample, new_cache_k, new_cache_v)


_drawn_inputs = setup_inputs


def setup_inputs(seed=0):
    import zlib

    import numpy as np

    out = dict(_drawn_inputs(seed))
    spreads = {}
    factors = {'norm1_g': 2.955,
     'q_norm_g': 8.0,
     'k_norm_g': 3.035,
     'conv_dw_b': 3.196,
     'conv_ln_g': 6.242,
     'conv_ln_b': 5.532,
     'cache_k': 8.0,
     'cache_v': 8.0}
    for name, (base, spread) in spreads.items():
        noise = np.random.default_rng([zlib.crc32(name.encode()), seed]).standard_normal(out[name].shape)
        drawn = base * np.exp(spread * noise) if base else spread * noise
        out[name] = __import__('jax').numpy.asarray(drawn.astype(out[name].dtype))
    for name, factor in factors.items():
        out[name] = (out[name] * factor).astype(out[name].dtype)
    return out
```

```python
from contextlib import ExitStack

import concourse.bass as bass
from concourse import mybir

ALU = mybir.AluOpType
ACT = mybir.ActivationFunctionType
AX = mybir.AxisListType
F32 = mybir.dt.float32
I32 = mybir.dt.int32
U32 = mybir.dt.uint32

P = 128
D = 1024
KD = D // P
LAYERS = 2
TILES = 3
HEADS, KV_HEADS, HD = 8, 2, 64
PAIRS = HEADS // KV_HEADS
QW, KVW = HEADS * HD, KV_HEADS * HD
CH = 512
CM = CH // P
TAPS = 31
PAD = TAPS // 2
CONV_SPAN = P + 2 * PAD + 2 * P
CONV_W = CONV_SPAN + 2 * PAD
CONV_OFF = [0, P + 2 * PAD, 2 * P + 2 * PAD]
E = 16
GROUPS = 4
EPG = E // GROUPS
FF = 512
KF = FF // P
CAP = TILES * P
SEG = 512
MODC = 6 * D // SEG
SLOTS = 6
ROUNDS = MODC // SLOTS + 1 + E // 2
EPS = 1e-6
HALF = D // 2
CONV_HEADS = 6
KEY_CHUNKS = [[0], [1, 2, 3], [1, 2, 3]]
V_CHUNK = [0, 2, 3]

PRE_TAPS = 13
TAPS_PER_HEAD = (TAPS - PRE_TAPS) // CONV_HEADS
assert PRE_TAPS + CONV_HEADS * TAPS_PER_HEAD == TAPS

XT, GATE, UP, HT, YB = 0, 2, 3, 4, 5


class Steps:

    def __init__(self, eng, sem):
        self.eng, self.sem, self.n = eng, sem, 0

    def link(self, ins):
        self.mark(ins)
        self.eng.wait_ge(self.sem, self.n)

    def mark(self, ins):
        self.n += 1
        ins.then_inc(self.sem, 1)


def past(value):
    return not isinstance(value, int) or value > 0


def group(t):
    return min(t, 1)


def build(nc, x_prompt, x_sample, cache_k, cache_v, c, c_ctx, w_mod, b_mod, norm1_g, norm2_g, w_in, q_norm_g,
          k_norm_g, conv_dw_w, conv_dw_b, conv_ln_g, conv_ln_b, w_out, w_router, b_router, w_gate, w_up, w_down,
          table, y_prompt, y_sample, new_k, new_v):
    mod_dram = nc.dram_tensor("mod_rows", (2, 6 * D), F32, kind="Internal").ap()
    h2_dram = nc.dram_tensor("h2_rows", (CAP, D), F32, kind="Internal").ap()
    slot_dram = nc.dram_tensor("slot_tokens", (E * CAP, 1), F32, kind="Internal").ap()
    y_dram = nc.dram_tensor("expert_rows", (E * CAP, D), F32, kind="Internal").ap()

    with ExitStack() as ctx:
        ctx.enter_context(nc.allow_non_contiguous_dma(reason="small parameter rows"))

        def sb(name, shape, dt=F32):
            return ctx.enter_context(nc.sbuf_tensor(name, shape, dt))

        def sem(name):
            return ctx.enter_context(nc.semaphore(name))

        ps = ctx.enter_context(nc.psum_tensor("ps", [P, 8, 512], F32))
        ring = sb("ring", [P, SLOTS, KD * SEG])
        x = sb("x", [P, TILES, D])
        shiftB = sb("shiftB", [P, 2, D])
        scaleB = sb("scaleB", [P, 2, D])
        gateB = sb("gateB", [P, 2, D])
        h = sb("h", [P, TILES, D])
        hT = sb("hT", [P, TILES, KD, P])
        table_sb = sb("table_sb", [P, table.shape[1]])
        wr = sb("wr", [P, KD, E])
        br = sb("br", [P, E])
        cc = sb("cc", [P, 2, KD])
        cs = sb("cs", [P, 2, KD])
        qkg = sb("qkg", [P, 2, HD])
        lnB = sb("lnB", [P, 2, CH])
        convw = sb("convw", [P, CM, TAPS + 1])
        stat = sb("stat", [P, 64])
        half_neg = sb("half_neg", [P, 16])
        slot_rows_sb = sb("slot_rows_sb", [E * TILES, P])
        route = sb("route", [P, TILES, E])
        gates = sb("gates", [P, TILES, 2])
        pick = sb("pick", [P, TILES * 2], U32)
        slot_tok = sb("slot_tok", [P, 48], U32)
        count = sb("count", [1, E], I32)
        scr = sb("scr", [P, 9832])

        o = 0

        def cut(n):
            nonlocal o
            o += n
            return scr[:, o - n:o]

        qk = cut(TILES * 640).rearrange("p (t n) -> p t n", t=TILES)
        tmp = cut(2 * 640).rearrange("p (t n) -> p t n", t=2)
        qT = cut(TILES * 512).rearrange("p (t n) -> p t n", t=TILES)
        kT = cut(512)
        acc = cut(CM * CONV_SPAN).rearrange("p (m n) -> p m n", m=CM)
        zT = cut(CM * CONV_W).rearrange("p (m n) -> p m n", m=CM)
        assert o >= 6 * D
        vall = cut(4 * KVW).rearrange("p (c n) -> p c n", c=4)
        ck = cut(KVW)
        sg = cut(CH)
        assert o <= 9832
        prob = scr[:, 0:TILES * 384].rearrange("p (t n) -> p t n", t=TILES)
        probT = scr[:, TILES * 384:2 * TILES * 384].rearrange("p (t n) -> p t n", t=TILES)
        modrow = scr[0:2, 0:6 * D]
        norm_rows = h[0:2, 0:2, :]
        o = 0
        xs = cut(2 * D).rearrange("p (b n) -> p b n", b=2)
        xsT = cut(D)
        hid = cut(FF)
        hidT = cut(FF)
        ybuf = cut(D)
        ov_a = cut(D)
        ov_b = cut(D)
        ov_hidT = cut(FF)
        rt = ybuf
        sel_all = rt[:, 528:576]
        pick_buf = [(xs[:, 0, :], xs[:, 1, :]), (xsT, ybuf)]

        o = 0

        def col(n):
            nonlocal o
            o += n
            return table_sb[:, o - n:o]

        ident, tri, ones = col(P), col(P), col(P)
        ropeC = col(2 * HD).rearrange("p (t n) -> p t n", t=2)
        ropeS = col(2 * HD).rearrange("p (t n) -> p t n", t=2)
        tie = col(16)
        slot_base = col(E)
        tok_id = col(TILES)

        x_in = sem("x_in"); table_in = sem("table_in"); c_in = sem("c_in"); router_in = sem("router_in")
        mod_in = sem("mod_in"); small_in = sem("small_in"); mod_st = sem("mod_st")
        bcA_in = sem("bcA_in"); bcG_in = sem("bcG_in")
        slot_loaded = [sem(f"slot_loaded{s}") for s in range(SLOTS)]
        slot_used = [sem(f"slot_used{s}") for s in range(SLOTS)]
        cache_st = sem("cache_st"); h2_st = sem("h2_st"); zero_st = sem("zero_st"); filled_st = sem("filled_st")
        scatter_st = sem("scatter_st"); slots_in = sem("slots_in"); y_st = sem("y_st")
        gathered = [sem(f"gathered{b}") for b in range(2)]
        picked = [sem(f"picked{b}") for b in range(2)]
        out_st = sem("out_st")
        convw_ps = sem("convw_ps"); hT_ps = sem("hT_ps"); proj_ps = sem("proj_ps"); zT_ps = sem("zT_ps")
        qkT_ps = sem("qkT_ps"); s_ps = sem("s_ps"); t_ps = sem("t_ps"); o_ps = sem("o_ps"); back_ps = sem("back_ps")
        outp_ps = sem("outp_ps"); logit_ps = sem("logit_ps"); pos_ps = sem("pos_ps"); slots_ps = sem("slots_ps")
        xT_ps = sem("xT_ps"); gate_ps = sem("gate_ps"); up_ps = sem("up_ps"); hidT_ps = sem("hidT_ps")
        y0_ps = sem("y0_ps")
        cs_ready = sem("cs_ready"); mod_taken = sem("mod_taken"); 
        convw_ready = sem("convw_ready"); h_ready = sem("h_ready"); z_ready = sem("z_ready")
        qk_ss = sem("qk_ss"); rope_ready = sem("rope_ready"); nmax = sem("nmax"); attn_out = sem("attn_out")
        conv_step = sem("conv_step"); ln_var = sem("ln_var"); ln_out = sem("ln_out"); mix_ready = sem("mix_ready")
        resid = sem("resid"); sel_ready = sem("sel_ready"); pos_ready = sem("pos_ready")
        slots_ready = sem("slots_ready"); hid_ready = sem("hid_ready"); xsT_ready = sem("xsT_ready")
        hidT_ready = sem("hidT_ready"); combined = sem("combined"); rinv_ready = sem("rinv_ready"); silu_ready = sem("silu_ready"); dve_step = sem("dve_step")
        c_sig = sem("c_sig"); sumsq = sem("sumsq"); hT_ready = sem("hT_ready"); proj_taken = sem("proj_taken")
        zT_ready = sem("zT_ready"); qkT_ready = sem("qkT_ready"); exp_done = sem("exp_done")
        probT_ready = sem("probT_ready"); ln_sig = sem("ln_sig"); score_ready = sem("score_ready")
        sig_ready = sem("sig_ready"); y_taken = sem("y_taken")
        const_set = sem("const_set"); pads_set = sem("pads_set"); rstd_ready = sem("rstd_ready")
        pool_step = sem("pool_step"); qk_rstd = sem("qk_rstd"); ln_rstd = sem("ln_rstd")
        ov_gathered = sem("ov_gathered");  ov_xT = sem("ov_xT"); ov_xsT = sem("ov_xsT"); ov_gate = sem("ov_gate")
        ov_up = sem("ov_up"); ov_sig = sem("ov_sig"); ov_hid = sem("ov_hid"); ov_silu = sem("ov_silu"); ov_hT = sem("ov_hT")
        ov_hidT_ready = sem("ov_hidT_ready"); ov_y = sem("ov_y"); ov_taken = sem("ov_taken"); ov_st = sem("ov_st")

        w_mod_v = w_mod.rearrange("l (p k) n -> l p k n", k=KD)
        w_in_v = w_in.rearrange("l (p k) n -> l p k n", k=KD)
        w_out_v = w_out.rearrange("l (p k) n -> l p k n", k=KD)
        w_gate_v = w_gate.rearrange("l e (p k) n -> l e p k n", k=KD)
        w_up_v = w_up.rearrange("l e (p k) n -> l e p k n", k=KD)
        w_down_v = w_down.rearrange("l e (p k) n -> l e p (k n)", k=KF)
        y_rows = y_dram.rearrange("(e t p) n -> (e t) p n", t=TILES, p=P)
        slot_rows = slot_dram.rearrange("(r n) o -> r (n o)", n=P)

        def slot_w(s, n=SEG):
            return ring[:, s, 0:KD * n].rearrange("p (k n) -> p k n", k=KD)

        def stats(a, n=1):
            return stat[:, a:a + n]

        SS1, R1, QKSS, QKR, LNV, LNR, NM, RS, RI = 0, 3, 6, 16, 26, 34, 37, 40, 43
        BN = 48

        block = ctx.enter_context(nc.Block())

        @block.sync
        def _(sp):
            for l in range(LAYERS):
                for r in range(MODC // SLOTS):
                    for s in range(SLOTS):
                        if past(l * ROUNDS + r):
                            sp.wait_ge(slot_used[s], l * ROUNDS + r)
                        sp.dma_start(slot_w(s), w_mod_v[bass.ds(l, 1), :, :, bass.ds(r * (SLOTS * SEG) + s * SEG, SEG)]
                                     .rearrange("l p k n -> (l p) k n")).then_inc(slot_loaded[s], 16)
                for s, (c0, n) in enumerate(((QW + 2 * KVW + CH, CH), (QW + 2 * KVW, CH), (0, QW), (QW, 2 * KVW))):
                    sp.wait_ge(slot_used[s], l * ROUNDS + 2)
                    sp.dma_start(slot_w(s, n), w_in_v[bass.ds(l, 1), :, :, c0:c0 + n]
                                 .rearrange("l p k n -> (l p) k n")).then_inc(slot_loaded[s], 16)
                for n in range(2):
                    sp.wait_ge(slot_used[4 + n], l * ROUNDS + 2)
                    sp.dma_start(slot_w(4 + n), w_out_v[bass.ds(l, 1), :, :, n * SEG:(n + 1) * SEG]
                                 .rearrange("l p k n -> (l p) k n")).then_inc(slot_loaded[4 + n], 16)
                with sp.Fori(0, E // 2) as i:
                    for j in range(2):
                        for m, w in enumerate((w_gate_v, w_up_v)):
                            s = 3 * j + m
                            sp.wait_ge(slot_used[s], l * ROUNDS + 3 + i)
                            sp.dma_start(slot_w(s), w[bass.ds(l, 1), bass.ds(i * 2 + j, 1)]
                                         .rearrange("l e p k n -> (l e p) k n")).then_inc(slot_loaded[s], 16)
                        s = 3 * j + 2
                        sp.wait_ge(slot_used[s], l * ROUNDS + 3 + i)
                        sp.dma_start(ring[:, s, 0:KF * D], w_down_v[bass.ds(l, 1), bass.ds(i * 2 + j, 1)]
                                     .rearrange("l e p n -> (l e p) n")).then_inc(slot_loaded[s], 16)
            sp.wait_ge(combined, TILES * LAYERS)
            sp.dma_start(y_prompt[0], x[:, 0, :]).then_inc(out_st, 16)
            sp.dma_start(y_sample[0].rearrange("(t p) n -> p t n", p=P), x[:, 1:3, :]).then_inc(out_st, 16)
            sp.wait_ge(out_st, 32)

        def overflow(eng, l, e, run, signals):
            at = (l * E + e) * 2
            n = eng.value_load(count[0:1, bass.ds(e, 1)], min_val=0, max_val=CAP)

            def skip(tiles):
                for s, by in signals:
                    eng.sem_inc(s, by * tiles)

            with eng.If(n > P):
                run(1, at)
                with eng.If(n > 2 * P):
                    run(2, at + 1)
                with eng.Else():
                    skip(1)
            with eng.Else():
                skip(2)

        @block.gpsimd
        def _(pool):
            g = nc.gpsimd
            step = Steps(pool, pool_step)
            pool.dma_start(x[:, 0, :], x_prompt[0]).then_inc(x_in, 16)
            pool.dma_start(x[:, 1:3, :], x_sample[0].rearrange("(t p) n -> p t n", p=P)).then_inc(x_in, 16)
            pool.dma_start(cc[:, 0, :], c_ctx.rearrange("(p k) -> p k", k=KD)).then_inc(c_in, 16)
            pool.dma_start(cc[:, 1, :], c[0].rearrange("(p k) -> p k", k=KD)).then_inc(c_in, 16)
            pool.dma_start(table_sb[:, :], table).then_inc(table_in, 16)
            pool.dma_start(wr[:, :, :], w_router.rearrange("(p k) e -> p k e", k=KD)).then_inc(router_in, 16)
            pool.dma_start(br[:, :], b_router.partition_broadcast(P)).then_inc(router_in, 16)
            g.memset(half_neg[:, :], -0.5).then_inc(const_set, 1)
            g.memset(slot_rows_sb[:, :], 0.0).then_inc(const_set, 1)
            pool.wait_ge(const_set, 2)
            pool.dma_start(slot_rows, slot_rows_sb[:, :]).then_inc(zero_st, 16)
            pool.wait_ge(zero_st, 16)
            pool.wait_ge(table_in, 16)

            def rstd(out, in_, n, scale, eps):
                step.link(g.tensor_scalar(out, in_, scale, eps, ALU.mult, ALU.add))
                return g.tensor_tensor(out, out, half_neg[:, 0:n], ALU.pow)

            for l in range(LAYERS):
                if past(l * TILES):
                    pool.wait_ge(combined, l * TILES)
                pool.dma_start(modrow, b_mod[bass.ds(l, 1), :].broadcast_to([2, 6 * D])).then_inc(mod_in, 16)
                pool.dma_start(norm_rows[:, 0, :], norm1_g[bass.ds(l, 1), :].broadcast_to([2, D])).then_inc(mod_in, 16)
                pool.dma_start(norm_rows[:, 1, :], norm2_g[bass.ds(l, 1), :].broadcast_to([2, D])).then_inc(mod_in, 16)
                pool.dma_start(sg[0:TAPS, :], conv_dw_w[bass.ds(l, 1)].rearrange("l k n -> (l k) n")).then_inc(small_in, 16)
                pool.dma_start(sg[TAPS:TAPS + 1, :], conv_dw_b[bass.ds(l, 1), :]).then_inc(small_in, 16)
                pool.dma_start(vall[:, 1, :], cache_v[:, bass.ds(l, 1)].rearrange("b l s h d -> (b l s) (h d)"))\
                    .then_inc(small_in, 16)
                pool.dma_start(ck, cache_k[:, bass.ds(l, 1)].rearrange("b l s h d -> (b l s) (h d)"))\
                    .then_inc(small_in, 16)
                pool.dma_start(qkg[:, 0, :], q_norm_g[bass.ds(l, 1), :].broadcast_to([P, HD])).then_inc(small_in, 16)
                pool.dma_start(qkg[:, 1, :], k_norm_g[bass.ds(l, 1), :].broadcast_to([P, HD])).then_inc(small_in, 16)
                pool.dma_start(lnB[:, 0, :], conv_ln_g[bass.ds(l, 1), :].broadcast_to([P, CH])).then_inc(small_in, 16)
                pool.dma_start(lnB[:, 1, :], conv_ln_b[bass.ds(l, 1), :].broadcast_to([P, CH])).then_inc(small_in, 16)

                def spread(dst, j, s):
                    pool.dma_start(dst, mod_dram[:, j * D:(j + 1) * D].partition_broadcast(P)).then_inc(s, 16)

                pool.wait_ge(sumsq, l * 6 + 3)
                rstd(stats(R1, 3), stats(SS1, 3), 3, 1.0 / D, EPS).then_inc(rstd_ready, 1)
                pool.wait_ge(mod_taken, (l + 1) * MODC)
                pool.dma_start(mod_dram, modrow).then_inc(mod_st, 16)
                pool.wait_ge(mod_st, l * 16 + 16)
                spread(scaleB[:, :, :], 1, bcA_in)
                spread(shiftB[:, :, :], 0, bcA_in)
                spread(gateB[:, :, :], 2, bcG_in)
                g.memset(zT[:, :, 0:PAD], 0.0).then_inc(pads_set, 1)
                g.memset(zT[:, :, PAD + P:PAD + P + 2 * PAD], 0.0).then_inc(pads_set, 1)
                g.memset(zT[:, :, CONV_W - PAD:CONV_W], 0.0).then_inc(pads_set, 1)
                pool.wait_ge(h_ready, l * 6 + 3)
                spread(scaleB[:, :, :], 4, bcA_in)
                spread(shiftB[:, :, :], 3, bcA_in)
                for t in range(TILES):
                    pool.wait_ge(qk_ss, l * 3 + t + 1)
                    step.link(g.tensor_scalar(stats(QKR, HEADS), stats(QKSS, HEADS), 1.0, HD * EPS, ALU.mult, ALU.add))
                    step.link(g.tensor_scalar(stats(QKR + HEADS, 2), stats(QKSS + HEADS, 2), 1.0 / HD, EPS,
                                              ALU.mult, ALU.add))
                    g.tensor_tensor(stats(QKR, 10), stats(QKR, 10), half_neg[:, 0:10], ALU.pow).then_inc(qk_rstd, 1)
                    if t == 0:
                        pool.wait_ge(rope_ready, l * 3 + 1)
                        pool.wait_ge(proj_taken, l * 9 + 7)
                        pool.dma_start(new_k[:, bass.ds(l, 1)].rearrange("b l s h d -> (b l s) (h d)"),
                                       qk[:, 0, QW:QW + KVW]).then_inc(cache_st, 16)
                        pool.dma_start(new_v[:, bass.ds(l, 1)].rearrange("b l s h d -> (b l s) (h d)"),
                                       vall[:, 0, :]).then_inc(cache_st, 16)
                pool.wait_ge(cache_st, l * 32 + 32)
                if l == 0:
                    pool.wait_ge(bcG_in, 16)
                    for t in range(1, TILES):
                        pool.dma_start(y_dram.rearrange("(e t p) n -> p e t n", t=TILES, p=P)[:, :, t, :],
                                       gateB[:, 0, :].unsqueeze(1).broadcast_to([P, E, D])).then_inc(filled_st, 16)
                for t in range(TILES):
                    pool.wait_ge(ln_var, l * 3 + t + 1)
                    rstd(stats(LNR, 1), stats(LNV + 1, 1), 1, 1.0, EPS).then_inc(ln_rstd, 1)
                pool.wait_ge(sumsq, l * 6 + 6)
                rstd(stats(R1, 3), stats(SS1, 3), 3, 1.0 / D, EPS).then_inc(rstd_ready, 1)
                pool.wait_ge(resid, l * 6 + 6)
                pool.wait_ge(filled_st, 32)
                spread(gateB[:, :, :], 5, bcG_in)
                for t in range(TILES):
                    pool.wait_ge(h_ready, l * 6 + 4 + t)
                    pool.dma_start(h2_dram[t * P:(t + 1) * P, :], h[:, t, :]).then_inc(h2_st, 16)
                pool.wait_ge(pos_ready, l + 1)
                for n in range(2 * TILES):
                    pool.indirect_dma_start(out=slot_dram,
                                            out_offset=bass.IndirectOffsetOnAxis(ap=pick[:, n:n + 1], axis=0),
                                            in_=tok_id[:, n // 2:n // 2 + 1], in_offset=None).then_inc(scatter_st, 16)
                pool.wait_ge(scatter_st, (l + 1) * (2 * TILES * 16))
                pool.dma_start(slot_rows_sb[:, :], slot_rows).then_inc(slots_in, 16)
                pool.wait_ge(slots_ready, l + 1)

                def gather(e):
                    pool.indirect_dma_start(out=xs[:, e % 2, :], out_offset=None, in_=h2_dram,
                                            in_offset=bass.IndirectOffsetOnAxis(
                                                ap=slot_tok[:, e * TILES:e * TILES + 1], axis=0))\
                        .then_inc(gathered[e % 2], 16)

                pool.wait_ge(h2_st, (l + 1) * (TILES * 16))
                gather(0)
                gather(1)
                for e in range(E):
                    def run(t, at):
                        if past(at):
                            pool.wait_ge(ov_hT, at)
                        pool.indirect_dma_start(out=ov_a, out_offset=None, in_=h2_dram,
                                                in_offset=bass.IndirectOffsetOnAxis(
                                                    ap=slot_tok[:, e * TILES + t:e * TILES + t + 1], axis=0))\
                            .then_inc(ov_gathered, 16)

                    overflow(pool, l, e, run, ((ov_gathered, 16),))
                    if e + 2 < E:
                        pool.wait_ge(xT_ps, (l * E + e + 1) * 2)
                        gather(e + 2)

                pool.wait_ge(y_st, (l + 1) * (E * 16))
                pool.wait_ge(ov_st, (l + 1) * (2 * E * 16))
                for t in range(TILES):
                    if t == 2:
                        pool.wait_ge(combined, l * TILES + 1)
                    for n in range(2):
                        pool.indirect_dma_start(out=pick_buf[t % 2][n], out_offset=None, in_=y_dram,
                                                in_offset=bass.IndirectOffsetOnAxis(ap=pick[:, 2 * t + n:2 * t + n + 1], axis=0))\
                            .then_inc(picked[t % 2], 16)

        def proj_wait(eng, l, c, t):
            if t < 2:
                eng.wait_ge(proj_ps, l * 8 + 2 * c + t + 1)
            else:
                eng.wait_ge(slot_used[c], l * ROUNDS + 3)

        def outp_wait(eng, l, n, t):
            if t < 2:
                eng.wait_ge(outp_ps, l * 4 + 2 * n + t + 1)
            else:
                eng.wait_ge(slot_used[4 + n], l * ROUNDS + 3)

        @block.scalar
        def _(act):
            a = nc.scalar
            act.wait_ge(c_in, 32)
            a.activation(cs[:, :, :], cc[:, :, :], ACT.Sigmoid).then_inc(c_sig, 1)
            act.wait_ge(x_in, 32)
            for l in range(LAYERS):
                def square_sum(t):
                    a.activation(hT[:, t].rearrange("p k n -> p (k n)"), x[:, t, :], ACT.Square,
                                 accum_out=stats(SS1 + t)).then_inc(sumsq, 1)

                def take_hT(which):
                    for n in range(6):
                        act.wait_ge(hT_ps, l * 18 + which * 6 + n + 1)
                        a.copy(hT[:, n // 2, 4 * (n % 2):4 * (n % 2) + 4, :].rearrange("p k n -> p (k n)"),
                               ps[:, n % 4, :]).then_inc(hT_ready, 1)

                if past(l * TILES):
                    act.wait_ge(combined, l * TILES)
                for t in range(TILES):
                    square_sum(t)
                take_hT(0)
                for t in range(TILES):
                    proj_wait(act, l, 0, t)
                    a.activation(h[:, t, 0:CH], ps[:, 4 + t, :], ACT.Sigmoid).then_inc(proj_taken, 1)

                def queries(t):
                    proj_wait(act, l, 2, t)
                    a.copy(qk[:, t, 0:QW], ps[:, 4 + (6 + t) % 4, :]).then_inc(proj_taken, 1)

                queries(0)
                for t in range(TILES):
                    act.wait_ge(zT_ps, l * 3 + t + 1)
                    a.copy(zT[:, :, PAD + CONV_OFF[t]:PAD + CONV_OFF[t] + P],
                           ps[:, t, :].rearrange("p (m n) -> p m n", m=CM)).then_inc(zT_ready, 1)
                queries(1)
                queries(2)
                for t in range(TILES):
                    proj_wait(act, l, 3, t)
                    a.copy(qk[:, t, QW:QW + KVW], ps[:, 4 + (9 + t) % 4, 0:KVW])
                    a.copy(vall[:, V_CHUNK[t], :], ps[:, 4 + (9 + t) % 4, KVW:2 * KVW]).then_inc(proj_taken, 1)
                for t in range(TILES):
                    act.wait_ge(qkT_ps, l * 4 + t + 1)
                    a.copy(qT[:, t, :], ps[:, 4 + t, :]).then_inc(qkT_ready, 1)
                act.wait_ge(qkT_ps, l * 4 + 4)
                a.copy(kT, ps[:, 7, :]).then_inc(qkT_ready, 1)
                act.wait_ge(cache_st, l * 32 + 32)
                with act.Fori(0, HEADS) as hd:
                    u = l * (HEADS * TILES) + hd * TILES
                    for t in range(TILES):
                        n = P * len(KEY_CHUNKS[t])
                        act.wait_ge(nmax, u + t + 1)
                        a.activation(prob[:, t, 0:n], ps[:, 4 + t, 0:n], ACT.Exp, bias=stats(NM + t),
                                     accum_out=stats(RS + t)).then_inc(exp_done, 1)
                    for t in range(TILES):
                        n = P * len(KEY_CHUNKS[t])
                        act.wait_ge(t_ps, u + t + 1)
                        a.copy(probT[:, t, 0:n], ps[:, 1 + t, 0:n]).then_inc(probT_ready, 1)
                for t in range(TILES):
                    act.wait_ge(ln_out, l * 3 + t + 1)
                    if past(l * 3 + t):
                        act.wait_ge(mix_ready, l * 3 + t)
                    a.activation(sg, h[:, t, CH:D], ACT.Sigmoid).then_inc(ln_sig, 1)
                take_hT(1)
                for t in range(TILES):
                    act.wait_ge(resid, l * 6 + 3 + t + 1)
                    square_sum(t)
                take_hT(2)
                act.wait_ge(logit_ps, l + 1)
                a.activation(route[:, :, :].rearrange("p t e -> p (t e)"), ps[:, 4, 0:TILES * E], ACT.Sigmoid)\
                    .then_inc(score_ready, 1)
                act.wait_ge(pos_ready, l + 1)

                def take_y(k, i, j):
                    if past((l * E + k) * 16):
                        act.wait_ge(y_st, (l * E + k) * 16)
                    act.wait_ge(y0_ps, l * E + k + 1)
                    a.copy(ybuf[:, 0:SEG], ps[:, YB, :])
                    act.wait_ge(slot_used[3 * j + 2], l * ROUNDS + 3 + i + 1)
                    a.copy(ybuf[:, SEG:D], ps[:, YB + 1, :]).then_inc(y_taken, 1)
                    act.wait_ge(y_taken, l * E + k + 1)
                    act.dma_start(y_rows[bass.ds(k * TILES, 1)].rearrange("r p n -> (r p) n"), ybuf).then_inc(y_st, 16)

                def expert(i, j, first):
                    e = i * 2 + j
                    act.wait_ge(gate_ps, l * E + e + 1)
                    a.activation(hid, ps[:, GATE, :], ACT.Sigmoid).then_inc(sig_ready, 1)

                    def run(t, at):
                        act.wait_ge(ov_gate, at + 1)
                        a.activation(ov_a[:, 0:FF], ps[:, GATE, :], ACT.Sigmoid).then_inc(ov_sig, 1)
                        act.wait_ge(ov_y, at + 1)
                        a.copy(ov_b, ps[:, YB:YB + 2, :].rearrange("p b n -> p (b n)")).then_inc(ov_taken, 1)
                        act.wait_ge(ov_taken, at + 1)
                        act.dma_start(y_rows[bass.ds(e * TILES + t, 1)].rearrange("r p n -> (r p) n"), ov_b)\
                            .then_inc(ov_st, 16)

                    overflow(act, l, e, run, ((ov_sig, 1), (ov_taken, 1), (ov_st, 16)))
                    if not first:
                        if j:
                            take_y(e - 1, i, 0)
                        else:
                            take_y(e - 1, i - 1, 1)

                expert(0, 0, True)
                expert(0, 1, False)
                with act.Fori(1, E // 2) as i:
                    expert(i, 0, False)
                    expert(i, 1, False)
                take_y(E - 1, E // 2 - 1, 1)

        @block.vector
        def _(dve):
            v = nc.vector
            step = Steps(dve, dve_step)
            dve.wait_ge(c_sig, 1)
            v.tensor_tensor(cs[:, :, :], cs[:, :, :], cc[:, :, :], ALU.mult).then_inc(cs_ready, 1)
            dve.wait_ge(table_in, 16)
            dve.wait_ge(router_in, 32)
            for l in range(LAYERS):
                dve.wait_ge(mod_in, l * 48 + 48)
                for r in range(MODC // SLOTS):
                    for s in range(SLOTS):
                        row = modrow[:, bass.ds(r * (SLOTS * SEG) + s * SEG, SEG)]
                        dve.wait_ge(slot_used[s], l * ROUNDS + r + 1)
                        v.tensor_tensor(row, ps[0:2, s, :], row, ALU.add).then_inc(mod_taken, 1)
                        if s in (2, 3):
                            dve.wait_ge(mod_taken, l * MODC + r * SLOTS + s + 1)
                            v.scalar_tensor_tensor(row, row, 1.0,
                                                   norm_rows[:, bass.ds(r, 1), (s - 2) * SEG:(s - 1) * SEG]
                                                   .rearrange("p r n -> p (r n)"), ALU.add, ALU.mult)
                dve.wait_ge(convw_ps, l + 1)
                v.tensor_copy(convw[:, :, :].rearrange("p m k -> p (m k)"), ps[:, 6, 0:P]).then_inc(convw_ready, 1)

                def norm(which, t):
                    dve.wait_ge(rstd_ready, l * 2 + which + 1)
                    dve.wait_ge(bcA_in, l * 64 + which * 32 + 32)
                    step.link(v.scalar_tensor_tensor(h[:, t, :], x[:, t, :], stats(R1 + t), scaleB[:, group(t), :],
                                                     ALU.mult, ALU.mult))
                    v.tensor_tensor(h[:, t, :], h[:, t, :], shiftB[:, group(t), :], ALU.add).then_inc(h_ready, 1)

                for t in range(TILES):
                    norm(0, t)
                for t in range(TILES):
                    proj_wait(dve, l, 1, t)
                    dve.wait_ge(proj_taken, l * 9 + t + 1)
                    v.tensor_tensor(h[:, t, 0:CH], ps[:, 4 + (3 + t) % 4, :], h[:, t, 0:CH], ALU.mult).then_inc(z_ready, 1)

                def tap(k, first=False):
                    for m in range(CM):
                        span = zT[:, m, bass.ds(k, CONV_SPAN)]
                        w = convw[:, m, bass.ds(k, 1)]
                        if first:
                            v.tensor_scalar(acc[:, m, :], span, w, convw[:, m, TAPS:TAPS + 1], ALU.mult, ALU.add)\
                                .then_inc(conv_step, 1)
                        else:
                            dve.wait_ge(conv_step, (l * TAPS + k - 1) * CM + m + 1)
                            v.scalar_tensor_tensor(acc[:, m, :], span, w, acc[:, m, :], ALU.mult, ALU.add)\
                                .then_inc(conv_step, 1)

                dve.wait_ge(zT_ready, l * 3 + 3)
                dve.wait_ge(pads_set, l * 3 + 3)
                dve.wait_ge(convw_ready, l + 1)
                tap(0, True)
                with dve.Fori(1, PRE_TAPS) as k:
                    tap(k)

                def heads(ap, n=10):
                    return ap.rearrange("p (h d) -> p h d", d=HD)

                def table_b(ap, n):
                    return ap.unsqueeze(1).broadcast_to([P, n, HD])

                for t in range(TILES):
                    dve.wait_ge(proj_taken, l * 9 + 6 + t + 1)
                    if t:
                        dve.wait_ge(rope_ready, l * 3 + t)
                    step.link(v.tensor_tensor(tmp[:, 0, :], qk[:, t, :], qk[:, t, :], ALU.mult))
                    v.tensor_reduce(stats(QKSS, 10), heads(tmp[:, 0, :]), AX.X, ALU.add).then_inc(qk_ss, 1)
                    dve.wait_ge(qk_rstd, l * 3 + t + 1)
                    step.link(v.tensor_tensor(heads(qk[:, t, :]), heads(qk[:, t, :]),
                                              stats(QKR, 10).unsqueeze(2).broadcast_to([P, 10, HD]), ALU.mult))
                    q, kk = qk[:, t, 0:QW], qk[:, t, QW:QW + KVW]
                    q_out = h[:, t, 0:QW].rearrange("p (j g d) -> p g j d", g=KV_HEADS, d=HD)

                    def grouped(ap):
                        return ap.rearrange("p (g j d) -> p g j d", g=KV_HEADS, d=HD)

                    dve.wait_ge(zT_ps, l * 3 + 3)
                    if t == 0:
                        qg = qkg[:, 0, :].unsqueeze(1).broadcast_to([P, PAIRS, HD])
                        for gg in range(KV_HEADS):
                            v.tensor_tensor(q_out[:, gg], grouped(q)[:, gg], qg, ALU.mult)
                        v.tensor_tensor(heads(kk), heads(kk), table_b(qkg[:, 1, :], 2), ALU.mult).then_inc(rope_ready, 1)
                        continue
                    step.mark(v.tensor_tensor(heads(q), heads(q), table_b(qkg[:, 0, :], HEADS), ALU.mult))
                    step.link(v.tensor_tensor(heads(kk), heads(kk), table_b(qkg[:, 1, :], 2), ALU.mult))
                    step.mark(v.tensor_tensor(heads(tmp[:, 0, :]), heads(qk[:, t, :]), table_b(ropeC[:, t - 1, :], 10),
                                              ALU.mult))

                    def axes(ap, half):
                        return ap.rearrange("p (h a s f) -> p h a s f", a=2, s=2, f=16)[:, :, :, half, :]

                    for half in range(2):
                        sin = ropeS[:, t - 1, :].rearrange("p (a s f) -> p a s f", a=2, s=2)[:, :, half, :]
                        ins = v.tensor_tensor(axes(tmp[:, 1, :], half), axes(qk[:, t, :], 1 - half),
                                              sin.unsqueeze(1).broadcast_to([P, 10, 2, 16]), ALU.mult)
                        (step.link if half else step.mark)(ins)
                    for gg in range(KV_HEADS):
                        v.tensor_tensor(q_out[:, gg], grouped(tmp[:, 0, 0:QW])[:, gg], grouped(tmp[:, 1, 0:QW])[:, gg],
                                        ALU.add)
                    v.tensor_tensor(kk, tmp[:, 0, QW:QW + KVW], tmp[:, 1, QW:QW + KVW], ALU.add).then_inc(rope_ready, 1)

                def head(hd, conv):
                    u = l * (HEADS * TILES) + hd * TILES
                    for t in range(TILES):
                        dve.wait_ge(s_ps, u + t + 1)
                        v.tensor_reduce(stats(NM + t), ps[:, 4 + t, 0:P * len(KEY_CHUNKS[t])], AX.X, ALU.max,
                                        negate=True).then_inc(nmax, 1)
                    if conv:
                        for n in range(TAPS_PER_HEAD):
                            tap(hd * TAPS_PER_HEAD + PRE_TAPS + n)
                    for t in range(TILES):
                        dve.wait_ge(o_ps, u + t + 1)
                        v.reciprocal(stats(RI + t), stats(RS + t)).then_inc(rinv_ready, 1)
                        dve.wait_ge(rinv_ready, u + t + 1)
                        v.tensor_scalar(h[:, t, bass.ds(hd * HD, HD)], ps[:, 1 + t, 384:384 + HD], stats(RI + t), None,
                                        ALU.mult).then_inc(attn_out, 1)

                with dve.Fori(0, CONV_HEADS) as hd:
                    head(hd, True)
                with dve.Fori(CONV_HEADS, HEADS) as hd:
                    head(hd, False)

                for t in range(TILES):
                    bank = 4 + t
                    dve.wait_ge(back_ps, l * 3 + t + 1)
                    step.link(v.bn_stats(stats(BN, 6), ps[:, bank, :]))
                    v.bn_aggr(stats(LNV, 2), stats(BN, 6)).then_inc(ln_var, 1)
                    dve.wait_ge(ln_rstd, l * 3 + t + 1)
                    z = h[:, t, CH:D]
                    step.link(v.tensor_scalar(z, ps[:, bank, :], stats(LNV), stats(LNR), ALU.subtract, ALU.mult))
                    step.link(v.tensor_tensor(z, z, lnB[:, 0, :], ALU.mult))
                    v.tensor_tensor(z, z, lnB[:, 1, :], ALU.add).then_inc(ln_out, 1)
                    dve.wait_ge(ln_sig, l * 3 + t + 1)
                    v.tensor_tensor(z, z, sg, ALU.mult).then_inc(mix_ready, 1)

                dve.wait_ge(bcG_in, l * 32 + 16)
                for n in range(2):
                    for t in range(TILES):
                        outp_wait(dve, l, n, t)
                        cols = slice(n * SEG, (n + 1) * SEG)
                        part = acc.rearrange("p m n -> p (m n)")[:, (3 * n + t) % 2 * SEG:((3 * n + t) % 2 + 1) * SEG]
                        if 3 * n + t >= 2:
                            dve.wait_ge(resid, l * 6 + 3 * n + t - 1)
                        step.link(v.tensor_tensor(part, ps[:, 4 + (3 * n + t) % 4, :], gateB[:, group(t), cols], ALU.mult))
                        v.tensor_tensor(x[:, t, cols], x[:, t, cols], part, ALU.add).then_inc(resid, 1)
                for t in range(TILES):
                    norm(1, t)

                o = 0

                def cutr(n):
                    nonlocal o
                    o += n
                    return rt[:, o - n:o]

                NE, NG = TILES * E, TILES * GROUPS
                gt, eq = cutr(NG * 16), cutr(NG * 16)
                sb_, rank, top, sel, pm, hi, lo, sw = (cutr(NE) for _ in range(8))
                gs, grank, gsel = cutr(NG), cutr(NG), cutr(NG)
                pmax, psum, wsum, wr_ = (cutr(TILES) for _ in range(4))
                s_flat = route[:, :, :].rearrange("p t e -> p (t e)")

                def by_tile(ap):
                    return ap.rearrange("p (t e) -> p t e", t=TILES)

                def beats(out_gt, out_eq, scores, n, m):
                    sv = scores.rearrange("p (n m) -> p n m", m=m)
                    mine = sv.unsqueeze(3).broadcast_to([P, n, m, m])
                    other = sv.unsqueeze(2).broadcast_to([P, n, m, m])
                    ov = [a_[:, 0:n * m * m].rearrange("p (n i j) -> p n i j", i=m, j=m) for a_ in (out_gt, out_eq)]
                    before = tie.rearrange("p (i j) -> p i j", i=m).unsqueeze(1).broadcast_to([P, n, m, m])
                    step.mark(v.tensor_tensor(ov[0], other, mine, ALU.is_gt))
                    step.link(v.tensor_tensor(ov[1], other, mine, ALU.is_equal))
                    step.link(v.tensor_tensor(ov[1], ov[1], before, ALU.mult))
                    step.link(v.tensor_tensor(out_gt[:, 0:n * m * m], out_gt[:, 0:n * m * m], out_eq[:, 0:n * m * m],
                                              ALU.add))
                    return out_gt[:, 0:n * m * m].rearrange("p (n j) -> p n j", j=m)

                dve.wait_ge(score_ready, l + 1)
                step.link(v.tensor_tensor(by_tile(sb_), route[:, :, :], br[:, :].unsqueeze(1).broadcast_to([P, TILES, E]),
                                          ALU.add))
                step.link(v.tensor_reduce(rank, beats(gt, eq, sb_, NG, EPG), AX.X, ALU.add))
                step.link(v.tensor_scalar(top, rank, 2.0, None, ALU.is_lt))
                step.link(v.tensor_tensor(pm, top, sb_, ALU.mult))
                step.link(v.tensor_reduce(gs, pm.rearrange("p (n m) -> p n m", m=EPG), AX.X, ALU.add))
                step.link(v.tensor_reduce(grank, beats(gt, eq, gs, TILES, GROUPS), AX.X, ALU.add))
                step.link(v.tensor_scalar(gsel, grank, 1.0, None, ALU.is_lt))
                v.tensor_tensor(sel.rearrange("p (n m) -> p n m", m=EPG), top.rearrange("p (n m) -> p n m", m=EPG),
                                gsel.unsqueeze(2).broadcast_to([P, NG, EPG]), ALU.mult).then_inc(sel_ready, 1)
                dve.wait_ge(pos_ps, l + 1)
                step.link(v.tensor_tensor(by_tile(pm), by_tile(ps[:, 5, 0:NE]),
                                          slot_base.unsqueeze(1).broadcast_to([P, TILES, E]), ALU.add))
                step.link(v.tensor_tensor(pm, pm, sel, ALU.mult))
                step.mark(v.tensor_reduce(pmax, by_tile(pm), AX.X, ALU.max))
                step.link(v.tensor_reduce(psum, by_tile(pm), AX.X, ALU.add))
                step.link(v.tensor_tensor(psum, psum, pmax, ALU.subtract))
                pick_v = pick[:, :].rearrange("p (t n) -> p t n", n=2)
                v.tensor_copy(pick_v[:, :, 0], psum)
                v.tensor_copy(pick_v[:, :, 1], pmax)
                v.tensor_copy(count[0:1, :], ps[0:1, 5, NE:NE + E]).then_inc(pos_ready, 1)
                step.mark(v.tensor_tensor(by_tile(hi), by_tile(pm), pmax.unsqueeze(2).broadcast_to([P, TILES, E]),
                                          ALU.is_equal))
                step.link(v.tensor_tensor(sw, s_flat, sel, ALU.mult))
                step.link(v.tensor_reduce(wsum, by_tile(sw), AX.X, ALU.add))
                step.mark(v.reciprocal(wr_, wsum))
                step.link(v.tensor_tensor(lo, sel, hi, ALU.subtract))
                step.mark(v.tensor_tensor(lo, lo, sw, ALU.mult))
                step.link(v.tensor_tensor(hi, hi, sw, ALU.mult))
                step.mark(v.tensor_reduce(psum, by_tile(lo), AX.X, ALU.add))
                step.link(v.tensor_reduce(pmax, by_tile(hi), AX.X, ALU.add))
                step.mark(v.tensor_tensor(gates[:, :, 0], psum, wr_, ALU.mult))
                step.link(v.tensor_tensor(gates[:, :, 1], pmax, wr_, ALU.mult))
                dve.wait_ge(slots_ps, l + 1)
                v.tensor_copy(slot_tok[:, :], ps[:, 6, 0:E * TILES]).then_inc(slots_ready, 1)
                dve.wait_ge(pos_ready, l + 1)

                def take_xT(e):
                    for n in range(2):
                        dve.wait_ge(xT_ps, (l * E + e) * 2 + n + 1)
                        ins = v.tensor_copy(xsT[:, n * 512:(n + 1) * 512], ps[:, XT + n, :])
                    ins.then_inc(xsT_ready, 1)

                def expert(i, j, last):
                    e = i * 2 + j
                    dve.wait_ge(sig_ready, l * E + e + 1)
                    v.tensor_tensor(hid, ps[:, GATE, :], hid, ALU.mult).then_inc(silu_ready, 1)
                    dve.wait_ge(silu_ready, l * E + e + 1)
                    dve.wait_ge(up_ps, l * E + e + 1)
                    v.tensor_tensor(hid, ps[:, UP, :], hid, ALU.mult).then_inc(hid_ready, 1)

                    def run(t, at):
                        if past(at * 16):
                            dve.wait_ge(ov_st, at * 16)
                        for n in range(2):
                            dve.wait_ge(ov_xT, at * 2 + n + 1)
                            ins = v.tensor_copy(ov_b[:, n * 512:(n + 1) * 512], ps[:, XT + n, :])
                        ins.then_inc(ov_xsT, 1)
                        dve.wait_ge(ov_sig, at + 1)
                        v.tensor_tensor(ov_a[:, 0:FF], ps[:, GATE, :], ov_a[:, 0:FF], ALU.mult).then_inc(ov_silu, 1)
                        dve.wait_ge(ov_silu, at + 1)
                        dve.wait_ge(ov_up, at + 1)
                        v.tensor_tensor(ov_a[:, 0:FF], ps[:, UP, :], ov_a[:, 0:FF], ALU.mult).then_inc(ov_hid, 1)
                        dve.wait_ge(ov_hT, at + 1)
                        v.tensor_copy(ov_hidT, ps[:, HT, :]).then_inc(ov_hidT_ready, 1)

                    overflow(dve, l, e, run, ((ov_xsT, 1), (ov_silu, 1), (ov_hid, 1), (ov_hidT_ready, 1)))
                    if not last:
                        take_xT(e + 1)
                    dve.wait_ge(hidT_ps, l * E + e + 1)
                    v.tensor_copy(hidT, ps[:, HT, :]).then_inc(hidT_ready, 1)

                take_xT(0)
                expert(0, 0, False)
                expert(0, 1, False)
                with dve.Fori(1, E // 2 - 1) as i:
                    expert(i, 0, False)
                    expert(i, 1, False)
                expert(E // 2 - 1, 0, False)
                expert(E // 2 - 1, 1, True)

                dve.wait_ge(bcG_in, l * 32 + 32)
                for t in range(TILES):
                    a0, a1 = pick_buf[t % 2]
                    dve.wait_ge(picked[t % 2], l * (64 if t % 2 == 0 else 32) + (t // 2 + 1) * 32)
                    step.link(v.tensor_scalar(a0, a0, gates[:, t, 0:1], None, ALU.mult))
                    step.link(v.scalar_tensor_tensor(a0, a1, gates[:, t, 1:2], a0, ALU.mult, ALU.add))
                    step.link(v.tensor_tensor(a0, a0, gateB[:, group(t), :], ALU.mult))
                    v.tensor_tensor(x[:, t, :], x[:, t, :], a0, ALU.add).then_inc(combined, 1)

        @block.tensor
        def _(pe):
            t_ = nc.tensor
            pe.wait_ge(cs_ready, 1)
            pe.wait_ge(table_in, 16)
            pe.wait_ge(router_in, 32)
            for l in range(LAYERS):
                base = l * ROUNDS

                def accumulate(out, stationary, moving, n):
                    for k in range(n):
                        mm = pe.matmul(out, stationary(k), moving(k), start=(k == 0), stop=(k == n - 1))
                    return mm

                if past(l * E):
                    pe.wait_ge(y_taken, l * E)
                for r in range(MODC // SLOTS):
                    if past(l * MODC + r * SLOTS):
                        pe.wait_ge(mod_taken, l * MODC + r * SLOTS)
                    for s in range(SLOTS):
                        pe.wait_ge(slot_loaded[s], (base + r + 1) * 16)
                        accumulate(ps[0:2, s, :], lambda k: cs[:, :, k], lambda k: slot_w(s)[:, k, :], KD)\
                            .then_inc(slot_used[s], 1)
                pe.wait_ge(small_in, (l + 1) * 128)
                for m in range(CM):
                    mm = pe.transpose(ps[:, 6, m * (TAPS + 1):(m + 1) * (TAPS + 1)], sg[0:TAPS + 1, m * P:(m + 1) * P],
                                      ident[0:TAPS + 1, 0:TAPS + 1])
                mm.then_inc(convw_ps, 1)

                def transposed(which, ready):
                    for n in range(6):
                        t = n // 2
                        if n % 2 == 0:
                            ready(t)
                        if n >= 4:
                            pe.wait_ge(hT_ready, l * 18 + which * 6 + n - 3)
                        for m in range(4):
                            k = 4 * (n % 2) + m
                            mm = pe.transpose(ps[:, n % 4, m * P:(m + 1) * P], h[:, t, k::KD], ident)
                        mm.then_inc(hT_ps, 1)

                def hT_wait(which, t):
                    pe.wait_ge(hT_ready, l * 18 + which * 6 + 2 * t + 2)

                transposed(0, lambda t: pe.wait_ge(h_ready, l * 6 + t + 1))

                def project(c, t, n=SEG):
                    g_ = 3 * c + t
                    hT_wait(0, t)
                    pe.wait_ge(slot_loaded[c], (base + 3) * 16)
                    if g_ >= 4:
                        pc, pt = (g_ - 4) // 3, (g_ - 4) % 3
                        if pc == 1:
                            pe.wait_ge(z_ready, l * 3 + pt + 1)
                        else:
                            pe.wait_ge(proj_taken, l * 9 + {0: 0, 2: 3}[pc] + pt + 1)
                    mm = accumulate(ps[:, 4 + g_ % 4, 0:n], lambda k: hT[:, t, k, :], lambda k: slot_w(c, n)[:, k, :], KD)
                    mm.then_inc(*((proj_ps, 1) if t < 2 else (slot_used[c], 1)))

                for c_ in range(2):
                    for t in range(TILES):
                        project(c_, t)
                project(2, 0)
                for t in range(TILES):
                    pe.wait_ge(z_ready, l * 3 + t + 1)
                    for m in range(CM):
                        mm = pe.transpose(ps[:, t, m * P:(m + 1) * P], h[:, t, m * P:(m + 1) * P], ident)
                    mm.then_inc(zT_ps, 1)
                project(2, 1)
                project(2, 2)
                for t in range(TILES):
                    project(3, t, 2 * KVW)

                pe.wait_ge(proj_taken, l * 9 + 9)
                pe.transpose(ps[:, 7, P:2 * P], ck, ident)
                for t in range(TILES):
                    pe.wait_ge(rope_ready, l * 3 + t + 1)
                    for j in range(PAIRS):
                        mm = pe.transpose(ps[:, 4 + t, j * P:(j + 1) * P], h[:, t, j * P:(j + 1) * P], ident)
                    mm.then_inc(qkT_ps, 1)
                    mm = pe.transpose(ps[:, 7, V_CHUNK[t] * P:(V_CHUNK[t] + 1) * P], qk[:, t, QW:QW + KVW], ident)
                mm.then_inc(qkT_ps, 1)

                def scores(hd, t):
                    g_, j = hd // PAIRS, hd % PAIRS
                    ks = KEY_CHUNKS[t]
                    pe.matmul(ps[:, 4 + t, 0:P * len(ks)], qT[g_ * HD:(g_ + 1) * HD, t, j * P:(j + 1) * P],
                              kT[g_ * HD:(g_ + 1) * HD, ks[0] * P:(ks[-1] + 1) * P], start=True, stop=True).then_inc(s_ps, 1)

                pe.wait_ge(qkT_ready, l * 4 + 4)
                for t in range(TILES):
                    scores(0, t)
                for hd in range(HEADS):
                    u = l * (HEADS * TILES) + hd * TILES
                    for t in range(TILES):
                        pe.wait_ge(exp_done, u + t + 1)
                        for n in range(len(KEY_CHUNKS[t])):
                            mm = pe.transpose(ps[:, 1 + t, n * P:(n + 1) * P], prob[:, t, n * P:(n + 1) * P], ident)
                        mm.then_inc(t_ps, 1)
                        if hd + 1 < HEADS:
                            scores(hd + 1, t)
                    for t in range(TILES):
                        pe.wait_ge(probT_ready, u + t + 1)
                        if hd:
                            pe.wait_ge(attn_out, u - TILES + t + 1)
                        g_ = hd // PAIRS
                        ks = KEY_CHUNKS[t]
                        accumulate(ps[:, 1 + t, 384:384 + HD], lambda n: probT[:, t, n * P:(n + 1) * P],
                                   lambda n: vall[:, ks[n], g_ * HD:(g_ + 1) * HD], len(ks)).then_inc(o_ps, 1)

                pe.wait_ge(conv_step, (l + 1) * (TAPS * CM))
                for t in range(TILES):
                    for m in range(CM):
                        mm = pe.transpose(ps[:, 4 + t, m * P:(m + 1) * P],
                                          acc[:, m, CONV_OFF[t]:CONV_OFF[t] + P], ident)
                    mm.then_inc(back_ps, 1)

                pe.wait_ge(attn_out, (l + 1) * (HEADS * TILES))
                transposed(1, lambda t: pe.wait_ge(mix_ready, l * 3 + t + 1))
                for n in range(2):
                    for t in range(TILES):
                        hT_wait(1, t)
                        pe.wait_ge(slot_loaded[4 + n], (base + 3) * 16)
                        if 3 * n + t >= 4:
                            pe.wait_ge(resid, l * 6 + 3 * n + t - 3)
                        mm = accumulate(ps[:, 4 + (3 * n + t) % 4, :], lambda k: hT[:, t, k, :],
                                        lambda k: slot_w(4 + n)[:, k, :], KD)
                        mm.then_inc(*((outp_ps, 1) if t < 2 else (slot_used[4 + n], 1)))

                transposed(2, lambda t: pe.wait_ge(h_ready, l * 6 + 3 + t + 1))
                for t in range(TILES):
                    hT_wait(2, t)
                    mm = accumulate(ps[:, 4, t * E:(t + 1) * E], lambda k: hT[:, t, k, :], lambda k: wr[:, k, :], KD)
                mm.then_inc(logit_ps, 1)
                pe.wait_ge(sel_ready, l + 1)
                for t in range(TILES):
                    accumulate(ps[:, 5, t * E:(t + 1) * E], lambda k: ones if k < t else tri,
                               lambda k: sel_all[:, k * E:(k + 1) * E], t + 1)
                accumulate(ps[:, 5, TILES * E:(TILES + 1) * E], lambda k: ones,
                           lambda k: sel_all[:, k * E:(k + 1) * E], TILES).then_inc(pos_ps, 1)
                pe.wait_ge(slots_in, (l + 1) * 16)
                pe.transpose(ps[:, 6, 0:E * TILES], slot_rows_sb[:, :], ident[0:E * TILES, 0:E * TILES]).then_inc(slots_ps, 1)
                pe.wait_ge(pos_ready, l + 1)

                def token_transposes(rows, s):
                    for n in range(2):
                        for m in range(4):
                            mm = pe.transpose(ps[:, XT + n, m * P:(m + 1) * P], rows[:, 4 * n + m::KD], ident)
                        mm.then_inc(s, 1)

                def xT(e, i, j):
                    pe.wait_ge(gathered[j], (l * (E // 2) + i + 1) * 16)
                    token_transposes(xs[:, j, :], xT_ps)

                def gate_up(bank, s, src):
                    return accumulate(ps[:, bank, :], lambda k: src[:, k * P:(k + 1) * P],
                                      lambda k: slot_w(s)[:, k, :], KD)

                def hidden_transposes(rows):
                    for k in range(KF):
                        mm = pe.transpose(ps[:, HT, k * P:(k + 1) * P], rows[:, k:FF:KF], ident)
                    return mm

                def down(s, src, n):
                    w = ring[:, s, 0:KF * D].rearrange("p (k n) -> p k n", k=KF)
                    return accumulate(ps[:, YB + n, :], lambda k: src[:, k * P:(k + 1) * P],
                                      lambda k: w[:, k, n * SEG:(n + 1) * SEG], KF)

                def down_main(k, i, j):
                    s = 3 * j + 2
                    pe.wait_ge(hidT_ready, l * E + k + 1)
                    if past(l * E + k):
                        pe.wait_ge(y_taken, l * E + k)
                    pe.wait_ge(slot_loaded[s], (base + 4 + i) * 16)
                    down(s, hidT, 0).then_inc(y0_ps, 1)
                    down(s, hidT, 1).then_inc(slot_used[s], 1)

                def release(s):
                    pe.matmul(ps[0:1, 7, 0:1], ones[:, 0:1], ones[:, 0:1], start=True, stop=True).then_inc(slot_used[s], 1)

                def expert(i, j, first, last):
                    e = i * 2 + j
                    g0 = l * E + e
                    pe.wait_ge(xsT_ready, g0 + 1)
                    if past(g0):
                        pe.wait_ge(hid_ready, g0)
                    pe.wait_ge(slot_loaded[3 * j], (base + 4 + i) * 16)
                    gate_up(GATE, 3 * j, xsT).then_inc(gate_ps, 1)
                    pe.wait_ge(slot_loaded[3 * j + 1], (base + 4 + i) * 16)
                    gate_up(UP, 3 * j + 1, xsT).then_inc(up_ps, 1)

                    def run(t, at):
                        pe.wait_ge(ov_gathered, (at + 1) * 16)
                        token_transposes(ov_a, ov_xT)
                        pe.wait_ge(ov_xsT, at + 1)
                        pe.wait_ge(hid_ready, g0 + 1)
                        gate_up(GATE, 3 * j, ov_b).then_inc(ov_gate, 1)
                        gate_up(UP, 3 * j + 1, ov_b).then_inc(ov_up, 1)
                        pe.wait_ge(ov_hid, at + 1)
                        if past(g0):
                            pe.wait_ge(hidT_ready, g0)
                        hidden_transposes(ov_a).then_inc(ov_hT, 1)
                        pe.wait_ge(ov_hidT_ready, at + 1)
                        if past(g0 if first else g0 - 1):
                            pe.wait_ge(y_taken, g0 if first else g0 - 1)
                        pe.wait_ge(slot_loaded[3 * j + 2], (base + 4 + i) * 16)
                        down(3 * j + 2, ov_hidT, 0)
                        down(3 * j + 2, ov_hidT, 1).then_inc(ov_y, 1)
                        pe.wait_ge(ov_taken, at + 1)

                    overflow(pe, l, e, run, ((ov_xT, 2), (ov_gate, 1), (ov_up, 1), (ov_hT, 1), (ov_y, 1)))
                    release(3 * j)
                    release(3 * j + 1)
                    if not last:
                        xT(e + 1, i + j, 1 - j)
                    if not first:
                        if j:
                            down_main(e - 1, i, 0)
                        else:
                            down_main(e - 1, i - 1, 1)
                    pe.wait_ge(hid_ready, g0 + 1)
                    hidden_transposes(hid).then_inc(hidT_ps, 1)

                xT(0, 0, 0)
                expert(0, 0, True, False)
                expert(0, 1, False, False)
                with pe.Fori(1, E // 2 - 1) as i:
                    expert(i, 0, False, False)
                    expert(i, 1, False, False)
                expert(E // 2 - 1, 0, False, False)
                expert(E // 2 - 1, 1, False, True)
                down_main(E - 1, E // 2 - 1, 1)


_INS = ['x_prompt', 'x_sample', 'cache_k', 'cache_v', 'c', 'c_ctx', 'w_mod', 'b_mod', 'norm1_g', 'norm2_g', 'w_in',
        'q_norm_g', 'k_norm_g', 'conv_dw_w', 'conv_dw_b', 'conv_ln_g', 'conv_ln_b', 'w_out', 'w_router', 'b_router',
        'w_gate', 'w_up', 'w_down']
_OUTS = [(1, 128, 1024), (1, 256, 1024), (1, 2, 128, 2, 64), (1, 2, 128, 2, 64)]


def _table():
    import numpy as np
    p = np.arange(P)
    freqs = (np.float32(10000.0) ** (-np.arange(16, dtype=np.float32) / 16)).astype(np.float32)
    cos, sin = [], []
    for t in range(2):
        n = t * P + p
        ang = np.stack([(n // 64).astype(np.float32)[:, None] * freqs, (n % 64).astype(np.float32)[:, None] * freqs], 1)
        cos.append(np.stack([np.cos(ang), np.cos(ang)], 2).reshape(P, HD))
        sin.append(np.stack([-np.sin(ang), np.sin(ang)], 2).reshape(P, HD))
    i4 = np.arange(4)
    tie = (i4[None, :] < i4[:, None]).astype(np.float32).reshape(1, 16)
    parts = [np.eye(P), (p[:, None] < p[None, :]), np.ones((P, P)), *cos, *sin, np.tile(tie, (P, 1)),
             np.tile(np.arange(E)[None] * CAP, (P, 1)), p[:, None] + P * np.arange(TILES)[None]]
    return np.ascontiguousarray(np.concatenate([a.astype(np.float32) for a in parts], 1))


def kernel(**inputs):
    import numpy as _np
    import concourse.bacc as _bacc
    from concourse.bass_utils import run_bass_kernel_spmd as _run

    nc = _bacc.Bacc("TRN2", target_bir_lowering=False, num_devices=1)
    arrays, args = {}, []
    for name in _INS + ['table']:
        a = _table() if name == 'table' else _np.ascontiguousarray(inputs[name])
        arrays[f"in_{name}_dram"] = a
        args.append(nc.dram_tensor(f"in_{name}_dram", a.shape, mybir.dt.from_np(a.dtype), kind="ExternalInput").ap())
    for i, shape in enumerate(_OUTS):
        args.append(nc.dram_tensor(f"out_{i}_dram", shape, F32, kind="ExternalOutput").ap())
    build(nc, *args)
    r = _run(nc, [arrays], core_ids=[0])
    return tuple(r.results[0][f"out_{i}_dram"] for i in range(len(_OUTS)))
```

```python
from contextlib import ExitStack

import concourse.bass as bass
from concourse import mybir

ALU = mybir.AluOpType
ACT = mybir.ActivationFunctionType
AX = mybir.AxisListType
F32 = mybir.dt.float32
I32 = mybir.dt.int32
U32 = mybir.dt.uint32

P = 128
D = 1024
KD = D // P
LAYERS = 2
TILES = 3
HEADS, KV_HEADS, HD = 8, 2, 64
PAIRS = HEADS // KV_HEADS
QW, KVW = HEADS * HD, KV_HEADS * HD
CH = 512
CM = CH // P
TAPS = 31
PAD = TAPS // 2
CONV_SPAN = P + 2 * PAD + 2 * P
CONV_W = CONV_SPAN + 2 * PAD
CONV_OFF = [0, P + 2 * PAD, 2 * P + 2 * PAD]
E = 16
GROUPS = 4
EPG = E // GROUPS
FF = 512
KF = FF // P
CAP = TILES * P
SEG = 512
MODC = 6 * D // SEG
SLOTS = 6
MOD1, MOD2 = 4, 10
MOD_A, IN_AT, MOD_B, OUT_AT, MOD_G, EXP_AT = [], [], [], [], [], []
_n = MOD1
for _l in range(LAYERS):
    MOD_A.append(0 if _l == 0 else MOD_G[_l - 1] + MODC - MOD2)
    IN_AT.append(_n)
    MOD_B.append(_n + 4)
    OUT_AT.append(MOD_B[_l] + MOD2 - MOD1)
    MOD_G.append(OUT_AT[_l] + 2)
    EXP_AT.append(MOD_G[_l] + MODC - MOD2 + (MOD1 if _l + 1 < LAYERS else 0))
    _n = EXP_AT[_l] + 3 * E
EPS = 1e-6
HALF = D // 2
KEY_CHUNKS = [[0], [1, 2, 3], [1, 2, 3]]
V_CHUNK = [0, 2, 3]
LOGITS = [7, 4, 7]
BACK = [0, 4, 7]

PRE_TAPS = 11
ROPE_TAPS = TILES
LATE_TAPS = 3
HEAD_TAPS = [2, 2, 2, 3, 3, 2]
assert PRE_TAPS + ROPE_TAPS + LATE_TAPS + sum(HEAD_TAPS) == TAPS

XT, GATE, UP, HT, YB = 0, 2, 3, 4, 5


class Steps:

    def __init__(self, eng, sem):
        self.eng, self.sem, self.n = eng, sem, 0

    def link(self, ins):
        self.mark(ins)
        self.eng.wait_ge(self.sem, self.n)

    def mark(self, ins):
        self.n += 1
        ins.then_inc(self.sem, 1)


def past(value):
    return not isinstance(value, int) or value > 0


def slot_of(n):
    return n % SLOTS


def uses(n):
    return n // SLOTS + 1


def mod_item(l, c):
    if c < MOD1:
        return MOD_A[l] + c
    return MOD_B[l] + c - MOD1 if c < MOD2 else MOD_G[l] + c - MOD2


def mod_bank(l, c):
    if c < MOD1:
        return c if l == 0 else (7, 3, 2, 7)[c]
    return (0, 1, 2, 3, 0, 0, 3, 2)[c - MOD1]


HEAD_FILL = [(8, 0, 3), (8, 3, 6), (8, 6, KD), (9, 0, 3), (9, 3, 6), (9, 6, KD)]


def out_bank(t, n):
    return 4 + (2 * t + n + 1) % 4


def group(t):
    return min(t, 1)


def build(nc, x_prompt, x_sample, cache_k, cache_v, c, c_ctx, w_mod, b_mod, norm1_g, norm2_g, w_in, q_norm_g,
          k_norm_g, conv_dw_w, conv_dw_b, conv_ln_g, conv_ln_b, w_out, w_router, b_router, w_gate, w_up, w_down,
          table, y_prompt, y_sample, new_k, new_v):
    mod_dram = nc.dram_tensor("mod_rows", (2, 6 * D), F32, kind="Internal").ap()
    h2_dram = nc.dram_tensor("h2_rows", (CAP, D), F32, kind="Internal").ap()
    slot_dram = nc.dram_tensor("slot_tokens", (E * CAP, 1), F32, kind="Internal").ap()
    y_dram = nc.dram_tensor("expert_rows", (E * CAP, D), F32, kind="Internal").ap()

    with ExitStack() as ctx:
        ctx.enter_context(nc.allow_non_contiguous_dma(reason="small parameter rows"))

        def sb(name, shape, dt=F32):
            return ctx.enter_context(nc.sbuf_tensor(name, shape, dt))

        def sem(name):
            return ctx.enter_context(nc.semaphore(name))

        ps = ctx.enter_context(nc.psum_tensor("ps", [P, 8, 512], F32))
        ring = sb("ring", [P, SLOTS, KD * SEG])
        x = sb("x", [P, TILES, D])
        shiftB = sb("shiftB", [P, 2, D])
        scaleB = sb("scaleB", [P, 2, D])
        gateB = sb("gateB", [P, 2, D])
        h = sb("h", [P, TILES, D])
        hT = sb("hT", [P, TILES, KD, P])
        table_sb = sb("table_sb", [P, table.shape[1]])
        wr = sb("wr", [P, KD, E])
        br = sb("br", [P, E])
        cc = sb("cc", [P, 2, KD])
        cs = sb("cs", [P, 2, KD])
        qkg = sb("qkg", [P, 2, HD])
        lnB = sb("lnB", [P, 2, CH])
        convw = sb("convw", [P, CM, TAPS + 1])
        stat = sb("stat", [P, 64])
        half_neg = sb("half_neg", [P, 16])
        slot_rows_sb = sb("slot_rows_sb", [E * TILES, P])
        route = sb("route", [P, TILES, E])
        gates = sb("gates", [P, TILES, 2])
        pick = sb("pick", [P, TILES * 2], U32)
        slot_tok = sb("slot_tok", [P, 48], U32)
        count = sb("count", [1, E], I32)
        scr = sb("scr", [P, 9832])

        o = 0

        def cut(n):
            nonlocal o
            o += n
            return scr[:, o - n:o]

        qk = cut(TILES * 640).rearrange("p (t n) -> p t n", t=TILES)
        tmp = cut(2 * 640).rearrange("p (t n) -> p t n", t=2)
        qT = cut(TILES * 512).rearrange("p (t n) -> p t n", t=TILES)
        kT = cut(512)
        acc = cut(CM * CONV_SPAN).rearrange("p (m n) -> p m n", m=CM)
        zT = cut(CM * CONV_W).rearrange("p (m n) -> p m n", m=CM)
        assert o >= 5120 + (MOD1 + 2) * SEG
        vall = cut(4 * KVW).rearrange("p (c n) -> p c n", c=4)
        ck = cut(KVW)
        sg = cut(CH)
        assert o <= 9832
        prob = scr[:, 0:TILES * 384].rearrange("p (t n) -> p t n", t=TILES)
        probT = scr[:, TILES * 384:2 * TILES * 384].rearrange("p (t n) -> p t n", t=TILES)
        part = qk[:, 0:2, 0:SEG]
        rowA, gainA = scr[0:2, 5120:5120 + MOD1 * SEG], scr[0:2, 5120 + MOD1 * SEG:5120 + (MOD1 + 2) * SEG]
        rowB, rowS, rowG = scaleB[0:2], shiftB[0:2, 0], scaleB[0:2, 0]
        gainB = hT[0:2, 0].rearrange("p k n -> p (k n)")
        o = 0
        xs = cut(2 * D).rearrange("p (b n) -> p b n", b=2)
        xsT = cut(D)
        hid = cut(FF)
        hidT = cut(FF)
        ybuf = cut(D)
        ov_a = cut(D)
        ov_b = cut(D)
        ov_hidT = cut(FF)
        rt = ybuf
        sel_all = rt[:, 528:576]
        pick_buf = [(xs[:, 0, :], xs[:, 1, :]), (xsT, ybuf), (ov_a, ov_b)]

        o = 0

        def col(n):
            nonlocal o
            o += n
            return table_sb[:, o - n:o]

        ident, tri, ones = col(P), col(P), col(P)
        ropeC = col(2 * HD).rearrange("p (t n) -> p t n", t=2)
        ropeS = col(2 * HD).rearrange("p (t n) -> p t n", t=2)
        tie = col(16)
        slot_base = col(E)
        tok_id = col(TILES)

        x_in = sem("x_in"); table_in = sem("table_in"); c_in = sem("c_in"); router_in = sem("router_in")
        rowB_in = sem("rowB_in"); gain_in = sem("gain_in"); small_in = sem("small_in")
        modA_st = sem("modA_st"); modB_st = sem("modB_st"); modG_st = sem("modG_st"); rowG_in = sem("rowG_in"); rowA_in = sem("rowA_in")
        bcA_in = sem("bcA_in"); bcG_in = sem("bcG_in")
        slot_loaded = [sem(f"slot_loaded{s}") for s in range(SLOTS)]
        slot_used = [sem(f"slot_used{s}") for s in range(SLOTS)]
        cache_st = sem("cache_st"); h2_st = sem("h2_st"); zero_st = sem("zero_st"); filled_st = sem("filled_st")
        scatter_st = sem("scatter_st"); slots_in = sem("slots_in"); y_st = sem("y_st")
        gathered = [sem(f"gathered{b}") for b in range(2)]
        picked = [sem(f"picked{t}") for t in range(TILES)]
        out_st = sem("out_st")
        first_bc_ps = sem("first_bc_ps")
        convw_ps = sem("convw_ps"); hT_ps = sem("hT_ps"); proj_ps = sem("proj_ps"); zT_ps = sem("zT_ps")
        qkT_ps = sem("qkT_ps"); s_ps = sem("s_ps"); t_ps = sem("t_ps"); o_ps = sem("o_ps"); back_ps = sem("back_ps")
        outp_ps = sem("outp_ps"); logit_ps = sem("logit_ps"); pos_ps = sem("pos_ps"); slots_ps = sem("slots_ps")
        xT_ps = sem("xT_ps"); gate_ps = sem("gate_ps"); up_ps = sem("up_ps"); hidT_ps = sem("hidT_ps")
        y0_ps = sem("y0_ps")
        cs_ready = sem("cs_ready"); first_shift = sem("first_shift"); mod_taken = sem("mod_taken"); mod_done = sem("mod_done"); ln_norm = sem("ln_norm"); 
        convw_ready = sem("convw_ready"); h_ready = sem("h_ready"); z_ready = sem("z_ready")
        qk_ss = sem("qk_ss"); rope_ready = sem("rope_ready"); nmax = sem("nmax"); attn_out = sem("attn_out")
        conv_step = sem("conv_step"); ln_var = sem("ln_var"); ln_out = sem("ln_out"); mix_ready = sem("mix_ready")
        resid = sem("resid"); sel_ready = sem("sel_ready"); pos_ready = sem("pos_ready")
        slots_ready = sem("slots_ready"); hid_ready = sem("hid_ready"); xsT_ready = sem("xsT_ready")
        hidT_ready = sem("hidT_ready"); combined = sem("combined"); rinv_ready = sem("rinv_ready"); silu_ready = sem("silu_ready"); dve_step = sem("dve_step")
        first_scale = sem("first_scale"); scaled = sem("scaled")
        c_sig = sem("c_sig"); sumsq = sem("sumsq"); hT_ready = sem("hT_ready"); proj_taken = sem("proj_taken")
        zT_ready = sem("zT_ready"); qkT_ready = sem("qkT_ready"); exp_done = sem("exp_done")
        probT_ready = sem("probT_ready"); ln_sig = sem("ln_sig"); score_ready = sem("score_ready")
        sig_ready = sem("sig_ready"); y_taken = sem("y_taken")
        const_set = sem("const_set"); pads_set = sem("pads_set"); rstd_ready = sem("rstd_ready")
        pool_step = sem("pool_step"); qk_rstd = sem("qk_rstd"); ln_rstd = sem("ln_rstd")
        ov_dma = sem("ov_dma")
        ov_gathered = sem("ov_gathered");  ov_xT = sem("ov_xT"); ov_xsT = sem("ov_xsT"); ov_gate = sem("ov_gate")
        ov_up = sem("ov_up"); ov_sig = sem("ov_sig"); ov_hid = sem("ov_hid"); ov_silu = sem("ov_silu"); ov_hT = sem("ov_hT")
        ov_hidT_ready = sem("ov_hidT_ready"); ov_y = sem("ov_y"); ov_taken = sem("ov_taken"); ov_st = sem("ov_st")

        w_mod_v = w_mod.rearrange("l (p k) n -> l p k n", k=KD)
        w_in_v = w_in.rearrange("l (p k) n -> l p k n", k=KD)
        w_out_v = w_out.rearrange("l (p k) n -> l p k n", k=KD)
        w_gate_v = w_gate.rearrange("l e (p k) n -> l e p k n", k=KD)
        w_up_v = w_up.rearrange("l e (p k) n -> l e p k n", k=KD)
        w_down_v = w_down.rearrange("l e (p k) n -> l e p (k n)", k=KF)
        y_rows = y_dram.rearrange("(e t p) n -> (e t) p n", t=TILES, p=P)
        slot_rows = slot_dram.rearrange("(r n) o -> r (n o)", n=P)

        def slot_w(s, n=SEG):
            return ring[:, s, 0:KD * n].rearrange("p (k n) -> p k n", k=KD)

        def stats(a, n=1):
            return stat[:, a:a + n]

        SS1, R1, QKSS, QKR, LNV, LNR, NM, RS, RI = 0, 3, 6, 16, 26, 34, 37, 43, 49
        BN = 52

        block = ctx.enter_context(nc.Block())

        @block.sync
        def _(sp):
            def load(n, src, size=SEG):
                if past(n // SLOTS):
                    sp.wait_ge(slot_used[slot_of(n)], n // SLOTS)
                sp.dma_start(slot_w(slot_of(n), size), src).then_inc(slot_loaded[slot_of(n)], 16)

            def load_mod(l, c):
                load(mod_item(l, c), w_mod_v[l, :, :, c * SEG:(c + 1) * SEG])

            sp.dma_start(cc[:, 0, :], c_ctx.rearrange("(p k) -> p k", k=KD)).then_inc(c_in, 16)
            sp.dma_start(cc[:, 1, :], c[0].rearrange("(p k) -> p k", k=KD)).then_inc(c_in, 16)
            for c_ in range(MOD1):
                load_mod(0, c_)
            for l in range(LAYERS):
                for m, (c0, n) in enumerate(((QW + 2 * KVW + CH, CH), (QW + 2 * KVW, CH), (0, QW), (QW, 2 * KVW))):
                    if l and m == 2:
                        sp.wait_ge(combined, (l - 1) * TILES + 2)
                    load(IN_AT[l] + m, w_in_v[l, :, :, c0:c0 + n], n)
                for c_ in range(MOD1, MOD2):
                    load_mod(l, c_)
                for n in range(2):
                    load(OUT_AT[l] + n, w_out_v[l, :, :, n * SEG:(n + 1) * SEG])
                for c_ in range(MOD2, MODC):
                    load_mod(l, c_)
                if l + 1 < LAYERS:
                    for c_ in range(MOD1):
                        load_mod(l + 1, c_)
                with sp.Fori(0, E // 2) as i:
                    for j in range(2):
                        for m, w in enumerate((w_gate_v, w_up_v, w_down_v)):
                            n = EXP_AT[l] + 3 * j + m
                            s = slot_of(n)
                            sp.wait_ge(slot_used[s], i + n // SLOTS)
                            src = w[bass.ds(l, 1), bass.ds(i * 2 + j, 1)]
                            if m < 2:
                                sp.dma_start(slot_w(s), src.rearrange("l e p k n -> (l e p) k n"))\
                                    .then_inc(slot_loaded[s], 16)
                            else:
                                sp.dma_start(ring[:, s, 0:KF * D], src.rearrange("l e p n -> (l e p) n"))\
                                    .then_inc(slot_loaded[s], 16)
            for t in range(TILES):
                sp.wait_ge(combined, (LAYERS - 1) * TILES + t + 1)
                out = y_prompt[0] if t == 0 else y_sample[0, (t - 1) * P:t * P, :]
                sp.dma_start(out, x[:, t, :]).then_inc(out_st, 16)
            sp.wait_ge(out_st, TILES * 16)

        def overflow(eng, l, e, run, signals):
            at = (l * E + e) * 2
            n = eng.value_load(count[0:1, bass.ds(e, 1)], min_val=0, max_val=CAP)

            def skip(first, tiles):
                for s, by in signals:
                    if past(first):
                        eng.wait_ge(s, first * by)
                    eng.sem_inc(s, by * tiles)

            with eng.If(n > P):
                run(1, at)
                with eng.If(n > 2 * P):
                    run(2, at + 1)
                with eng.Else():
                    skip(at + 1, 1)
            with eng.Else():
                skip(at, 2)

        @block.gpsimd
        def _(pool):
            g = nc.gpsimd
            step = Steps(pool, pool_step)
            ov_count = pool.alloc_register("ov_count")
            pool.reg_mov(ov_count, 16)
            g.memset(half_neg[:, :], -0.5).then_inc(const_set, 1)
            g.memset(slot_rows_sb[:, :], 0.0).then_inc(const_set, 1)
            pool.wait_ge(const_set, 2)
            pool.dma_start(slot_rows, slot_rows_sb[:, :]).then_inc(zero_st, 16)
            pool.wait_ge(zero_st, 16)
            pool.wait_ge(table_in, 16)

            def rstd(out, in_, n, scale, eps):
                step.link(g.tensor_scalar(out, in_, scale, eps, ALU.mult, ALU.add))
                return g.tensor_tensor(out, out, half_neg[:, 0:n], ALU.pow)

            def spread(dst, j, s):
                pool.dma_start(dst, mod_dram[:, j * D:(j + 1) * D].partition_broadcast(P)).then_inc(s, 16)

            def norm_rstd(which, l, t):
                pool.wait_ge(sumsq, l * 6 + which * 3 + t + 1)
                rstd(stats(R1 + t), stats(SS1 + t), 1, 1.0 / D, EPS).then_inc(rstd_ready, 1)

            def mod_a(l):
                pool.wait_ge(mod_done, 2 * l + 1)
                pool.dma_start(mod_dram[:, 0:MOD1 * SEG], rowA).then_inc(modA_st, 16)
                pool.wait_ge(modA_st, l * 16)
                pool.wait_ge(h_ready, l * 6)
                spread(scaleB[:, :, :], 1, bcA_in)
                spread(shiftB[:, :, :], 0, bcA_in)

            for t in range(TILES):
                norm_rstd(0, 0, t)
            for l in range(LAYERS):
                if l:
                    for t in range(TILES):
                        norm_rstd(0, l, t)
                pool.wait_ge(h_ready, l * 6 + 3)
                pool.dma_start(rowB, b_mod[l:l + 1, 2 * D:4 * D].rearrange("l (j n) -> l j n", n=D)
                               .broadcast_to([2, 2, D])).then_inc(rowB_in, 16)
                pool.dma_start(rowS, b_mod[l:l + 1, 4 * D:5 * D].broadcast_to([2, D])).then_inc(rowB_in, 16)
                g.memset(zT[:, :, 0:PAD], 0.0).then_inc(pads_set, 1)
                g.memset(zT[:, :, PAD + P:PAD + P + 2 * PAD], 0.0).then_inc(pads_set, 1)
                g.memset(zT[:, :, CONV_W - PAD:CONV_W], 0.0).then_inc(pads_set, 1)
                if l == 0:
                    for n in range(4):
                        for t in range(1, TILES):
                            pool.dma_start(y_dram.rearrange("(e t p) n -> p e t n", t=TILES, p=P)[:, 4 * n:4 * n + 4, t, :],
                                           x[:, 0, :].unsqueeze(1).broadcast_to([P, 4, D])).then_inc(filled_st, 16)
                pool.wait_ge(slot_used[slot_of(IN_AT[l] + 3)], uses(IN_AT[l] + 3))
                pool.dma_start(gainB, norm2_g[l:l + 1, :].broadcast_to([2, D])).then_inc(gain_in, 16)
                for t in range(TILES):
                    pool.wait_ge(qk_ss, l * 3 + t + 1)
                    step.link(g.tensor_scalar(stats(QKR, HEADS), stats(QKSS, HEADS), 1.0, HD * EPS, ALU.mult, ALU.add))
                    step.link(g.tensor_scalar(stats(QKR + HEADS, 2), stats(QKSS + HEADS, 2), 1.0 / HD, EPS,
                                              ALU.mult, ALU.add))
                    g.tensor_tensor(stats(QKR, 10), stats(QKR, 10), half_neg[:, 0:10], ALU.pow).then_inc(qk_rstd, 1)
                    if t == 0:
                        pool.wait_ge(rope_ready, l * 3 + 1)
                        pool.wait_ge(proj_taken, l * 9 + 7)
                        pool.dma_start(new_k[:, l].rearrange("b s h d -> (b s) (h d)"),
                                       qk[:, 0, QW:QW + KVW]).then_inc(cache_st, 16)
                        pool.dma_start(new_v[:, l].rearrange("b s h d -> (b s) (h d)"),
                                       vall[:, 0, :]).then_inc(cache_st, 16)
                pool.wait_ge(mod_taken, l * MODC + 2 * MOD1)
                pool.dma_start(mod_dram[:, 2 * D:4 * D].rearrange("g (j n) -> g j n", n=D), rowB).then_inc(modB_st, 16)
                pool.wait_ge(modB_st, l * 32 + 16)
                spread(gateB[:, :, :], 2, bcG_in)
                pool.wait_ge(mod_done, 2 * l + 2)
                pool.dma_start(mod_dram[:, 4 * D:5 * D], rowS).then_inc(modB_st, 16)
                pool.wait_ge(modB_st, l * 32 + 32)
                spread(scaleB[:, :, :], 4, bcA_in)
                spread(shiftB[:, :, :], 3, bcA_in)
                pool.wait_ge(cache_st, l * 32 + 32)

                def ln_affine(t):
                    z = h[:, t, CH:D]
                    pool.wait_ge(ln_norm, l * 3 + t + 1)
                    step.link(g.tensor_tensor(z, z, lnB[:, 0, :], ALU.mult))
                    g.tensor_tensor(z, z, lnB[:, 1, :], ALU.add).then_inc(ln_out, 1)

                def ln_silu(t):
                    pool.wait_ge(ln_sig, l * 3 + t + 1)
                    g.tensor_tensor(h[:, t, CH:D], h[:, t, CH:D], sg, ALU.mult).then_inc(mix_ready, 1)

                for t in range(TILES):
                    pool.wait_ge(ln_var, l * 3 + t + 1)
                    rstd(stats(LNR, 1), stats(LNV + 1, 1), 1, 1.0, EPS).then_inc(ln_rstd, 1)
                    ln_affine(t)
                    if t:
                        ln_silu(t - 1)
                ln_silu(2)
                for t in range(TILES):
                    norm_rstd(1, l, t)
                pool.wait_ge(h_ready, l * 6 + 6)
                pool.dma_start(rowG, b_mod[l:l + 1, 5 * D:6 * D].broadcast_to([2, D])).then_inc(rowG_in, 16)
                pool.wait_ge(pos_ready, l + 1)
                for n in range(TILES * 2):
                    pool.indirect_dma_start(out=slot_dram,
                                            out_offset=bass.IndirectOffsetOnAxis(ap=pick[:, n:n + 1], axis=0),
                                            in_=tok_id[:, n // 2:n // 2 + 1], in_offset=None).then_inc(scatter_st, 16)
                pool.wait_ge(scatter_st, (l + 1) * (2 * TILES * 16))
                pool.dma_start(slot_rows_sb[:, :], slot_rows).then_inc(slots_in, 16)
                pool.wait_ge(slots_ready, l + 1)

                def gather(e):
                    pool.indirect_dma_start(out=xs[:, e % 2, :], out_offset=None, in_=h2_dram,
                                            in_offset=bass.IndirectOffsetOnAxis(
                                                ap=slot_tok[:, e * TILES:e * TILES + 1], axis=0))\
                        .then_inc(gathered[e % 2], 16)

                pool.wait_ge(h2_st, (l + 1) * (TILES * 16))
                gather(0)
                gather(1)
                pool.wait_ge(mod_taken, (l + 1) * MODC)
                pool.dma_start(mod_dram[:, 5 * D:6 * D], rowG).then_inc(modG_st, 16)
                pool.wait_ge(modG_st, (l + 1) * 16)
                spread(gateB[:, :, :], 5, bcG_in)
                if l + 1 < LAYERS:
                    mod_a(l + 1)
                for e in range(E):
                    def run(t, at):
                        if past(at):
                            pool.wait_ge(ov_hT, at)
                        pool.indirect_dma_start(out=ov_a, out_offset=None, in_=h2_dram,
                                                in_offset=bass.IndirectOffsetOnAxis(
                                                    ap=slot_tok[:, e * TILES + t:e * TILES + t + 1], axis=0))\
                            .then_inc(ov_dma, 16)
                        pool.wait_ge(ov_dma, pool.snap(ov_count))
                        pool.reg_add(ov_count, ov_count, 16)
                        pool.sem_inc(ov_gathered, 1)

                    overflow(pool, l, e, run, ((ov_gathered, 1),))
                    if e + 2 < E:
                        pool.wait_ge(xT_ps, (l * E + e + 1) * 2)
                        gather(e + 2)

                pool.wait_ge(y_st, (l + 1) * (E * 16))
                pool.wait_ge(ov_st, (l + 1) * (2 * E * 16))
                for t in range(TILES):
                    for n in range(2):
                        pool.indirect_dma_start(out=pick_buf[t][n], out_offset=None, in_=y_dram,
                                                in_offset=bass.IndirectOffsetOnAxis(ap=pick[:, 2 * t + n:2 * t + n + 1], axis=0))\
                            .then_inc(picked[t], 16)

        def proj_wait(eng, l, c, t):
            if t < 2:
                eng.wait_ge(proj_ps, l * 8 + 2 * c + t + 1)
            else:
                eng.wait_ge(slot_used[slot_of(IN_AT[l] + c)], uses(IN_AT[l] + c))

        def outp_wait(eng, l, n, t):
            if t < 2:
                eng.wait_ge(outp_ps, l * 4 + 2 * t + n + 1)
            else:
                eng.wait_ge(slot_used[slot_of(OUT_AT[l] + n)], uses(OUT_AT[l] + n))

        @block.scalar
        def _(act):
            a = nc.scalar

            def small_loads(l):
                act.dma_start(rowA, b_mod[l:l + 1, 0:MOD1 * SEG].broadcast_to([2, MOD1 * SEG])).then_inc(rowA_in, 16)
                act.dma_start(gainA, norm1_g[l:l + 1, :].broadcast_to([2, D])).then_inc(rowA_in, 16)
                act.dma_start(sg[0:TAPS, :], conv_dw_w[l]).then_inc(small_in, 16)
                act.dma_start(sg[TAPS:TAPS + 1, :], conv_dw_b[l:l + 1, :]).then_inc(small_in, 16)
                act.dma_start(vall[:, 1, :], cache_v[:, l].rearrange("b s h d -> (b s) (h d)")).then_inc(small_in, 16)
                act.dma_start(ck, cache_k[:, l].rearrange("b s h d -> (b s) (h d)")).then_inc(small_in, 16)
                act.dma_start(qkg[:, 0, :], q_norm_g[l:l + 1, :].broadcast_to([P, HD])).then_inc(small_in, 16)
                act.dma_start(qkg[:, 1, :], k_norm_g[l:l + 1, :].broadcast_to([P, HD])).then_inc(small_in, 16)
                act.dma_start(lnB[:, 0, :], conv_ln_g[l:l + 1, :].broadcast_to([P, CH])).then_inc(small_in, 16)
                act.dma_start(lnB[:, 1, :], conv_ln_b[l:l + 1, :].broadcast_to([P, CH])).then_inc(small_in, 16)

            act.dma_start(table_sb[:, :], table).then_inc(table_in, 16)
            act.dma_start(x[:, 0, :], x_prompt[0]).then_inc(x_in, 16)
            act.dma_start(x[:, 1:3, :], x_sample[0].rearrange("(t p) n -> p t n", p=P)).then_inc(x_in, 16)
            act.wait_ge(c_in, 32)
            a.activation(cs[:, :, :], cc[:, :, :], ACT.Sigmoid).then_inc(c_sig, 1)
            act.dma_start(wr[:, :, :], w_router.rearrange("(p k) e -> p k e", k=KD)).then_inc(router_in, 16)
            act.dma_start(br[:, :], b_router.partition_broadcast(P)).then_inc(router_in, 16)
            small_loads(0)
            act.wait_ge(x_in, 32)

            def scale_pick(l, t):
                act.wait_ge(picked[t], (l + 1) * 32)
                a.activation(pick_buf[t][0], pick_buf[t][0], ACT.Copy, scale=gates[:, t, 0:1]).then_inc(scaled, 1)

            for l in range(LAYERS):
                def square_sum(t):
                    a.activation(h[:, t, :], x[:, t, :], ACT.Square, accum_out=stats(SS1 + t)).then_inc(sumsq, 1)

                def take_hT(which, t):
                    for n in range(2 * t, 2 * t + 2):
                        act.wait_ge(hT_ps, l * 18 + which * 6 + n + 1)
                        a.copy(hT[:, n // 2, 4 * (n % 2):4 * (n % 2) + 4, :].rearrange("p k n -> p (k n)"),
                               ps[:, n % 4, :]).then_inc(hT_ready, 1)

                for t in range(TILES):
                    if l:
                        if t == 0:
                            for n in range(TILES):
                                scale_pick(l - 1, n)
                        act.wait_ge(combined, (l - 1) * TILES + t + 1)
                    square_sum(t)
                if l == 0:
                    for n in range(4):
                        act.wait_ge(first_bc_ps, n + 1)
                        a.copy(scaleB[:, n // 2, n % 2 * SEG:(n % 2 + 1) * SEG], ps[:, 4 + n, :]).then_inc(first_scale, 1)
                for t in range(TILES):
                    take_hT(0, t)

                def h2_tile(t):
                    act.wait_ge(h_ready, l * 6 + 4 + t)
                    act.dma_start(h2_dram[t * P:(t + 1) * P, :], h[:, t, :]).then_inc(h2_st, 16)
                    take_hT(2, t)
                    act.wait_ge(logit_ps, l * 3 + t + 1)
                    a.activation(route[:, t, :], ps[:, LOGITS[t], 0:E], ACT.Sigmoid).then_inc(score_ready, 1)

                for t in range(TILES):
                    proj_wait(act, l, 0, t)
                    a.activation(h[:, t, 0:CH], ps[:, 4 + t, :], ACT.Sigmoid).then_inc(proj_taken, 1)

                def queries(t):
                    proj_wait(act, l, 2, t)
                    a.copy(qk[:, t, 0:QW], ps[:, 4 + (6 + t) % 4, :]).then_inc(proj_taken, 1)

                queries(0)
                for t in range(TILES):
                    act.wait_ge(zT_ps, l * 3 + t + 1)
                    a.copy(zT[:, :, PAD + CONV_OFF[t]:PAD + CONV_OFF[t] + P],
                           ps[:, t, :].rearrange("p (m n) -> p m n", m=CM)).then_inc(zT_ready, 1)
                queries(1)
                queries(2)
                for t in range(TILES):
                    proj_wait(act, l, 3, t)
                    a.copy(qk[:, t, QW:QW + KVW], ps[:, 4 + (9 + t) % 4, 0:KVW])
                    a.copy(vall[:, V_CHUNK[t], :], ps[:, 4 + (9 + t) % 4, KVW:2 * KVW]).then_inc(proj_taken, 1)
                for t in range(TILES):
                    act.wait_ge(qkT_ps, l * 4 + t + 1)
                    a.copy(qT[:, t, :], ps[:, 4 + t, :]).then_inc(qkT_ready, 1)
                act.wait_ge(qkT_ps, l * 4 + 4)
                a.copy(kT, ps[:, 7, :]).then_inc(qkT_ready, 1)
                act.wait_ge(cache_st, l * 32 + 32)
                def softmax(hd, odd):
                    for t in range(TILES):
                        n = P * len(KEY_CHUNKS[t])
                        act.wait_ge(nmax, (l * HEADS + hd) * TILES + t + 1)
                        a.activation(prob[:, t, 0:n], ps[:, 4 + t, 0:n], ACT.Exp, bias=stats(NM + TILES * odd + t),
                                     accum_out=stats(RS + TILES * odd + t)).then_inc(exp_done, 1)

                def take_probT(hd):
                    for t in range(TILES):
                        n = P * len(KEY_CHUNKS[t])
                        act.wait_ge(t_ps, (l * HEADS + hd) * TILES + t + 1)
                        a.copy(probT[:, t, 0:n], ps[:, 1 + t, 0:n]).then_inc(probT_ready, 1)

                softmax(0, 0)
                with act.Fori(0, HEADS // 2 - 1) as i:
                    for j in range(2):
                        take_probT(i * 2 + j)
                        softmax(i * 2 + j + 1, 1 - j)
                take_probT(HEADS - 2)
                softmax(HEADS - 1, 1)
                take_probT(HEADS - 1)
                for t in range(TILES):
                    act.wait_ge(ln_out, l * 3 + t + 1)
                    if past(l * 3 + t):
                        act.wait_ge(mix_ready, l * 3 + t)
                    a.activation(sg, h[:, t, CH:D], ACT.Sigmoid).then_inc(ln_sig, 1)
                    if t:
                        take_hT(1, t - 1)
                take_hT(1, 2)
                if l + 1 < LAYERS:
                    act.wait_ge(mix_ready, l * 3 + 3)
                    small_loads(l + 1)
                for t in range(TILES):
                    act.wait_ge(resid, l * 6 + 2 * t + 2)
                    square_sum(t)
                    if t:
                        h2_tile(t - 1)
                h2_tile(2)
                act.wait_ge(pos_ready, l + 1)

                def take_y(k, i, j):
                    if past((l * E + k) * 16):
                        act.wait_ge(y_st, (l * E + k) * 16)
                    act.wait_ge(y0_ps, l * E + k + 1)
                    a.copy(ybuf[:, 0:SEG], ps[:, YB, :])
                    act.wait_ge(slot_used[slot_of(EXP_AT[l] + 3 * j + 2)], i + uses(EXP_AT[l] + 3 * j + 2))
                    a.copy(ybuf[:, SEG:D], ps[:, YB + 1, :]).then_inc(y_taken, 1)
                    act.wait_ge(y_taken, l * E + k + 1)
                    act.dma_start(y_rows[bass.ds(k * TILES, 1)].rearrange("r p n -> (r p) n"), ybuf).then_inc(y_st, 16)

                def expert(i, j, first):
                    e = i * 2 + j
                    act.wait_ge(gate_ps, l * E + e + 1)
                    a.activation(hid, ps[:, GATE, :], ACT.Sigmoid).then_inc(sig_ready, 1)

                    def run(t, at):
                        act.wait_ge(ov_gate, at + 1)
                        a.activation(ov_a[:, 0:FF], ps[:, GATE, :], ACT.Sigmoid).then_inc(ov_sig, 1)
                        act.wait_ge(ov_y, at + 1)
                        a.copy(ov_b, ps[:, YB:YB + 2, :].rearrange("p b n -> p (b n)")).then_inc(ov_taken, 1)
                        act.wait_ge(ov_taken, at + 1)
                        act.dma_start(y_rows[bass.ds(e * TILES + t, 1)].rearrange("r p n -> (r p) n"), ov_b)\
                            .then_inc(ov_st, 16)

                    overflow(act, l, e, run, ((ov_sig, 1), (ov_taken, 1), (ov_st, 16)))
                    if not first:
                        if j:
                            take_y(e - 1, i, 0)
                        else:
                            take_y(e - 1, i - 1, 1)

                expert(0, 0, True)
                expert(0, 1, False)
                with act.Fori(1, E // 2) as i:
                    expert(i, 0, False)
                    expert(i, 1, False)
                take_y(E - 1, E // 2 - 1, 1)
            for t in range(TILES):
                scale_pick(LAYERS - 1, t)

        @block.vector
        def _(dve):
            v = nc.vector
            step = Steps(dve, dve_step)
            dve.wait_ge(c_sig, 1)
            v.tensor_tensor(cs[:, :, :], cs[:, :, :], cc[:, :, :], ALU.mult).then_inc(cs_ready, 1)

            def mod_take(l, c):
                n = mod_item(l, c)
                if c == 0:
                    dve.wait_ge(rowA_in, (l + 1) * 32)
                if c == MOD1:
                    dve.wait_ge(rowB_in, (l + 1) * 32)
                if c == MOD2:
                    dve.wait_ge(rowG_in, (l + 1) * 16)
                half = slice(c % 2 * SEG, (c % 2 + 1) * SEG)
                if c < MOD1:
                    row = rowA[:, c * SEG:(c + 1) * SEG]
                else:
                    row = (rowB[:, 0], rowB[:, 1], rowS, rowG)[(c - MOD1) // 2][:, half]
                dve.wait_ge(slot_used[slot_of(n)], uses(n))
                v.tensor_tensor(row, ps[0:2, mod_bank(l, c), :], row, ALU.add).then_inc(mod_taken, 1)
                if c // 2 in (1, 4):
                    if c == 8:
                        dve.wait_ge(gain_in, (l + 1) * 16)
                    dve.wait_ge(mod_taken, l * MODC + c + 1)
                    gain = (gainA if c < MOD1 else gainB)[:, half]
                    ins = v.scalar_tensor_tensor(row, row, 1.0, gain, ALU.add, ALU.mult)
                    if c % 2:
                        ins.then_inc(mod_done, 1)

            def combine(l, t):
                dve.wait_ge(bcG_in, l * 32 + 32)
                a0, a1 = pick_buf[t]
                dve.wait_ge(picked[t], (l + 1) * 32)
                dve.wait_ge(scaled, l * TILES + t + 1)
                step.link(v.scalar_tensor_tensor(a0, a1, gates[:, t, 1:2], a0, ALU.mult, ALU.add))
                step.link(v.tensor_tensor(a0, a0, gateB[:, group(t), :], ALU.mult))
                v.tensor_tensor(x[:, t, :], x[:, t, :], a0, ALU.add).then_inc(combined, 1)

            for c_ in range(MOD1):
                mod_take(0, c_)
            for n in range(4):
                dve.wait_ge(first_bc_ps, 4 + n + 1)
                v.tensor_copy(shiftB[:, n // 2, n % 2 * SEG:(n % 2 + 1) * SEG], ps[:, n, :]).then_inc(first_shift, 1)
            dve.wait_ge(first_shift, 4)
            dve.wait_ge(first_scale, 4)
            dve.wait_ge(table_in, 16)
            dve.wait_ge(router_in, 32)
            for l in range(LAYERS):
                def norm(which, t):
                    dve.wait_ge(rstd_ready, l * 6 + which * 3 + t + 1)
                    if past(l * 64 + which * 32):
                        dve.wait_ge(bcA_in, l * 64 + which * 32)
                    step.link(v.scalar_tensor_tensor(h[:, t, :], x[:, t, :], stats(R1 + t), scaleB[:, group(t), :],
                                                     ALU.mult, ALU.mult))
                    v.tensor_tensor(h[:, t, :], h[:, t, :], shiftB[:, group(t), :], ALU.add).then_inc(h_ready, 1)

                if l:
                    combine(l - 1, 0)
                    combine(l - 1, 1)
                norm(0, 0)
                if l:
                    combine(l - 1, 2)
                norm(0, 1)
                norm(0, 2)
                dve.wait_ge(convw_ps, l + 1)
                v.tensor_copy(convw[:, :, :].rearrange("p m k -> p (m k)"), ps[:, 6, 0:P]).then_inc(convw_ready, 1)
                for t in range(TILES):
                    proj_wait(dve, l, 1, t)
                    dve.wait_ge(proj_taken, l * 9 + t + 1)
                    v.tensor_tensor(h[:, t, 0:CH], ps[:, 4 + (3 + t) % 4, :], h[:, t, 0:CH], ALU.mult).then_inc(z_ready, 1)

                def tap(k, first=False):
                    for m in range(CM):
                        span = zT[:, m, bass.ds(k, CONV_SPAN)]
                        w = convw[:, m, bass.ds(k, 1)]
                        if first:
                            v.tensor_scalar(acc[:, m, :], span, w, convw[:, m, TAPS:TAPS + 1], ALU.mult, ALU.add)\
                                .then_inc(conv_step, 1)
                        else:
                            dve.wait_ge(conv_step, (l * TAPS + k - 1) * CM + m + 1)
                            v.scalar_tensor_tensor(acc[:, m, :], span, w, acc[:, m, :], ALU.mult, ALU.add)\
                                .then_inc(conv_step, 1)

                dve.wait_ge(zT_ready, l * 3 + 3)
                dve.wait_ge(pads_set, l * 3 + 3)
                dve.wait_ge(convw_ready, l + 1)
                tap(0, True)
                with dve.Fori(1, PRE_TAPS) as k:
                    tap(k)

                def heads(ap, n=10):
                    return ap.rearrange("p (h d) -> p h d", d=HD)

                def table_b(ap, n):
                    return ap.unsqueeze(1).broadcast_to([P, n, HD])

                def rope(t):
                    dve.wait_ge(proj_taken, l * 9 + 6 + t + 1)
                    if t:
                        dve.wait_ge(rope_ready, l * 3 + t)
                    step.link(v.tensor_tensor(tmp[:, 0, :], qk[:, t, :], qk[:, t, :], ALU.mult))
                    v.tensor_reduce(stats(QKSS, 10), heads(tmp[:, 0, :]), AX.X, ALU.add).then_inc(qk_ss, 1)
                    tap(PRE_TAPS + t)
                    dve.wait_ge(qk_rstd, l * 3 + t + 1)
                    step.link(v.tensor_tensor(heads(qk[:, t, :]), heads(qk[:, t, :]),
                                              stats(QKR, 10).unsqueeze(2).broadcast_to([P, 10, HD]), ALU.mult))
                    q, kk = qk[:, t, 0:QW], qk[:, t, QW:QW + KVW]
                    q_out = h[:, t, 0:QW].rearrange("p (j g d) -> p g j d", g=KV_HEADS, d=HD)

                    def grouped(ap):
                        return ap.rearrange("p (g j d) -> p g j d", g=KV_HEADS, d=HD)

                    dve.wait_ge(zT_ps, l * 3 + 3)
                    if t == 0:
                        qg = qkg[:, 0, :].unsqueeze(1).broadcast_to([P, PAIRS, HD])
                        for gg in range(KV_HEADS):
                            v.tensor_tensor(q_out[:, gg], grouped(q)[:, gg], qg, ALU.mult)
                        v.tensor_tensor(heads(kk), heads(kk), table_b(qkg[:, 1, :], 2), ALU.mult).then_inc(rope_ready, 1)
                        return
                    step.mark(v.tensor_tensor(heads(q), heads(q), table_b(qkg[:, 0, :], HEADS), ALU.mult))
                    step.link(v.tensor_tensor(heads(kk), heads(kk), table_b(qkg[:, 1, :], 2), ALU.mult))
                    step.mark(v.tensor_tensor(heads(tmp[:, 0, :]), heads(qk[:, t, :]), table_b(ropeC[:, t - 1, :], 10),
                                              ALU.mult))

                    def axes(ap, half):
                        return ap.rearrange("p (h a s f) -> p h a s f", a=2, s=2, f=16)[:, :, :, half, :]

                    for half in range(2):
                        sin = ropeS[:, t - 1, :].rearrange("p (a s f) -> p a s f", a=2, s=2)[:, :, half, :]
                        ins = v.tensor_tensor(axes(tmp[:, 1, :], half), axes(qk[:, t, :], 1 - half),
                                              sin.unsqueeze(1).broadcast_to([P, 10, 2, 16]), ALU.mult)
                        (step.link if half else step.mark)(ins)
                    for gg in range(KV_HEADS):
                        v.tensor_tensor(q_out[:, gg], grouped(tmp[:, 0, 0:QW])[:, gg], grouped(tmp[:, 1, 0:QW])[:, gg],
                                        ALU.add)
                    v.tensor_tensor(kk, tmp[:, 0, QW:QW + KVW], tmp[:, 1, QW:QW + KVW], ALU.add).then_inc(rope_ready, 1)

                for t in range(TILES):
                    rope(t)
                    mod_take(l, MOD1 + t)
                for k in range(LATE_TAPS):
                    tap(PRE_TAPS + ROPE_TAPS + k)
                mod_take(l, MOD1 + 3)

                def score_max(hd):
                    for t in range(TILES):
                        dve.wait_ge(s_ps, (l * HEADS + hd) * TILES + t + 1)
                        v.tensor_reduce(stats(NM + TILES * (hd % 2) + t), ps[:, 4 + t, 0:P * len(KEY_CHUNKS[t])], AX.X,
                                        ALU.max, negate=True).then_inc(nmax, 1)

                def head_output(hd):
                    dve.wait_ge(o_ps, l * HEADS + hd + 1)
                    v.reciprocal(stats(RI, TILES), stats(RS + TILES * (hd % 2), TILES)).then_inc(rinv_ready, 1)
                    dve.wait_ge(rinv_ready, l * HEADS + hd + 1)
                    v.tensor_tensor(h[:, :, hd * HD:(hd + 1) * HD],
                                    ps[:, 7, 0:TILES * HD].rearrange("p (t d) -> p t d", d=HD),
                                    stats(RI, TILES).unsqueeze(2).broadcast_to([P, TILES, HD]), ALU.mult)\
                        .then_inc(attn_out, 1)

                def ln_stats(t):
                    dve.wait_ge(back_ps, l * 3 + t + 1)
                    step.link(v.bn_stats(stats(BN, 6), ps[:, BACK[t], :]))
                    v.bn_aggr(stats(LNV, 2), stats(BN, 6)).then_inc(ln_var, 1)

                def ln_normalize(t):
                    dve.wait_ge(ln_rstd, l * 3 + t + 1)
                    v.tensor_scalar(h[:, t, CH:D], ps[:, BACK[t], :], stats(LNV), stats(LNR), ALU.subtract, ALU.mult)\
                        .then_inc(ln_norm, 1)

                score_max(0)
                for hd in range(HEADS):
                    if hd + 1 < HEADS:
                        score_max(hd + 1)
                    if hd < len(HEAD_TAPS):
                        for n in range(HEAD_TAPS[hd]):
                            tap(PRE_TAPS + ROPE_TAPS + LATE_TAPS + sum(HEAD_TAPS[:hd]) + n)
                        if HEAD_FILL[hd][2] == KD:
                            mod_take(l, HEAD_FILL[hd][0])
                    if hd == HEADS - 1:
                        ln_normalize(0)
                    if hd >= HEADS - 2:
                        ln_stats(hd - HEADS + 2)
                    head_output(hd)
                ln_normalize(1)
                ln_stats(2)
                ln_normalize(2)

                dve.wait_ge(bcG_in, l * 32 + 16)
                if l == 0:
                    dve.wait_ge(filled_st, 8 * 16)
                for t in range(TILES):
                    for n in range(2):
                        u = 2 * t + n
                        outp_wait(dve, l, n, t)
                        cols = slice(n * SEG, (n + 1) * SEG)
                        if u >= 2:
                            dve.wait_ge(resid, l * 6 + u - 1)
                        step.link(v.tensor_tensor(part[:, u % 2, :], ps[:, out_bank(t, n), :], gateB[:, group(t), cols],
                                                  ALU.mult))
                        v.tensor_tensor(x[:, t, cols], x[:, t, cols], part[:, u % 2, :], ALU.add).then_inc(resid, 1)
                    norm(1, t)

                o = 0

                def cutr(n):
                    nonlocal o
                    o += n
                    return rt[:, o - n:o]

                NE, NG = TILES * E, TILES * GROUPS
                gt, eq = cutr(NG * 16), cutr(NG * 16)
                sb_, rank, top, sel, pm, hi, lo, sw = (cutr(NE) for _ in range(8))
                gs, grank, gsel = cutr(NG), cutr(NG), cutr(NG)
                pmax, psum, wsum, wr_ = (cutr(TILES) for _ in range(4))
                s_flat = route[:, :, :].rearrange("p t e -> p (t e)")

                def by_tile(ap):
                    return ap.rearrange("p (t e) -> p t e", t=TILES)

                def beats(out_gt, out_eq, scores, n, m):
                    sv = scores.rearrange("p (n m) -> p n m", m=m)
                    mine = sv.unsqueeze(3).broadcast_to([P, n, m, m])
                    other = sv.unsqueeze(2).broadcast_to([P, n, m, m])
                    ov = [a_[:, 0:n * m * m].rearrange("p (n i j) -> p n i j", i=m, j=m) for a_ in (out_gt, out_eq)]
                    before = tie.rearrange("p (i j) -> p i j", i=m).unsqueeze(1).broadcast_to([P, n, m, m])
                    step.mark(v.tensor_tensor(ov[0], other, mine, ALU.is_gt))
                    step.link(v.tensor_tensor(ov[1], other, mine, ALU.is_equal))
                    step.link(v.tensor_tensor(ov[1], ov[1], before, ALU.mult))
                    step.link(v.tensor_tensor(out_gt[:, 0:n * m * m], out_gt[:, 0:n * m * m], out_eq[:, 0:n * m * m],
                                              ALU.add))
                    return out_gt[:, 0:n * m * m].rearrange("p (n j) -> p n j", j=m)

                dve.wait_ge(score_ready, l * 3 + 3)
                step.link(v.tensor_tensor(by_tile(sb_), route[:, :, :], br[:, :].unsqueeze(1).broadcast_to([P, TILES, E]),
                                          ALU.add))
                step.link(v.tensor_reduce(rank, beats(gt, eq, sb_, NG, EPG), AX.X, ALU.add))
                step.link(v.tensor_scalar(top, rank, 2.0, None, ALU.is_lt))
                step.link(v.tensor_tensor(pm, top, sb_, ALU.mult))
                step.link(v.tensor_reduce(gs, pm.rearrange("p (n m) -> p n m", m=EPG), AX.X, ALU.add))
                step.link(v.tensor_reduce(grank, beats(gt, eq, gs, TILES, GROUPS), AX.X, ALU.add))
                step.link(v.tensor_scalar(gsel, grank, 1.0, None, ALU.is_lt))
                v.tensor_tensor(sel.rearrange("p (n m) -> p n m", m=EPG), top.rearrange("p (n m) -> p n m", m=EPG),
                                gsel.unsqueeze(2).broadcast_to([P, NG, EPG]), ALU.mult).then_inc(sel_ready, 1)
                dve.wait_ge(pos_ps, l + 1)
                step.link(v.tensor_tensor(by_tile(pm), by_tile(ps[:, 5, 0:NE]),
                                          slot_base.unsqueeze(1).broadcast_to([P, TILES, E]), ALU.add))
                step.link(v.tensor_tensor(pm, pm, sel, ALU.mult))
                step.mark(v.tensor_reduce(pmax, by_tile(pm), AX.X, ALU.max))
                step.link(v.tensor_reduce(psum, by_tile(pm), AX.X, ALU.add))
                step.link(v.tensor_tensor(psum, psum, pmax, ALU.subtract))
                pick_v = pick[:, :].rearrange("p (t n) -> p t n", n=2)
                v.tensor_copy(pick_v[:, :, 0], psum)
                v.tensor_copy(pick_v[:, :, 1], pmax)
                v.tensor_copy(count[0:1, :], ps[0:1, 5, NE:NE + E]).then_inc(pos_ready, 1)
                mod_take(l, MOD2)
                step.mark(v.tensor_tensor(by_tile(hi), by_tile(pm), pmax.unsqueeze(2).broadcast_to([P, TILES, E]),
                                          ALU.is_equal))
                step.link(v.tensor_tensor(sw, s_flat, sel, ALU.mult))
                step.link(v.tensor_reduce(wsum, by_tile(sw), AX.X, ALU.add))
                step.mark(v.reciprocal(wr_, wsum))
                step.link(v.tensor_tensor(lo, sel, hi, ALU.subtract))
                step.mark(v.tensor_tensor(lo, lo, sw, ALU.mult))
                step.link(v.tensor_tensor(hi, hi, sw, ALU.mult))
                step.mark(v.tensor_reduce(psum, by_tile(lo), AX.X, ALU.add))
                step.link(v.tensor_reduce(pmax, by_tile(hi), AX.X, ALU.add))
                step.mark(v.tensor_tensor(gates[:, :, 0], psum, wr_, ALU.mult))
                step.link(v.tensor_tensor(gates[:, :, 1], pmax, wr_, ALU.mult))
                if l + 1 < LAYERS:
                    mod_take(l, MOD2 + 1)
                    mod_take(l + 1, 0)
                dve.wait_ge(slots_ps, l + 1)
                v.tensor_copy(slot_tok[:, :], ps[:, 6, 0:E * TILES]).then_inc(slots_ready, 1)
                if l + 1 < LAYERS:
                    for c_ in range(1, MOD1):
                        mod_take(l + 1, c_)
                else:
                    mod_take(l, MOD2 + 1)
                dve.wait_ge(pos_ready, l + 1)

                def take_xT(e):
                    for n in range(2):
                        dve.wait_ge(xT_ps, (l * E + e) * 2 + n + 1)
                        ins = v.tensor_copy(xsT[:, n * 512:(n + 1) * 512], ps[:, XT + n, :])
                    ins.then_inc(xsT_ready, 1)

                def expert(i, j, last):
                    e = i * 2 + j
                    dve.wait_ge(sig_ready, l * E + e + 1)
                    v.tensor_tensor(hid, ps[:, GATE, :], hid, ALU.mult).then_inc(silu_ready, 1)
                    dve.wait_ge(silu_ready, l * E + e + 1)
                    dve.wait_ge(up_ps, l * E + e + 1)
                    v.tensor_tensor(hid, ps[:, UP, :], hid, ALU.mult).then_inc(hid_ready, 1)

                    def run(t, at):
                        if past(at * 16):
                            dve.wait_ge(ov_st, at * 16)
                        for n in range(2):
                            dve.wait_ge(ov_xT, at * 2 + n + 1)
                            ins = v.tensor_copy(ov_b[:, n * 512:(n + 1) * 512], ps[:, XT + n, :])
                        ins.then_inc(ov_xsT, 1)
                        dve.wait_ge(ov_sig, at + 1)
                        v.tensor_tensor(ov_a[:, 0:FF], ps[:, GATE, :], ov_a[:, 0:FF], ALU.mult).then_inc(ov_silu, 1)
                        dve.wait_ge(ov_silu, at + 1)
                        dve.wait_ge(ov_up, at + 1)
                        v.tensor_tensor(ov_a[:, 0:FF], ps[:, UP, :], ov_a[:, 0:FF], ALU.mult).then_inc(ov_hid, 1)
                        dve.wait_ge(ov_hT, at + 1)
                        v.tensor_copy(ov_hidT, ps[:, HT, :]).then_inc(ov_hidT_ready, 1)

                    overflow(dve, l, e, run, ((ov_xsT, 1), (ov_silu, 1), (ov_hid, 1), (ov_hidT_ready, 1)))
                    if not last:
                        take_xT(e + 1)
                    dve.wait_ge(hidT_ps, l * E + e + 1)
                    v.tensor_copy(hidT, ps[:, HT, :]).then_inc(hidT_ready, 1)

                take_xT(0)
                expert(0, 0, False)
                expert(0, 1, False)
                with dve.Fori(1, E // 2 - 1) as i:
                    expert(i, 0, False)
                    expert(i, 1, False)
                expert(E // 2 - 1, 0, False)
                expert(E // 2 - 1, 1, True)
            for t in range(TILES):
                combine(LAYERS - 1, t)

        @block.tensor
        def _(pe):
            t_ = nc.tensor
            pe.wait_ge(cs_ready, 1)

            def accumulate(out, stationary, moving, n):
                for k in range(n):
                    mm = pe.matmul(out, stationary(k), moving(k), start=(k == 0), stop=(k == n - 1))
                return mm

            def loaded(n):
                pe.wait_ge(slot_loaded[slot_of(n)], uses(n) * 16)

            def modulation(l, c, k0=0, k1=KD):
                n = mod_item(l, c)
                if k0 == 0:
                    loaded(n)
                for k in range(k0, k1):
                    mm = pe.matmul(ps[0:2, mod_bank(l, c), :], cs[:, :, k], slot_w(slot_of(n))[:, k, :],
                                   start=(k == 0), stop=(k == KD - 1))
                if k1 == KD:
                    mm.then_inc(slot_used[slot_of(n)], 1)

            for c_ in range(MOD1):
                modulation(0, c_)
            pe.wait_ge(table_in, 16)
            pe.wait_ge(mod_done, 1)
            for first, bank in ((2, 4), (0, 0)):
                for n in range(4):
                    c_ = first + n % 2
                    pe.matmul(ps[:, bank + n, :], ident[0:2, n // 2:n // 2 + 1].broadcast_to([2, P]),
                              rowA[:, c_ * SEG:(c_ + 1) * SEG], start=True, stop=True).then_inc(first_bc_ps, 1)
            pe.wait_ge(router_in, 32)
            for l in range(LAYERS):
                if past(l * E):
                    pe.wait_ge(y_taken, l * E)
                def transposed(which, t):
                    for n in range(2 * t, 2 * t + 2):
                        if n >= 4:
                            pe.wait_ge(hT_ready, l * 18 + which * 6 + n - 3)
                        for m in range(4):
                            k = 4 * (n % 2) + m
                            mm = pe.transpose(ps[:, n % 4, m * P:(m + 1) * P], h[:, t, k::KD], ident)
                        mm.then_inc(hT_ps, 1)

                def hT_wait(which, t):
                    pe.wait_ge(hT_ready, l * 18 + which * 6 + 2 * t + 2)

                for t in range(TILES):
                    pe.wait_ge(h_ready, l * 6 + t + 1)
                    transposed(0, t)
                pe.wait_ge(small_in, (l + 1) * 128)
                for m in range(CM):
                    mm = pe.transpose(ps[:, 6, m * (TAPS + 1):(m + 1) * (TAPS + 1)], sg[0:TAPS + 1, m * P:(m + 1) * P],
                                      ident[0:TAPS + 1, 0:TAPS + 1])
                mm.then_inc(convw_ps, 1)

                def project(c, t, n=SEG):
                    g_ = 3 * c + t
                    s = slot_of(IN_AT[l] + c)
                    hT_wait(0, t)
                    loaded(IN_AT[l] + c)
                    if g_ == 2:
                        pe.wait_ge(convw_ready, l + 1)
                    if g_ >= 4:
                        pc, pt = (g_ - 4) // 3, (g_ - 4) % 3
                        if pc == 1:
                            pe.wait_ge(z_ready, l * 3 + pt + 1)
                        else:
                            pe.wait_ge(proj_taken, l * 9 + {0: 0, 2: 3}[pc] + pt + 1)
                    mm = accumulate(ps[:, 4 + g_ % 4, 0:n], lambda k: hT[:, t, k, :], lambda k: slot_w(s, n)[:, k, :], KD)
                    mm.then_inc(*((proj_ps, 1) if t < 2 else (slot_used[s], 1)))

                for c_ in range(2):
                    for t in range(TILES):
                        project(c_, t)
                project(2, 0)
                for t in range(TILES):
                    pe.wait_ge(z_ready, l * 3 + t + 1)
                    for m in range(CM):
                        mm = pe.transpose(ps[:, t, m * P:(m + 1) * P], h[:, t, m * P:(m + 1) * P], ident)
                    mm.then_inc(zT_ps, 1)
                project(2, 1)
                project(2, 2)
                for t in range(TILES):
                    project(3, t, 2 * KVW)

                pe.wait_ge(zT_ready, l * 3 + 3)
                modulation(l, MOD1)
                pe.wait_ge(proj_taken, l * 9 + 9)
                pe.transpose(ps[:, 7, P:2 * P], ck, ident)
                for t in range(TILES):
                    pe.wait_ge(rope_ready, l * 3 + t + 1)
                    for j in range(PAIRS):
                        mm = pe.transpose(ps[:, 4 + t, j * P:(j + 1) * P], h[:, t, j * P:(j + 1) * P], ident)
                    mm.then_inc(qkT_ps, 1)
                    mm = pe.transpose(ps[:, 7, V_CHUNK[t] * P:(V_CHUNK[t] + 1) * P], qk[:, t, QW:QW + KVW], ident)
                    if t == 2:
                        mm.then_inc(qkT_ps, 1)
                    modulation(l, MOD1 + 1 + t)

                def scores(hd, t):
                    g_, j = hd // PAIRS, hd % PAIRS
                    ks = KEY_CHUNKS[t]
                    pe.matmul(ps[:, 4 + t, 0:P * len(ks)], qT[g_ * HD:(g_ + 1) * HD, t, j * P:(j + 1) * P],
                              kT[g_ * HD:(g_ + 1) * HD, ks[0] * P:(ks[-1] + 1) * P], start=True, stop=True).then_inc(s_ps, 1)

                def conv_back(t):
                    if t == 0:
                        pe.wait_ge(conv_step, (l + 1) * (TAPS * CM))
                        pe.wait_ge(mod_taken, l * MODC + MOD2)
                    if t == 2:
                        pe.wait_ge(attn_out, (l + 1) * HEADS)
                    for m in range(CM):
                        mm = pe.transpose(ps[:, BACK[t], m * P:(m + 1) * P], acc[:, m, CONV_OFF[t]:CONV_OFF[t] + P], ident)
                    mm.then_inc(back_ps, 1)

                pe.wait_ge(qkT_ready, l * 4 + 4)
                for t in range(TILES):
                    scores(0, t)
                for hd in range(HEADS):
                    u = l * (HEADS * TILES) + hd * TILES
                    for t in range(TILES):
                        pe.wait_ge(exp_done, u + t + 1)
                        if hd == 0 and t == 0:
                            pe.wait_ge(mod_taken, l * MODC + 2 * MOD1)
                        for n in range(len(KEY_CHUNKS[t])):
                            mm = pe.transpose(ps[:, 1 + t, n * P:(n + 1) * P], prob[:, t, n * P:(n + 1) * P], ident)
                        mm.then_inc(t_ps, 1)
                        if hd + 1 < HEADS:
                            scores(hd + 1, t)
                    if hd < len(HEAD_FILL):
                        c, k0, k1 = HEAD_FILL[hd]
                        if k0 == 0 and c > 8:
                            pe.wait_ge(mod_taken, l * MODC + c)
                        modulation(l, c, k0, k1)
                    else:
                        conv_back(hd - len(HEAD_FILL))
                    if hd:
                        pe.wait_ge(attn_out, l * HEADS + hd)
                    for t in range(TILES):
                        pe.wait_ge(probT_ready, u + t + 1)
                        g_ = hd // PAIRS
                        ks = KEY_CHUNKS[t]
                        mm = accumulate(ps[:, 7, t * HD:(t + 1) * HD], lambda n: probT[:, t, n * P:(n + 1) * P],
                                   lambda n: vall[:, ks[n], g_ * HD:(g_ + 1) * HD], len(ks))
                    mm.then_inc(o_ps, 1)

                conv_back(2)

                def project_out(t, n):
                    u = 2 * t + n
                    s = slot_of(OUT_AT[l] + n)
                    hT_wait(1, t)
                    loaded(OUT_AT[l] + n)
                    if u == 2:
                        pe.wait_ge(ln_norm, l * 3 + 3)
                    if u >= 4:
                        pe.wait_ge(resid, l * 6 + u - 3)
                    mm = accumulate(ps[:, out_bank(t, n), :], lambda k: hT[:, t, k, :], lambda k: slot_w(s)[:, k, :], KD)
                    mm.then_inc(*((outp_ps, 1) if t < 2 else (slot_used[s], 1)))

                def mix_transposed(t):
                    pe.wait_ge(mix_ready, l * 3 + t + 1)
                    transposed(1, t)

                def h2_transposed(t):
                    pe.wait_ge(h_ready, l * 6 + 3 + t + 1)
                    transposed(2, t)

                def router(t):
                    hT_wait(2, t)
                    if t < 2:
                        pe.wait_ge(resid, l * 6 + 3 + t)
                    else:
                        pe.wait_ge(score_ready, l * 3 + 1)
                    accumulate(ps[:, LOGITS[t], 0:E], lambda k: hT[:, t, k, :], lambda k: wr[:, k, :], KD)\
                        .then_inc(logit_ps, 1)

                mix_transposed(0)
                project_out(0, 0)
                mix_transposed(1)
                project_out(0, 1)
                project_out(1, 0)
                mix_transposed(2)
                project_out(1, 1)
                project_out(2, 0)
                h2_transposed(0)
                project_out(2, 1)
                router(0)
                h2_transposed(1)
                router(1)
                h2_transposed(2)
                router(2)

                modulation(l, MOD2, 0, KD // 2)
                pe.wait_ge(sel_ready, l + 1)
                for t in range(TILES):
                    accumulate(ps[:, 5, t * E:(t + 1) * E], lambda k: ones if k < t else tri,
                               lambda k: sel_all[:, k * E:(k + 1) * E], t + 1)
                accumulate(ps[:, 5, TILES * E:(TILES + 1) * E], lambda k: ones,
                           lambda k: sel_all[:, k * E:(k + 1) * E], TILES).then_inc(pos_ps, 1)
                modulation(l, MOD2, KD // 2, KD)
                if l + 1 < LAYERS:
                    modulation(l, MOD2 + 1)
                    modulation(l + 1, 0)
                else:
                    modulation(l, MOD2 + 1, 0, KD // 2)
                pe.wait_ge(slots_in, (l + 1) * 16)
                pe.transpose(ps[:, 6, 0:E * TILES], slot_rows_sb[:, :], ident[0:E * TILES, 0:E * TILES]).then_inc(slots_ps, 1)
                if l + 1 < LAYERS:
                    for c_ in range(1, MOD1):
                        pe.wait_ge(mod_taken, (l + 1) * MODC - 2 + c_)
                        modulation(l + 1, c_)
                else:
                    modulation(l, MOD2 + 1, KD // 2, KD)
                pe.wait_ge(pos_ready, l + 1)

                def expert_slot(j, m):
                    return slot_of(EXP_AT[l] + 3 * j + m)

                def expert_loaded(i, j, m):
                    pe.wait_ge(slot_loaded[expert_slot(j, m)], (i + uses(EXP_AT[l] + 3 * j + m)) * 16)

                def token_transposes(rows, s):
                    for n in range(2):
                        for m in range(4):
                            mm = pe.transpose(ps[:, XT + n, m * P:(m + 1) * P], rows[:, 4 * n + m::KD], ident)
                        mm.then_inc(s, 1)

                def xT(e, i, j):
                    pe.wait_ge(gathered[j], (l * (E // 2) + i + 1) * 16)
                    token_transposes(xs[:, j, :], xT_ps)

                def gate_up(bank, s, src):
                    return accumulate(ps[:, bank, :], lambda k: src[:, k * P:(k + 1) * P],
                                      lambda k: slot_w(s)[:, k, :], KD)

                def hidden_transposes(rows):
                    for k in range(KF):
                        mm = pe.transpose(ps[:, HT, k * P:(k + 1) * P], rows[:, k:FF:KF], ident)
                    return mm

                def down(s, src, n):
                    w = ring[:, s, 0:KF * D].rearrange("p (k n) -> p k n", k=KF)
                    return accumulate(ps[:, YB + n, :], lambda k: src[:, k * P:(k + 1) * P],
                                      lambda k: w[:, k, n * SEG:(n + 1) * SEG], KF)

                def down_main(k, i, j):
                    s = expert_slot(j, 2)
                    pe.wait_ge(hidT_ready, l * E + k + 1)
                    if past(l * E + k):
                        pe.wait_ge(y_taken, l * E + k)
                    expert_loaded(i, j, 2)
                    down(s, hidT, 0).then_inc(y0_ps, 1)
                    down(s, hidT, 1).then_inc(slot_used[s], 1)

                def release(s):
                    pe.matmul(ps[0:1, 7, 0:1], ones[:, 0:1], ones[:, 0:1], start=True, stop=True).then_inc(slot_used[s], 1)

                def expert(i, j, first, last):
                    e = i * 2 + j
                    g0 = l * E + e
                    pe.wait_ge(xsT_ready, g0 + 1)
                    if past(g0):
                        pe.wait_ge(hid_ready, g0)
                    expert_loaded(i, j, 0)
                    gate_up(GATE, expert_slot(j, 0), xsT).then_inc(gate_ps, 1)
                    expert_loaded(i, j, 1)
                    gate_up(UP, expert_slot(j, 1), xsT).then_inc(up_ps, 1)

                    def run(t, at):
                        pe.wait_ge(ov_gathered, at + 1)
                        token_transposes(ov_a, ov_xT)
                        pe.wait_ge(ov_xsT, at + 1)
                        pe.wait_ge(hid_ready, g0 + 1)
                        gate_up(GATE, expert_slot(j, 0), ov_b).then_inc(ov_gate, 1)
                        gate_up(UP, expert_slot(j, 1), ov_b).then_inc(ov_up, 1)
                        pe.wait_ge(ov_hid, at + 1)
                        if past(g0):
                            pe.wait_ge(hidT_ready, g0)
                        hidden_transposes(ov_a).then_inc(ov_hT, 1)
                        pe.wait_ge(ov_hidT_ready, at + 1)
                        if past(g0 if first else g0 - 1):
                            pe.wait_ge(y_taken, g0 if first else g0 - 1)
                        expert_loaded(i, j, 2)
                        down(expert_slot(j, 2), ov_hidT, 0)
                        down(expert_slot(j, 2), ov_hidT, 1).then_inc(ov_y, 1)
                        pe.wait_ge(ov_taken, at + 1)

                    overflow(pe, l, e, run, ((ov_xT, 2), (ov_gate, 1), (ov_up, 1), (ov_hT, 1), (ov_y, 1)))
                    release(expert_slot(j, 0))
                    release(expert_slot(j, 1))
                    if not last:
                        xT(e + 1, i + j, 1 - j)
                    if not first:
                        if j:
                            down_main(e - 1, i, 0)
                        else:
                            down_main(e - 1, i - 1, 1)
                    pe.wait_ge(hid_ready, g0 + 1)
                    hidden_transposes(hid).then_inc(hidT_ps, 1)

                pe.wait_ge(mod_taken, (l + 1) * MODC + (MOD1 if l + 1 < LAYERS else 0))
                xT(0, 0, 0)
                expert(0, 0, True, False)
                expert(0, 1, False, False)
                with pe.Fori(1, E // 2 - 1) as i:
                    expert(i, 0, False, False)
                    expert(i, 1, False, False)
                expert(E // 2 - 1, 0, False, False)
                expert(E // 2 - 1, 1, False, True)
                down_main(E - 1, E // 2 - 1, 1)


_INS = ['x_prompt', 'x_sample', 'cache_k', 'cache_v', 'c', 'c_ctx', 'w_mod', 'b_mod', 'norm1_g', 'norm2_g', 'w_in',
        'q_norm_g', 'k_norm_g', 'conv_dw_w', 'conv_dw_b', 'conv_ln_g', 'conv_ln_b', 'w_out', 'w_router', 'b_router',
        'w_gate', 'w_up', 'w_down']
_OUTS = [(1, 128, 1024), (1, 256, 1024), (1, 2, 128, 2, 64), (1, 2, 128, 2, 64)]


def _table():
    import numpy as np
    p = np.arange(P)
    freqs = (np.float32(10000.0) ** (-np.arange(16, dtype=np.float32) / 16)).astype(np.float32)
    cos, sin = [], []
    for t in range(2):
        n = t * P + p
        ang = np.stack([(n // 64).astype(np.float32)[:, None] * freqs, (n % 64).astype(np.float32)[:, None] * freqs], 1)
        cos.append(np.stack([np.cos(ang), np.cos(ang)], 2).reshape(P, HD))
        sin.append(np.stack([-np.sin(ang), np.sin(ang)], 2).reshape(P, HD))
    i4 = np.arange(4)
    tie = (i4[None, :] < i4[:, None]).astype(np.float32).reshape(1, 16)
    parts = [np.eye(P), (p[:, None] < p[None, :]), np.ones((P, P)), *cos, *sin, np.tile(tie, (P, 1)),
             np.tile(np.arange(E)[None] * CAP, (P, 1)), p[:, None] + P * np.arange(TILES)[None]]
    return np.ascontiguousarray(np.concatenate([a.astype(np.float32) for a in parts], 1))


def kernel(**inputs):
    import numpy as _np
    import concourse.bacc as _bacc
    from concourse.bass_utils import run_bass_kernel_spmd as _run

    nc = _bacc.Bacc("TRN2", target_bir_lowering=False, num_devices=1)
    arrays, args = {}, []
    for name in _INS + ['table']:
        a = _table() if name == 'table' else _np.ascontiguousarray(inputs[name])
        arrays[f"in_{name}_dram"] = a
        args.append(nc.dram_tensor(f"in_{name}_dram", a.shape, mybir.dt.from_np(a.dtype), kind="ExternalInput").ap())
    for i, shape in enumerate(_OUTS):
        args.append(nc.dram_tensor(f"out_{i}_dram", shape, F32, kind="ExternalOutput").ap())
    build(nc, *args)
    r = _run(nc, [arrays], core_ids=[0])
    return tuple(r.results[0][f"out_{i}_dram"] for i in range(len(_OUTS)))
```

```python
from contextlib import ExitStack

import concourse.bass as bass
from concourse import mybir

ALU = mybir.AluOpType
ACT = mybir.ActivationFunctionType
AX = mybir.AxisListType
F32 = mybir.dt.float32
I32 = mybir.dt.int32
U32 = mybir.dt.uint32

P = 128
D = 1024
KD = D // P
LAYERS = 2
TILES = 3
HEADS, KV_HEADS, HD = 8, 2, 64
PAIRS = HEADS // KV_HEADS
QW, KVW = HEADS * HD, KV_HEADS * HD
CH = 512
CM = CH // P
TAPS = 31
PAD = TAPS // 2
CONV_W = 3 * P + 4 * PAD
CONV_OFF = [0, P + 2 * PAD, 2 * P + 2 * PAD]
E = 16
GROUPS = 4
EPG = E // GROUPS
FF = 512
KF = FF // P
CAP = TILES * P
SEG = 512
MODC = 6 * D // SEG
SLOTS = 6
MOD1, MODN, MOD2 = 4, 6, 10
MOD_A, MOD_N, IN_AT, MOD_B, OUT_AT, MOD_G, EXP_AT = [], [], [], [], [], [], []
_n = MOD1
for _l in range(LAYERS):
    MOD_A.append(0 if _l == 0 else MOD_G[_l - 1] + MODC - MOD2)
    MOD_N.append(_n)
    IN_AT.append(MOD_N[_l] + MODN - MOD1)
    MOD_B.append(IN_AT[_l] + 4)
    OUT_AT.append(MOD_B[_l] + MOD2 - MODN)
    MOD_G.append(OUT_AT[_l] + 2)
    EXP_AT.append(MOD_G[_l] + MODC - MOD2 + (MOD1 if _l + 1 < LAYERS else 0))
    _n = EXP_AT[_l] + 3 * E
PROJ = [(0, 0), (1, 0), (0, 1), (0, 2), (1, 1), (1, 2), (2, 0), (3, 0), (2, 1), (3, 1), (2, 2), (3, 2)]
EPS = 1e-6
KEY_CHUNKS = [[0], [1, 2, 3], [1, 2, 3]]
V_CHUNK = [0, 2, 3]
LOGITS = [4, 7, 4]
BACK = [4, 3, 7]

PROMPT_TAPS = [16, 23]
ROPE_AT = [1, 3, 5]
ROPE_TAPS = 6
LATE_TAPS = 4
HEAD_TAPS = [3, 3, 3, 3, 3, 3, 3]
assert ROPE_TAPS + LATE_TAPS + sum(HEAD_TAPS) == TAPS

XT, GATE, UP, HT, YB = 0, 2, 3, 4, 5


class Steps:

    def __init__(self, eng, sem):
        self.eng, self.sem, self.n = eng, sem, 0

    def link(self, ins):
        self.mark(ins)
        self.eng.wait_ge(self.sem, self.n)

    def mark(self, ins):
        self.n += 1
        ins.then_inc(self.sem, 1)


def past(value):
    return not isinstance(value, int) or value > 0


def slot_of(n):
    return n % SLOTS


def uses(n):
    return n // SLOTS + 1


def mod_item(l, c):
    if c < MOD1:
        return MOD_A[l] + c
    if c < MODN:
        return MOD_N[l] + c - MOD1
    return MOD_B[l] + c - MODN if c < MOD2 else MOD_G[l] + c - MOD2


def mod_bank(l, c):
    if c < MOD1:
        return c if l == 0 else (7, 3, 2, 7)[c]
    return (4, 7, 0, 1, 0, 0, 3, 2)[c - MOD1]


HEAD_FILL = [(8 + hd // 4, hd % 4 * (KD // 4), (hd % 4 + 1) * (KD // 4)) for hd in range(HEADS)]


def proj_bank(c, t):
    return 4 + PROJ.index((c, t)) % 4


def taken(c, t):
    return [p for p in PROJ if p[0] != 1].index((c, t)) + 1


def out_bank(t, n):
    return (5, 6, 4, 7)[(2 * t + n) % 4]


def group(t):
    return min(t, 1)


def build(nc, x_prompt, x_sample, cache_k, cache_v, c, c_ctx, w_mod, b_mod, norm1_g, norm2_g, w_in, q_norm_g,
          k_norm_g, conv_dw_w, conv_dw_b, conv_ln_g, conv_ln_b, w_out, w_router, b_router, w_gate, w_up, w_down,
          table, y_prompt, y_sample, new_k, new_v):
    mod_dram = nc.dram_tensor("mod_rows", (2, 6 * D), F32, kind="Internal").ap()
    h2_dram = nc.dram_tensor("h2_rows", (CAP, D), F32, kind="Internal").ap()
    slot_dram = nc.dram_tensor("slot_tokens", (E * CAP, 1), F32, kind="Internal").ap()
    y_dram = nc.dram_tensor("expert_rows", (E * CAP, D), F32, kind="Internal").ap()

    with ExitStack() as ctx:
        ctx.enter_context(nc.allow_non_contiguous_dma(reason="small parameter rows"))

        def sb(name, shape, dt=F32):
            return ctx.enter_context(nc.sbuf_tensor(name, shape, dt))

        def sem(name):
            return ctx.enter_context(nc.semaphore(name))

        ps = ctx.enter_context(nc.psum_tensor("ps", [P, 8, 512], F32))
        ring = sb("ring", [P, SLOTS, KD * SEG])
        x = sb("x", [P, TILES, D])
        shiftB = sb("shiftB", [P, 2, D])
        scaleB = sb("scaleB", [P, 2, D])
        gateB = sb("gateB", [P, 2, D])
        h = sb("h", [P, TILES, D])
        hT = sb("hT", [P, TILES, KD, P])
        table_sb = sb("table_sb", [P, table.shape[1]])
        wr = sb("wr", [P, KD, E])
        br = sb("br", [P, E])
        cc = sb("cc", [P, 2, KD])
        cs = sb("cs", [P, 2, KD])
        qkg = sb("qkg", [P, 2, HD])
        lnB = sb("lnB", [P, 2, CH])
        convw = sb("convw", [P, CM, TAPS + 1])
        stat = sb("stat", [P, 64])
        half_neg = sb("half_neg", [P, 16])
        slot_rows_sb = sb("slot_rows_sb", [E * TILES, P])
        route = sb("route", [P, TILES, E])
        gates = sb("gates", [P, TILES, 2])
        pick = sb("pick", [P, TILES * 2], U32)
        slot_tok = sb("slot_tok", [P, 48], U32)
        count = sb("count", [1, E], I32)
        rowC = sb("rowC", [2, D])
        scr = sb("scr", [P, 9712])

        o = 0

        def cut(n):
            nonlocal o
            o += n
            return scr[:, o - n:o]

        qk = cut(TILES * 640).rearrange("p (t n) -> p t n", t=TILES)
        tmp = cut(2 * 640).rearrange("p (t n) -> p t n", t=2)
        qT = cut(TILES * 512).rearrange("p (t n) -> p t n", t=TILES)
        kT = cut(512)
        acc = cut(CM * CAP).rearrange("p (m n) -> p m n", m=CM)
        zT = cut(CM * CONV_W).rearrange("p (m n) -> p m n", m=CM)
        assert o >= 5120 + (MOD1 + 2) * SEG
        qk_sq = scr[:, TILES * 640 + 2 * 640:2 * TILES * 640 + 2 * 640].rearrange("p (t n) -> p t n", t=TILES)
        vall = cut(4 * KVW).rearrange("p (c n) -> p c n", c=4)
        ck = cut(KVW)
        sg = cut(CH)
        assert o <= 9712
        prob = scr[:, 0:TILES * 384].rearrange("p (t n) -> p t n", t=TILES)
        probT = scr[:, TILES * 384:2 * TILES * 384].rearrange("p (t n) -> p t n", t=TILES)
        part = qk[:, 0:2, 0:SEG]
        rowA, gainA = scr[0:2, 5120:5120 + MOD1 * SEG], scr[0:2, 5120 + MOD1 * SEG:5120 + (MOD1 + 2) * SEG]
        rowB, rowS, rowG = scaleB[0:2, 0], shiftB[0:2, 0], scaleB[0:2, 0]
        gainB = hT[0:2, 0].rearrange("p k n -> p (k n)")
        o = 0
        xs = cut(2 * D).rearrange("p (b n) -> p b n", b=2)
        xsT = cut(D)
        hid = cut(FF)
        hidT = cut(FF)
        ybuf = cut(D)
        ov_a = cut(D)
        ov_b = cut(D)
        ov_hidT = cut(FF)
        rt = ybuf
        sel_all = rt[:, 528:576]
        pick_buf = [(xs[:, 0, :], xs[:, 1, :]), (xsT, ybuf), (ov_a, ov_b)]

        o = 0

        def col(n):
            nonlocal o
            o += n
            return table_sb[:, o - n:o]

        ident, tri, ones = col(P), col(P), col(P)
        ropeC = col(2 * HD).rearrange("p (t n) -> p t n", t=2)
        ropeS = col(2 * HD).rearrange("p (t n) -> p t n", t=2)
        tie = col(16)
        slot_base = col(E)
        tok_id = col(TILES)

        x_in = sem("x_in"); table_in = sem("table_in"); c_in = sem("c_in"); router_in = sem("router_in")
        rowB_in = sem("rowB_in"); gain_in = sem("gain_in"); small_in = sem("small_in")
        modA_st = sem("modA_st"); modB_st = sem("modB_st"); modG_st = sem("modG_st"); rowC_in = sem("rowC_in")
        modC_st = sem("modC_st"); rowG_in = sem("rowG_in"); rowA_in = sem("rowA_in")
        bcA_in = sem("bcA_in"); bcG_in = sem("bcG_in")
        slot_loaded = [sem(f"slot_loaded{s}") for s in range(SLOTS)]
        slot_used = [sem(f"slot_used{s}") for s in range(SLOTS)]
        first_half = sem("first_half"); cache_st = sem("cache_st"); h2_st = sem("h2_st")
        zero_st = sem("zero_st"); filled_st = sem("filled_st")
        scatter_st = sem("scatter_st"); slots_in = sem("slots_in"); y_st = sem("y_st")
        gathered = [sem(f"gathered{b}") for b in range(2)]
        picked = [sem(f"picked{t}") for t in range(TILES)]
        out_st = sem("out_st")
        first_bc_ps = sem("first_bc_ps")
        convw_ps = sem("convw_ps"); hT_ps = sem("hT_ps"); proj_ps = sem("proj_ps"); zT_ps = sem("zT_ps")
        qkT_ps = sem("qkT_ps"); s_ps = sem("s_ps"); t_ps = sem("t_ps"); o_ps = sem("o_ps"); back_ps = sem("back_ps")
        outp_ps = sem("outp_ps"); logit_ps = sem("logit_ps"); pos_ps = sem("pos_ps"); slots_ps = sem("slots_ps")
        xT_ps = sem("xT_ps"); gate_ps = sem("gate_ps"); up_ps = sem("up_ps"); hidT_ps = sem("hidT_ps")
        y0_ps = sem("y0_ps")
        cs_ready = sem("cs_ready"); first_shift = sem("first_shift"); mod_taken = sem("mod_taken")
        mod_done = sem("mod_done"); ln_norm = sem("ln_norm")
        convw_ready = sem("convw_ready"); h_ready = sem("h_ready"); z_ready = sem("z_ready")
        qk_ss = sem("qk_ss"); qk_squared = sem("qk_squared"); rope_ready = sem("rope_ready"); nmax = sem("nmax")
        attn_out = sem("attn_out")
        conv_step = [sem("conv_prompt_step"), sem("conv_sample_step")]; ln_var = sem("ln_var")
        ln_out = sem("ln_out"); mix_ready = sem("mix_ready")
        resid = sem("resid"); sel_ready = sem("sel_ready"); pos_ready = sem("pos_ready")
        slots_ready = sem("slots_ready"); hid_ready = sem("hid_ready"); xsT_ready = sem("xsT_ready")
        hidT_ready = sem("hidT_ready"); combined = sem("combined"); rinv_ready = sem("rinv_ready")
        silu_ready = sem("silu_ready"); dve_step = sem("dve_step")
        first_scale = sem("first_scale"); scaled = sem("scaled")
        c_sig = sem("c_sig"); sumsq = sem("sumsq"); hT_ready = sem("hT_ready"); proj_taken = sem("proj_taken")
        zT_ready = sem("zT_ready"); qkT_ready = sem("qkT_ready"); exp_done = sem("exp_done")
        probT_ready = sem("probT_ready"); ln_sig = sem("ln_sig"); score_ready = sem("score_ready")
        sig_ready = sem("sig_ready"); y_taken = sem("y_taken")
        const_set = sem("const_set"); pads_set = sem("pads_set"); rstd_ready = sem("rstd_ready")
        pool_step = sem("pool_step"); qk_rstd = sem("qk_rstd"); ln_rstd = sem("ln_rstd")
        ov_dma = sem("ov_dma")
        ov_gathered = sem("ov_gathered");  ov_xT = sem("ov_xT"); ov_xsT = sem("ov_xsT"); ov_gate = sem("ov_gate")
        ov_up = sem("ov_up"); ov_sig = sem("ov_sig"); ov_hid = sem("ov_hid"); ov_silu = sem("ov_silu")
        ov_hT = sem("ov_hT")
        ov_hidT_ready = sem("ov_hidT_ready"); ov_y = sem("ov_y"); ov_taken = sem("ov_taken"); ov_st = sem("ov_st")

        w_mod_v = w_mod.rearrange("l (p k) n -> l p k n", k=KD)
        w_in_v = w_in.rearrange("l (p k) n -> l p k n", k=KD)
        w_out_v = w_out.rearrange("l (k p) n -> l p k n", k=KD)
        w_gate_v = w_gate.rearrange("l e (p k) n -> l e p k n", k=KD)
        w_up_v = w_up.rearrange("l e (p k) n -> l e p k n", k=KD)
        w_down_v = w_down.rearrange("l e (p k) n -> l e p (k n)", k=KF)
        y_rows = y_dram.rearrange("(e t p) n -> (e t) p n", t=TILES, p=P)
        slot_rows = slot_dram.rearrange("(r n) o -> r (n o)", n=P)

        def slot_w(s, n=SEG):
            return ring[:, s, 0:KD * n].rearrange("p (k n) -> p k n", k=KD)

        def stats(a, n=1):
            return stat[:, a:a + n]

        SS1, R1, QKSS, QKR, LNV, LNR, NM, RS, RI = 0, 3, 6, 16, 26, 34, 37, 43, 49
        BN = 52

        block = ctx.enter_context(nc.Block())

        @block.sync
        def _(sp):
            def load(n, src, size=SEG):
                if past(n // SLOTS):
                    sp.wait_ge(slot_used[slot_of(n)], n // SLOTS)
                sp.dma_start(slot_w(slot_of(n), size), src).then_inc(slot_loaded[slot_of(n)], 16)

            def load_mod(l, c):
                load(mod_item(l, c), w_mod_v[l, :, :, c * SEG:(c + 1) * SEG])

            sp.dma_start(cc[:, 0, :], c_ctx.rearrange("(p k) -> p k", k=KD)).then_inc(c_in, 16)
            sp.dma_start(cc[:, 1, :], c[0].rearrange("(p k) -> p k", k=KD)).then_inc(c_in, 16)
            half = KD // 2
            sp.dma_start(slot_w(0)[:, 0:half, :], w_mod_v[0, :, 0:half, 0:SEG]).then_inc(first_half, 16)
            sp.dma_start(slot_w(0)[:, half:KD, :], w_mod_v[0, :, half:KD, 0:SEG]).then_inc(slot_loaded[0], 16)
            for c_ in range(1, MOD1):
                load_mod(0, c_)
            sp.dma_start(x[:, 0, :], x_prompt[0]).then_inc(x_in, 16)
            sp.dma_start(x[:, 1:3, :], x_sample[0].rearrange("(t p) n -> p t n", p=P)).then_inc(x_in, 16)
            for l in range(LAYERS):
                for c_ in range(MOD1, MODN):
                    load_mod(l, c_)
                for m, (c0, n) in enumerate(((QW + 2 * KVW + CH, CH), (QW + 2 * KVW, CH), (0, QW), (QW, 2 * KVW))):
                    if l and m == 2:
                        sp.wait_ge(combined, (l - 1) * TILES + 2)
                    load(IN_AT[l] + m, w_in_v[l, :, :, c0:c0 + n], n)
                for c_ in range(MODN, MOD2):
                    load_mod(l, c_)
                for n in range(2):
                    load(OUT_AT[l] + n, w_out_v[l, :, :, n * SEG:(n + 1) * SEG])
                for c_ in range(MOD2, MODC):
                    load_mod(l, c_)
                if l + 1 < LAYERS:
                    for c_ in range(MOD1):
                        load_mod(l + 1, c_)
                with sp.Fori(0, E // 2) as i:
                    for j in range(2):
                        for m, w in enumerate((w_gate_v, w_up_v, w_down_v)):
                            n = EXP_AT[l] + 3 * j + m
                            s = slot_of(n)
                            sp.wait_ge(slot_used[s], i + n // SLOTS)
                            src = w[bass.ds(l, 1), bass.ds(i * 2 + j, 1)]
                            if m < 2:
                                sp.dma_start(slot_w(s), src.rearrange("l e p k n -> (l e p) k n"))\
                                    .then_inc(slot_loaded[s], 16)
                            else:
                                sp.dma_start(ring[:, s, 0:KF * D], src.rearrange("l e p n -> (l e p) n"))\
                                    .then_inc(slot_loaded[s], 16)
            for t in range(TILES):
                sp.wait_ge(combined, (LAYERS - 1) * TILES + t + 1)
                out = y_prompt[0] if t == 0 else y_sample[0, (t - 1) * P:t * P, :]
                sp.dma_start(out, x[:, t, :]).then_inc(out_st, 16)
            sp.wait_ge(out_st, TILES * 16)

        def overflow(eng, l, e, run, signals):
            at = (l * E + e) * 2
            n = eng.value_load(count[0:1, bass.ds(e, 1)], min_val=0, max_val=CAP)

            def skip(first, tiles):
                for s, by in signals:
                    if past(first):
                        eng.wait_ge(s, first * by)
                    eng.sem_inc(s, by * tiles)

            with eng.If(n > P):
                run(1, at)
                with eng.If(n > 2 * P):
                    run(2, at + 1)
                with eng.Else():
                    skip(at + 1, 1)
            with eng.Else():
                skip(at, 2)

        @block.gpsimd
        def _(pool):
            g = nc.gpsimd
            step = Steps(pool, pool_step)
            ov_count = pool.alloc_register("ov_count")
            pool.reg_mov(ov_count, 16)
            g.memset(half_neg[:, :], -0.5).then_inc(const_set, 1)
            g.memset(slot_rows_sb[:, :], 0.0).then_inc(const_set, 1)
            pool.wait_ge(const_set, 2)
            pool.dma_start(slot_rows, slot_rows_sb[:, :]).then_inc(zero_st, 16)
            pool.wait_ge(zero_st, 16)
            pool.wait_ge(table_in, 16)

            def rstd(out, in_, n, scale, eps):
                step.link(g.tensor_scalar(out, in_, scale, eps, ALU.mult, ALU.add))
                return g.tensor_tensor(out, out, half_neg[:, 0:n], ALU.pow)

            def spread(dst, j, s):
                pool.dma_start(dst, mod_dram[:, j * D:(j + 1) * D].partition_broadcast(P)).then_inc(s, 16)

            def norm_rstd(which, l, t):
                pool.wait_ge(sumsq, l * 6 + which * 3 + t + 1)
                rstd(stats(R1 + t), stats(SS1 + t), 1, 1.0 / D, EPS).then_inc(rstd_ready, 1)

            def mod_a(l):
                pool.wait_ge(mod_done, 2 * l + 1)
                pool.dma_start(mod_dram[:, 0:MOD1 * SEG], rowA).then_inc(modA_st, 16)
                pool.wait_ge(modA_st, l * 16)
                pool.wait_ge(h_ready, l * 6)
                spread(scaleB[:, :, :], 1, bcA_in)
                spread(shiftB[:, :, :], 0, bcA_in)

            pool.dma_start(rowC[:, :], b_mod[0:1, 2 * D:3 * D].broadcast_to([2, D])).then_inc(rowC_in, 16)
            for t in range(TILES):
                norm_rstd(0, 0, t)
            for l in range(LAYERS):
                if l:
                    for t in range(TILES):
                        norm_rstd(0, l, t)
                pool.wait_ge(h_ready, l * 6 + 3)
                pool.dma_start(rowB, b_mod[l:l + 1, 3 * D:4 * D].broadcast_to([2, D])).then_inc(rowB_in, 16)
                pool.dma_start(rowS, b_mod[l:l + 1, 4 * D:5 * D].broadcast_to([2, D])).then_inc(rowB_in, 16)
                g.memset(zT[:, :, 0:PAD], 0.0).then_inc(pads_set, 1)
                g.memset(zT[:, :, PAD + P:PAD + P + 2 * PAD], 0.0).then_inc(pads_set, 1)
                g.memset(zT[:, :, CONV_W - PAD:CONV_W], 0.0).then_inc(pads_set, 1)
                if l == 0:
                    for n in range(4):
                        for t in range(1, TILES):
                            pool.dma_start(y_dram.rearrange("(e t p) n -> p e t n", t=TILES, p=P)[:, 4 * n:4 * n + 4, t, :],
                                           x[:, 0, :].unsqueeze(1).broadcast_to([P, 4, D])).then_inc(filled_st, 16)
                pool.wait_ge(mod_taken, l * MODC + MODN)
                pool.dma_start(mod_dram[:, 2 * D:3 * D], rowC[:, :]).then_inc(modC_st, 16)
                pool.wait_ge(modC_st, (l + 1) * 16)
                spread(gateB[:, :, :], 2, bcG_in)
                if l + 1 < LAYERS:
                    pool.dma_start(rowC[:, :], b_mod[l + 1:l + 2, 2 * D:3 * D].broadcast_to([2, D])).then_inc(rowC_in, 16)
                for t in range(TILES):
                    pool.wait_ge(qk_ss, l * 3 + t + 1)
                    step.link(g.tensor_scalar(stats(QKR, HEADS), stats(QKSS, HEADS), 1.0, HD * EPS, ALU.mult, ALU.add))
                    step.link(g.tensor_scalar(stats(QKR + HEADS, 2), stats(QKSS + HEADS, 2), 1.0 / HD, EPS,
                                              ALU.mult, ALU.add))
                    g.tensor_tensor(stats(QKR, 10), stats(QKR, 10), half_neg[:, 0:10], ALU.pow).then_inc(qk_rstd, 1)
                    if t == 0:
                        pool.wait_ge(rope_ready, l * 3 + 1)
                        pool.wait_ge(proj_taken, l * 9 + taken(3, 0))
                        pool.dma_start(new_k[:, l].rearrange("b s h d -> (b s) (h d)"),
                                       qk[:, 0, QW:QW + KVW]).then_inc(cache_st, 16)
                        pool.dma_start(new_v[:, l].rearrange("b s h d -> (b s) (h d)"),
                                       vall[:, 0, :]).then_inc(cache_st, 16)
                pool.wait_ge(slot_used[slot_of(IN_AT[l] + 3)], uses(IN_AT[l] + 3))
                pool.dma_start(gainB, norm2_g[l:l + 1, :].broadcast_to([2, D])).then_inc(gain_in, 16)
                pool.wait_ge(mod_done, 2 * l + 2)
                pool.dma_start(mod_dram[:, 3 * D:4 * D], rowB).then_inc(modB_st, 16)
                pool.dma_start(mod_dram[:, 4 * D:5 * D], rowS).then_inc(modB_st, 16)
                pool.wait_ge(cache_st, l * 32 + 32)

                def ln_affine(t):
                    z = h[:, t, CH:D]
                    pool.wait_ge(ln_norm, l * 3 + t + 1)
                    step.link(g.tensor_tensor(z, z, lnB[:, 0, :], ALU.mult))
                    g.tensor_tensor(z, z, lnB[:, 1, :], ALU.add).then_inc(ln_out, 1)

                def ln_silu(t):
                    pool.wait_ge(ln_sig, l * 3 + t + 1)
                    g.tensor_tensor(h[:, t, CH:D], h[:, t, CH:D], sg, ALU.mult).then_inc(mix_ready, 1)

                for t in range(TILES):
                    pool.wait_ge(ln_var, l * 3 + t + 1)
                    rstd(stats(LNR, 1), stats(LNV + 1, 1), 1, 1.0, EPS).then_inc(ln_rstd, 1)
                    ln_affine(t)
                    if t:
                        ln_silu(t - 1)
                ln_silu(2)
                pool.wait_ge(modB_st, l * 32 + 32)
                spread(scaleB[:, :, :], 4, bcA_in)
                spread(shiftB[:, :, :], 3, bcA_in)
                for t in range(TILES):
                    norm_rstd(1, l, t)
                pool.wait_ge(h_ready, l * 6 + 6)
                pool.dma_start(rowG, b_mod[l:l + 1, 5 * D:6 * D].broadcast_to([2, D])).then_inc(rowG_in, 16)
                pool.wait_ge(pos_ready, l + 1)
                for n in range(TILES * 2):
                    pool.indirect_dma_start(out=slot_dram,
                                            out_offset=bass.IndirectOffsetOnAxis(ap=pick[:, n:n + 1], axis=0),
                                            in_=tok_id[:, n // 2:n // 2 + 1], in_offset=None).then_inc(scatter_st, 16)
                pool.wait_ge(scatter_st, (l + 1) * (2 * TILES * 16))
                pool.dma_start(slot_rows_sb[:, :], slot_rows).then_inc(slots_in, 16)
                pool.wait_ge(slots_ready, l + 1)

                def gather(e):
                    pool.indirect_dma_start(out=xs[:, e % 2, :], out_offset=None, in_=h2_dram,
                                            in_offset=bass.IndirectOffsetOnAxis(
                                                ap=slot_tok[:, e * TILES:e * TILES + 1], axis=0))\
                        .then_inc(gathered[e % 2], 16)

                pool.wait_ge(h2_st, (l + 1) * (TILES * 16))
                gather(0)
                gather(1)
                pool.wait_ge(mod_taken, (l + 1) * MODC)
                pool.dma_start(mod_dram[:, 5 * D:6 * D], rowG).then_inc(modG_st, 16)
                pool.wait_ge(modG_st, (l + 1) * 16)
                spread(gateB[:, :, :], 5, bcG_in)
                if l + 1 < LAYERS:
                    mod_a(l + 1)
                for e in range(E):
                    def run(t, at):
                        if past(at):
                            pool.wait_ge(ov_hT, at)
                        pool.indirect_dma_start(out=ov_a, out_offset=None, in_=h2_dram,
                                                in_offset=bass.IndirectOffsetOnAxis(
                                                    ap=slot_tok[:, e * TILES + t:e * TILES + t + 1], axis=0))\
                            .then_inc(ov_dma, 16)
                        pool.wait_ge(ov_dma, pool.snap(ov_count))
                        pool.reg_add(ov_count, ov_count, 16)
                        pool.sem_inc(ov_gathered, 1)

                    overflow(pool, l, e, run, ((ov_gathered, 1),))
                    if e + 2 < E:
                        pool.wait_ge(xT_ps, (l * E + e + 1) * 2)
                        gather(e + 2)

                pool.wait_ge(y_st, (l + 1) * (E * 16))
                pool.wait_ge(ov_st, (l + 1) * (2 * E * 16))
                for t in range(TILES):
                    for n in range(2):
                        pool.indirect_dma_start(out=pick_buf[t][n], out_offset=None, in_=y_dram,
                                                in_offset=bass.IndirectOffsetOnAxis(ap=pick[:, 2 * t + n:2 * t + n + 1], axis=0))\
                            .then_inc(picked[t], 16)

        def proj_wait(eng, l, c, t):
            if t < 2:
                eng.wait_ge(proj_ps, l * 8 + [p for p in PROJ if p[1] < 2].index((c, t)) + 1)
            else:
                eng.wait_ge(slot_used[slot_of(IN_AT[l] + c)], uses(IN_AT[l] + c))

        def outp_wait(eng, l, n, t):
            if t < 2:
                eng.wait_ge(outp_ps, l * 4 + 2 * t + n + 1)
            else:
                eng.wait_ge(slot_used[slot_of(OUT_AT[l] + n)], uses(OUT_AT[l] + n))

        @block.scalar
        def _(act):
            a = nc.scalar

            def small_loads(l):
                act.dma_start(rowA, b_mod[l:l + 1, 0:MOD1 * SEG].broadcast_to([2, MOD1 * SEG])).then_inc(rowA_in, 16)
                act.dma_start(gainA, norm1_g[l:l + 1, :].broadcast_to([2, D])).then_inc(rowA_in, 16)
                act.dma_start(sg[0:TAPS, :], conv_dw_w[l]).then_inc(small_in, 16)
                act.dma_start(sg[TAPS:TAPS + 1, :], conv_dw_b[l:l + 1, :]).then_inc(small_in, 16)
                act.dma_start(vall[:, 1, :], cache_v[:, l].rearrange("b s h d -> (b s) (h d)")).then_inc(small_in, 16)
                act.dma_start(ck, cache_k[:, l].rearrange("b s h d -> (b s) (h d)")).then_inc(small_in, 16)
                act.dma_start(qkg[:, 0, :], q_norm_g[l:l + 1, :].broadcast_to([P, HD])).then_inc(small_in, 16)
                act.dma_start(qkg[:, 1, :], k_norm_g[l:l + 1, :].broadcast_to([P, HD])).then_inc(small_in, 16)
                act.dma_start(lnB[:, 0, :], conv_ln_g[l:l + 1, :].broadcast_to([P, CH])).then_inc(small_in, 16)
                act.dma_start(lnB[:, 1, :], conv_ln_b[l:l + 1, :].broadcast_to([P, CH])).then_inc(small_in, 16)

            act.dma_start(table_sb[:, :], table).then_inc(table_in, 16)
            act.wait_ge(c_in, 32)
            a.activation(cs[:, :, :], cc[:, :, :], ACT.Sigmoid).then_inc(c_sig, 1)
            act.dma_start(wr[:, :, :], w_router.rearrange("(p k) e -> p k e", k=KD)).then_inc(router_in, 16)
            act.dma_start(br[:, :], b_router.partition_broadcast(P)).then_inc(router_in, 16)
            small_loads(0)
            act.wait_ge(x_in, 32)

            def scale_pick(l, t):
                act.wait_ge(picked[t], (l + 1) * 32)
                a.activation(pick_buf[t][0], pick_buf[t][0], ACT.Copy, scale=gates[:, t, 0:1]).then_inc(scaled, 1)

            for l in range(LAYERS):
                def square_sum(t):
                    a.activation(h[:, t, :], x[:, t, :], ACT.Square, accum_out=stats(SS1 + t)).then_inc(sumsq, 1)

                def take_hT(which, t):
                    for n in range(2 * t, 2 * t + 2):
                        act.wait_ge(hT_ps, l * 18 + which * 6 + n + 1)
                        a.copy(hT[:, n // 2, 4 * (n % 2):4 * (n % 2) + 4, :].rearrange("p k n -> p (k n)"),
                               ps[:, n % 4, :]).then_inc(hT_ready, 1)

                for t in range(TILES):
                    if l:
                        if t == 0:
                            for n in range(TILES):
                                scale_pick(l - 1, n)
                        act.wait_ge(combined, (l - 1) * TILES + t + 1)
                    square_sum(t)
                if l == 0:
                    for n in range(4):
                        act.wait_ge(first_bc_ps, n + 1)
                        a.copy(scaleB[:, n // 2, n % 2 * SEG:(n % 2 + 1) * SEG], ps[:, 4 + (n + 1) % 4, :]).then_inc(first_scale, 1)
                for t in range(TILES):
                    take_hT(0, t)

                def take_mixT(t, half):
                    n = 3 * half + t
                    act.wait_ge(hT_ps, l * 18 + 6 + n + 1)
                    a.copy(hT[:, t, 4 * half:4 * half + 4, :].rearrange("p k n -> p (k n)"), ps[:, n % 4, :])\
                        .then_inc(hT_ready, 1)

                def h2_tile(t):
                    act.wait_ge(h_ready, l * 6 + 4 + t)
                    act.dma_start(h2_dram[t * P:(t + 1) * P, :], h[:, t, :]).then_inc(h2_st, 16)
                    take_hT(2, t)
                    act.wait_ge(logit_ps, l * 3 + t + 1)
                    a.activation(route[:, t, :], ps[:, LOGITS[t], 0:E], ACT.Sigmoid).then_inc(score_ready, 1)

                def gate_sigmoid(t):
                    proj_wait(act, l, 0, t)
                    a.activation(h[:, t, 0:CH], ps[:, proj_bank(0, t), :], ACT.Sigmoid).then_inc(proj_taken, 1)

                def queries(t):
                    proj_wait(act, l, 2, t)
                    a.copy(qk[:, t, 0:QW], ps[:, proj_bank(2, t), :]).then_inc(proj_taken, 1)

                def take_zT(t):
                    act.wait_ge(zT_ps, l * 3 + t + 1)
                    a.copy(zT[:, :, PAD + CONV_OFF[t]:PAD + CONV_OFF[t] + P],
                           ps[:, t, :].rearrange("p (m n) -> p m n", m=CM)).then_inc(zT_ready, 1)

                gate_sigmoid(0)
                gate_sigmoid(1)
                take_zT(0)
                gate_sigmoid(2)
                queries(0)
                take_zT(1)
                take_zT(2)
                for t in range(TILES):
                    if t:
                        queries(t)
                    proj_wait(act, l, 3, t)
                    a.copy(qk[:, t, QW:QW + KVW], ps[:, proj_bank(3, t), 0:KVW])
                    a.copy(vall[:, V_CHUNK[t], :], ps[:, proj_bank(3, t), KVW:2 * KVW]).then_inc(proj_taken, 1)
                    act.wait_ge(proj_taken, l * 9 + taken(3, t))
                    a.activation(qk_sq[:, t, :], qk[:, t, :], ACT.Square).then_inc(qk_squared, 1)
                for t in range(TILES):
                    act.wait_ge(qkT_ps, l * 4 + t + 1)
                    a.copy(qT[:, t, :], ps[:, 4 + t, :]).then_inc(qkT_ready, 1)
                act.wait_ge(qkT_ps, l * 4 + 4)
                a.copy(kT, ps[:, 7, :]).then_inc(qkT_ready, 1)
                act.wait_ge(cache_st, l * 32 + 32)
                def softmax(hd, odd):
                    for t in range(TILES):
                        n = P * len(KEY_CHUNKS[t])
                        act.wait_ge(nmax, (l * HEADS + hd) * TILES + t + 1)
                        a.activation(prob[:, t, 0:n], ps[:, 4 + t, 0:n], ACT.Exp, bias=stats(NM + TILES * odd + t),
                                     accum_out=stats(RS + TILES * odd + t)).then_inc(exp_done, 1)

                def take_probT(hd):
                    for t in range(TILES):
                        n = P * len(KEY_CHUNKS[t])
                        act.wait_ge(t_ps, (l * HEADS + hd) * TILES + t + 1)
                        a.copy(probT[:, t, 0:n], ps[:, 1 + t, 0:n]).then_inc(probT_ready, 1)

                softmax(0, 0)
                with act.Fori(0, HEADS // 2 - 1) as i:
                    for j in range(2):
                        take_probT(i * 2 + j)
                        softmax(i * 2 + j + 1, 1 - j)
                take_probT(HEADS - 2)
                softmax(HEADS - 1, 1)
                take_probT(HEADS - 1)
                for t in range(TILES):
                    take_mixT(t, 0)
                for t in range(TILES):
                    act.wait_ge(ln_out, l * 3 + t + 1)
                    if past(l * 3 + t):
                        act.wait_ge(mix_ready, l * 3 + t)
                    a.activation(sg, h[:, t, CH:D], ACT.Sigmoid).then_inc(ln_sig, 1)
                    if t:
                        take_mixT(t - 1, 1)
                take_mixT(2, 1)
                if l + 1 < LAYERS:
                    act.wait_ge(mix_ready, l * 3 + 3)
                    small_loads(l + 1)
                for t in range(TILES):
                    act.wait_ge(resid, l * 6 + 2 * t + 2)
                    square_sum(t)
                    if t:
                        h2_tile(t - 1)
                h2_tile(2)
                act.wait_ge(pos_ready, l + 1)

                def take_y(k, i, j):
                    if past((l * E + k) * 16):
                        act.wait_ge(y_st, (l * E + k) * 16)
                    act.wait_ge(y0_ps, l * E + k + 1)
                    a.copy(ybuf[:, 0:SEG], ps[:, YB, :])
                    act.wait_ge(slot_used[slot_of(EXP_AT[l] + 3 * j + 2)], i + uses(EXP_AT[l] + 3 * j + 2))
                    a.copy(ybuf[:, SEG:D], ps[:, YB + 1, :]).then_inc(y_taken, 1)
                    act.wait_ge(y_taken, l * E + k + 1)
                    act.dma_start(y_rows[bass.ds(k * TILES, 1)].rearrange("r p n -> (r p) n"), ybuf).then_inc(y_st, 16)

                def expert(i, j, first):
                    e = i * 2 + j
                    act.wait_ge(gate_ps, l * E + e + 1)
                    a.activation(hid, ps[:, GATE, :], ACT.Sigmoid).then_inc(sig_ready, 1)

                    def run(t, at):
                        act.wait_ge(ov_gate, at + 1)
                        a.activation(ov_a[:, 0:FF], ps[:, GATE, :], ACT.Sigmoid).then_inc(ov_sig, 1)
                        act.wait_ge(ov_y, at + 1)
                        a.copy(ov_b, ps[:, YB:YB + 2, :].rearrange("p b n -> p (b n)")).then_inc(ov_taken, 1)
                        act.wait_ge(ov_taken, at + 1)
                        act.dma_start(y_rows[bass.ds(e * TILES + t, 1)].rearrange("r p n -> (r p) n"), ov_b)\
                            .then_inc(ov_st, 16)

                    overflow(act, l, e, run, ((ov_sig, 1), (ov_taken, 1), (ov_st, 16)))
                    if not first:
                        if j:
                            take_y(e - 1, i, 0)
                        else:
                            take_y(e - 1, i - 1, 1)

                expert(0, 0, True)
                expert(0, 1, False)
                with act.Fori(1, E // 2) as i:
                    expert(i, 0, False)
                    expert(i, 1, False)
                take_y(E - 1, E // 2 - 1, 1)
            for t in range(TILES):
                scale_pick(LAYERS - 1, t)

        @block.vector
        def _(dve):
            v = nc.vector
            step = Steps(dve, dve_step)
            dve.wait_ge(c_sig, 1)
            v.tensor_tensor(cs[:, :, :], cs[:, :, :], cc[:, :, :], ALU.mult).then_inc(cs_ready, 1)

            def mod_take(l, c):
                n = mod_item(l, c)
                if c == 0:
                    dve.wait_ge(rowA_in, (l + 1) * 32)
                if c == MOD1:
                    dve.wait_ge(rowC_in, (l + 1) * 16)
                if c == MODN:
                    dve.wait_ge(rowB_in, (l + 1) * 32)
                if c == MOD2:
                    dve.wait_ge(rowG_in, (l + 1) * 16)
                half = slice(c % 2 * SEG, (c % 2 + 1) * SEG)
                if c < MOD1:
                    row = rowA[:, c * SEG:(c + 1) * SEG]
                else:
                    row = (rowC, rowB, rowS, rowG)[(c - MOD1) // 2][:, half]
                dve.wait_ge(slot_used[slot_of(n)], uses(n))
                v.tensor_tensor(row, ps[0:2, mod_bank(l, c), :], row, ALU.add).then_inc(mod_taken, 1)
                if c // 2 in (1, 4):
                    if c == 8:
                        dve.wait_ge(gain_in, (l + 1) * 16)
                    dve.wait_ge(mod_taken, l * MODC + c + 1)
                    gain = (gainA if c < MOD1 else gainB)[:, half]
                    ins = v.scalar_tensor_tensor(row, row, 1.0, gain, ALU.add, ALU.mult)
                    if c % 2:
                        ins.then_inc(mod_done, 1)

            def combine(l, t):
                dve.wait_ge(bcG_in, l * 32 + 32)
                a0, a1 = pick_buf[t]
                dve.wait_ge(picked[t], (l + 1) * 32)
                dve.wait_ge(scaled, l * TILES + t + 1)
                step.link(v.scalar_tensor_tensor(a0, a1, gates[:, t, 1:2], a0, ALU.mult, ALU.add))
                step.link(v.tensor_tensor(a0, a0, gateB[:, group(t), :], ALU.mult))
                v.tensor_tensor(x[:, t, :], x[:, t, :], a0, ALU.add).then_inc(combined, 1)

            for c_ in range(MOD1 + 1):
                mod_take(0, c_)
            for n in range(4):
                dve.wait_ge(first_bc_ps, 4 + n + 1)
                v.tensor_copy(shiftB[:, n // 2, n % 2 * SEG:(n % 2 + 1) * SEG], ps[:, n, :]).then_inc(first_shift, 1)
            dve.wait_ge(first_shift, 4)
            dve.wait_ge(first_scale, 4)
            dve.wait_ge(table_in, 16)
            dve.wait_ge(router_in, 32)
            for l in range(LAYERS):
                def norm(which, t):
                    dve.wait_ge(rstd_ready, l * 6 + which * 3 + t + 1)
                    if past(l * 64 + which * 32):
                        dve.wait_ge(bcA_in, l * 64 + which * 32)
                    step.link(v.scalar_tensor_tensor(h[:, t, :], x[:, t, :], stats(R1 + t), scaleB[:, group(t), :],
                                                     ALU.mult, ALU.mult))
                    v.tensor_tensor(h[:, t, :], h[:, t, :], shiftB[:, group(t), :], ALU.add).then_inc(h_ready, 1)

                if l:
                    mod_take(l, MOD1)
                    mod_take(l, MOD1 + 1)
                    combine(l - 1, 0)
                    combine(l - 1, 1)
                norm(0, 0)
                if l:
                    combine(l - 1, 2)
                norm(0, 1)
                norm(0, 2)
                if l == 0:
                    mod_take(l, MOD1 + 1)

                def conv_input(t):
                    proj_wait(dve, l, 1, t)
                    dve.wait_ge(proj_taken, l * 9 + taken(0, t))
                    v.tensor_tensor(h[:, t, 0:CH], ps[:, proj_bank(1, t), :], h[:, t, 0:CH], ALU.mult)\
                        .then_inc(z_ready, 1)

                def tap(part_, k, first=False):
                    o0, n = (CONV_OFF[0], P) if part_ == 0 else (CONV_OFF[1], 2 * P)
                    for m in range(CM):
                        span = zT[:, m, bass.ds(k + o0, n)]
                        w = convw[:, m, bass.ds(k, 1)]
                        out = acc[:, m, part_ * P:part_ * P + n]
                        if first:
                            v.tensor_scalar(out, span, w, convw[:, m, TAPS:TAPS + 1], ALU.mult, ALU.add)\
                                .then_inc(conv_step[part_], 1)
                        else:
                            dve.wait_ge(conv_step[part_], (l * TAPS + k - 1) * CM + m + 1)
                            v.scalar_tensor_tensor(out, span, w, out, ALU.mult, ALU.add).then_inc(conv_step[part_], 1)

                conv_input(0)
                dve.wait_ge(convw_ps, l + 1)
                v.tensor_copy(convw[:, :, :].rearrange("p m k -> p (m k)"), ps[:, 3, 0:P]).then_inc(convw_ready, 1)
                dve.wait_ge(zT_ready, l * 3 + 1)
                dve.wait_ge(pads_set, l * 3 + 3)
                dve.wait_ge(convw_ready, l + 1)
                tap(0, 0, True)
                for k in range(1, TAPS):
                    if k in PROMPT_TAPS:
                        conv_input(PROMPT_TAPS.index(k) + 1)
                    tap(0, k)
                dve.wait_ge(zT_ready, l * 3 + 3)
                tap(1, 0, True)

                def heads(ap, n=10):
                    return ap.rearrange("p (h d) -> p h d", d=HD)

                def table_b(ap, n):
                    return ap.unsqueeze(1).broadcast_to([P, n, HD])

                def rope(t):
                    dve.wait_ge(proj_taken, l * 9 + taken(3, t))
                    if t:
                        dve.wait_ge(rope_ready, l * 3 + t)
                    dve.wait_ge(qk_squared, l * 3 + t + 1)
                    v.tensor_reduce(stats(QKSS, 10), heads(qk_sq[:, t, :]), AX.X, ALU.add).then_inc(qk_ss, 1)
                    tap(1, ROPE_AT[t])
                    dve.wait_ge(qk_rstd, l * 3 + t + 1)
                    step.link(v.tensor_tensor(heads(qk[:, t, :]), heads(qk[:, t, :]),
                                              stats(QKR, 10).unsqueeze(2).broadcast_to([P, 10, HD]), ALU.mult))
                    q, kk = qk[:, t, 0:QW], qk[:, t, QW:QW + KVW]
                    q_out = h[:, t, 0:QW].rearrange("p (j g d) -> p g j d", g=KV_HEADS, d=HD)

                    def grouped(ap):
                        return ap.rearrange("p (g j d) -> p g j d", g=KV_HEADS, d=HD)

                    dve.wait_ge(zT_ps, l * 3 + 3)
                    if t == 0:
                        qg = qkg[:, 0, :].unsqueeze(1).broadcast_to([P, PAIRS, HD])
                        for gg in range(KV_HEADS):
                            v.tensor_tensor(q_out[:, gg], grouped(q)[:, gg], qg, ALU.mult)
                        v.tensor_tensor(heads(kk), heads(kk), table_b(qkg[:, 1, :], 2), ALU.mult).then_inc(rope_ready, 1)
                        return
                    step.mark(v.tensor_tensor(heads(q), heads(q), table_b(qkg[:, 0, :], HEADS), ALU.mult))
                    step.link(v.tensor_tensor(heads(kk), heads(kk), table_b(qkg[:, 1, :], 2), ALU.mult))
                    step.mark(v.tensor_tensor(heads(tmp[:, 0, :]), heads(qk[:, t, :]), table_b(ropeC[:, t - 1, :], 10),
                                              ALU.mult))

                    def axes(ap, half):
                        return ap.rearrange("p (h a s f) -> p h a s f", a=2, s=2, f=16)[:, :, :, half, :]

                    for half in range(2):
                        sin = ropeS[:, t - 1, :].rearrange("p (a s f) -> p a s f", a=2, s=2)[:, :, half, :]
                        ins = v.tensor_tensor(axes(tmp[:, 1, :], half), axes(qk[:, t, :], 1 - half),
                                              sin.unsqueeze(1).broadcast_to([P, 10, 2, 16]), ALU.mult)
                        (step.link if half else step.mark)(ins)
                    for gg in range(KV_HEADS):
                        v.tensor_tensor(q_out[:, gg], grouped(tmp[:, 0, 0:QW])[:, gg], grouped(tmp[:, 1, 0:QW])[:, gg],
                                        ALU.add)
                    v.tensor_tensor(kk, tmp[:, 0, QW:QW + KVW], tmp[:, 1, QW:QW + KVW], ALU.add).then_inc(rope_ready, 1)

                for t in range(TILES):
                    rope(t)
                    if t < 2:
                        tap(1, ROPE_AT[t] + 1)
                mod_take(l, MODN)
                for k in range(LATE_TAPS):
                    tap(1, ROPE_TAPS + k)
                mod_take(l, MODN + 1)

                def score_max(hd):
                    for t in range(TILES):
                        dve.wait_ge(s_ps, (l * HEADS + hd) * TILES + t + 1)
                        v.tensor_reduce(stats(NM + TILES * (hd % 2) + t), ps[:, 4 + t, 0:P * len(KEY_CHUNKS[t])], AX.X,
                                        ALU.max, negate=True).then_inc(nmax, 1)

                def head_output(hd):
                    dve.wait_ge(o_ps, l * HEADS + hd + 1)
                    v.reciprocal(stats(RI, TILES), stats(RS + TILES * (hd % 2), TILES)).then_inc(rinv_ready, 1)
                    dve.wait_ge(rinv_ready, l * HEADS + hd + 1)
                    v.tensor_tensor(h[:, :, hd * HD:(hd + 1) * HD],
                                    ps[:, 7, 0:TILES * HD].rearrange("p (t d) -> p t d", d=HD),
                                    stats(RI, TILES).unsqueeze(2).broadcast_to([P, TILES, HD]), ALU.mult)\
                        .then_inc(attn_out, 1)

                def ln_stats(t):
                    dve.wait_ge(back_ps, l * 3 + t + 1)
                    step.link(v.bn_stats(stats(BN, 6), ps[:, BACK[t], :]))
                    v.bn_aggr(stats(LNV, 2), stats(BN, 6)).then_inc(ln_var, 1)

                def ln_normalize(t):
                    dve.wait_ge(ln_rstd, l * 3 + t + 1)
                    v.tensor_scalar(h[:, t, CH:D], ps[:, BACK[t], :], stats(LNV), stats(LNR), ALU.subtract, ALU.mult)\
                        .then_inc(ln_norm, 1)

                score_max(0)
                for hd in range(HEADS):
                    if 0 < hd < HEADS - 1:
                        score_max(hd + 1)
                    if hd < len(HEAD_TAPS):
                        for n in range(HEAD_TAPS[hd]):
                            tap(1, ROPE_TAPS + LATE_TAPS + sum(HEAD_TAPS[:hd]) + n)
                    if hd == 0:
                        score_max(1)
                    if HEAD_FILL[hd][2] == KD:
                        mod_take(l, HEAD_FILL[hd][0])
                    head_output(hd)
                ln_stats(0)
                ln_normalize(0)
                ln_stats(1)
                ln_normalize(1)
                ln_stats(2)
                ln_normalize(2)

                dve.wait_ge(bcG_in, l * 32 + 16)
                if l == 0:
                    dve.wait_ge(filled_st, 8 * 16)
                for t in range(TILES):
                    for n in range(2):
                        u = 2 * t + n
                        outp_wait(dve, l, n, t)
                        cols = slice(n * SEG, (n + 1) * SEG)
                        if u >= 2:
                            dve.wait_ge(resid, l * 6 + u - 1)
                        step.link(v.tensor_tensor(part[:, u % 2, :], ps[:, out_bank(t, n), :], gateB[:, group(t), cols],
                                                  ALU.mult))
                        v.tensor_tensor(x[:, t, cols], x[:, t, cols], part[:, u % 2, :], ALU.add).then_inc(resid, 1)
                    norm(1, t)

                o = 0

                def cutr(n):
                    nonlocal o
                    o += n
                    return rt[:, o - n:o]

                NE, NG = TILES * E, TILES * GROUPS
                gt, eq = cutr(NG * 16), cutr(NG * 16)
                sb_, rank, top, sel, pm, hi, lo, sw = (cutr(NE) for _ in range(8))
                gs, grank, gsel = cutr(NG), cutr(NG), cutr(NG)
                pmax, psum, wsum, wr_ = (cutr(TILES) for _ in range(4))
                s_flat = route[:, :, :].rearrange("p t e -> p (t e)")

                def by_tile(ap):
                    return ap.rearrange("p (t e) -> p t e", t=TILES)

                def beats(out_gt, out_eq, scores, n, m):
                    sv = scores.rearrange("p (n m) -> p n m", m=m)
                    mine = sv.unsqueeze(3).broadcast_to([P, n, m, m])
                    other = sv.unsqueeze(2).broadcast_to([P, n, m, m])
                    ov = [a_[:, 0:n * m * m].rearrange("p (n i j) -> p n i j", i=m, j=m) for a_ in (out_gt, out_eq)]
                    before = tie.rearrange("p (i j) -> p i j", i=m).unsqueeze(1).broadcast_to([P, n, m, m])
                    step.mark(v.tensor_tensor(ov[0], other, mine, ALU.is_gt))
                    step.link(v.tensor_tensor(ov[1], other, mine, ALU.is_equal))
                    step.link(v.tensor_tensor(ov[1], ov[1], before, ALU.mult))
                    step.link(v.tensor_tensor(out_gt[:, 0:n * m * m], out_gt[:, 0:n * m * m], out_eq[:, 0:n * m * m],
                                              ALU.add))
                    return out_gt[:, 0:n * m * m].rearrange("p (n j) -> p n j", j=m)

                dve.wait_ge(score_ready, l * 3 + 3)
                step.link(v.tensor_tensor(by_tile(sb_), route[:, :, :], br[:, :].unsqueeze(1).broadcast_to([P, TILES, E]),
                                          ALU.add))
                step.link(v.tensor_reduce(rank, beats(gt, eq, sb_, NG, EPG), AX.X, ALU.add))
                step.link(v.tensor_scalar(top, rank, 2.0, None, ALU.is_lt))
                step.link(v.tensor_tensor(pm, top, sb_, ALU.mult))
                step.link(v.tensor_reduce(gs, pm.rearrange("p (n m) -> p n m", m=EPG), AX.X, ALU.add))
                step.link(v.tensor_reduce(grank, beats(gt, eq, gs, TILES, GROUPS), AX.X, ALU.add))
                step.link(v.tensor_scalar(gsel, grank, 1.0, None, ALU.is_lt))
                v.tensor_tensor(sel.rearrange("p (n m) -> p n m", m=EPG), top.rearrange("p (n m) -> p n m", m=EPG),
                                gsel.unsqueeze(2).broadcast_to([P, NG, EPG]), ALU.mult).then_inc(sel_ready, 1)
                dve.wait_ge(pos_ps, l + 1)
                step.link(v.tensor_tensor(by_tile(pm), by_tile(ps[:, 5, 0:NE]),
                                          slot_base.unsqueeze(1).broadcast_to([P, TILES, E]), ALU.add))
                step.link(v.tensor_tensor(pm, pm, sel, ALU.mult))
                step.mark(v.tensor_reduce(pmax, by_tile(pm), AX.X, ALU.max))
                step.link(v.tensor_reduce(psum, by_tile(pm), AX.X, ALU.add))
                step.link(v.tensor_tensor(psum, psum, pmax, ALU.subtract))
                pick_v = pick[:, :].rearrange("p (t n) -> p t n", n=2)
                v.tensor_copy(pick_v[:, :, 0], psum)
                v.tensor_copy(pick_v[:, :, 1], pmax)
                v.tensor_copy(count[0:1, :], ps[0:1, 5, NE:NE + E]).then_inc(pos_ready, 1)
                mod_take(l, MOD2)
                step.mark(v.tensor_tensor(by_tile(hi), by_tile(pm), pmax.unsqueeze(2).broadcast_to([P, TILES, E]),
                                          ALU.is_equal))
                step.link(v.tensor_tensor(sw, s_flat, sel, ALU.mult))
                step.link(v.tensor_reduce(wsum, by_tile(sw), AX.X, ALU.add))
                step.mark(v.reciprocal(wr_, wsum))
                step.link(v.tensor_tensor(lo, sel, hi, ALU.subtract))
                step.mark(v.tensor_tensor(lo, lo, sw, ALU.mult))
                step.link(v.tensor_tensor(hi, hi, sw, ALU.mult))
                step.mark(v.tensor_reduce(psum, by_tile(lo), AX.X, ALU.add))
                step.link(v.tensor_reduce(pmax, by_tile(hi), AX.X, ALU.add))
                step.mark(v.tensor_tensor(gates[:, :, 0], psum, wr_, ALU.mult))
                step.link(v.tensor_tensor(gates[:, :, 1], pmax, wr_, ALU.mult))
                if l + 1 < LAYERS:
                    mod_take(l, MOD2 + 1)
                    mod_take(l + 1, 0)
                dve.wait_ge(slots_ps, l + 1)
                v.tensor_copy(slot_tok[:, :], ps[:, 6, 0:E * TILES]).then_inc(slots_ready, 1)
                if l + 1 < LAYERS:
                    for c_ in range(1, MOD1):
                        mod_take(l + 1, c_)
                else:
                    mod_take(l, MOD2 + 1)
                dve.wait_ge(pos_ready, l + 1)

                def take_xT(e):
                    for n in range(2):
                        dve.wait_ge(xT_ps, (l * E + e) * 2 + n + 1)
                        ins = v.tensor_copy(xsT[:, n * 512:(n + 1) * 512], ps[:, XT + n, :])
                    ins.then_inc(xsT_ready, 1)

                def expert(i, j, last):
                    e = i * 2 + j
                    dve.wait_ge(sig_ready, l * E + e + 1)
                    v.tensor_tensor(hid, ps[:, GATE, :], hid, ALU.mult).then_inc(silu_ready, 1)
                    dve.wait_ge(silu_ready, l * E + e + 1)
                    dve.wait_ge(up_ps, l * E + e + 1)
                    v.tensor_tensor(hid, ps[:, UP, :], hid, ALU.mult).then_inc(hid_ready, 1)

                    def run(t, at):
                        if past(at * 16):
                            dve.wait_ge(ov_st, at * 16)
                        for n in range(2):
                            dve.wait_ge(ov_xT, at * 2 + n + 1)
                            ins = v.tensor_copy(ov_b[:, n * 512:(n + 1) * 512], ps[:, XT + n, :])
                        ins.then_inc(ov_xsT, 1)
                        dve.wait_ge(ov_sig, at + 1)
                        v.tensor_tensor(ov_a[:, 0:FF], ps[:, GATE, :], ov_a[:, 0:FF], ALU.mult).then_inc(ov_silu, 1)
                        dve.wait_ge(ov_silu, at + 1)
                        dve.wait_ge(ov_up, at + 1)
                        v.tensor_tensor(ov_a[:, 0:FF], ps[:, UP, :], ov_a[:, 0:FF], ALU.mult).then_inc(ov_hid, 1)
                        dve.wait_ge(ov_hT, at + 1)
                        v.tensor_copy(ov_hidT, ps[:, HT, :]).then_inc(ov_hidT_ready, 1)

                    overflow(dve, l, e, run, ((ov_xsT, 1), (ov_silu, 1), (ov_hid, 1), (ov_hidT_ready, 1)))
                    if not last:
                        take_xT(e + 1)
                    dve.wait_ge(hidT_ps, l * E + e + 1)
                    v.tensor_copy(hidT, ps[:, HT, :]).then_inc(hidT_ready, 1)

                take_xT(0)
                expert(0, 0, False)
                expert(0, 1, False)
                with dve.Fori(1, E // 2 - 1) as i:
                    expert(i, 0, False)
                    expert(i, 1, False)
                expert(E // 2 - 1, 0, False)
                expert(E // 2 - 1, 1, True)
            for t in range(TILES):
                combine(LAYERS - 1, t)

        @block.tensor
        def _(pe):
            pe.wait_ge(cs_ready, 1)

            def accumulate(out, stationary, moving, n):
                for k in range(n):
                    mm = pe.matmul(out, stationary(k), moving(k), start=(k == 0), stop=(k == n - 1))
                return mm

            def loaded(n):
                pe.wait_ge(slot_loaded[slot_of(n)], uses(n) * 16)

            def modulation(l, c, k0=0, k1=KD):
                n = mod_item(l, c)
                if k1 <= KD // 2 and n == 0:
                    pe.wait_ge(first_half, 16)
                elif k0 == 0 or n == 0:
                    loaded(n)
                for k in range(k0, k1):
                    mm = pe.matmul(ps[0:2, mod_bank(l, c), :], cs[:, :, k], slot_w(slot_of(n))[:, k, :],
                                   start=(k == 0), stop=(k == KD - 1))
                if k1 == KD:
                    mm.then_inc(slot_used[slot_of(n)], 1)

            modulation(0, 0, 0, KD // 2)
            modulation(0, 0, KD // 2, KD)
            for c_ in range(1, MOD1):
                modulation(0, c_)
            modulation(0, MOD1)
            pe.wait_ge(table_in, 16)
            pe.wait_ge(mod_done, 1)
            for first, banks in ((2, (5, 6, 7, mod_bank(0, MOD1))), (0, (0, 1, 2, 3))):
                for n in range(4):
                    if banks[n] == mod_bank(0, MOD1):
                        pe.wait_ge(mod_taken, MOD1 + 1)
                    c_ = first + n % 2
                    pe.matmul(ps[:, banks[n], :], ident[0:2, n // 2:n // 2 + 1].broadcast_to([2, P]),
                              rowA[:, c_ * SEG:(c_ + 1) * SEG], start=True, stop=True).then_inc(first_bc_ps, 1)
            pe.wait_ge(first_scale, 3)
            modulation(0, MOD1 + 1, 0, KD // 2)
            pe.wait_ge(router_in, 32)
            for l in range(LAYERS):
                if l:
                    modulation(l, MOD1)
                    modulation(l, MOD1 + 1)
                    pe.wait_ge(y_taken, l * E)
                def transposed(which, t):
                    for n in range(2 * t, 2 * t + 2):
                        if n >= 4:
                            pe.wait_ge(hT_ready, l * 18 + which * 6 + n - 3)
                        for m in range(4):
                            k = 4 * (n % 2) + m
                            mm = pe.transpose(ps[:, n % 4, m * P:(m + 1) * P], h[:, t, k::KD], ident)
                        mm.then_inc(hT_ps, 1)

                def hT_wait(which, t):
                    pe.wait_ge(hT_ready, l * 18 + which * 6 + 2 * t + 2)

                for t in range(TILES):
                    pe.wait_ge(h_ready, l * 6 + t + 1)
                    transposed(0, t)
                    if l == 0 and t == 0:
                        modulation(l, MOD1 + 1, KD // 2, KD)


                def project(c, t, n=SEG):
                    i = PROJ.index((c, t))
                    s = slot_of(IN_AT[l] + c)
                    hT_wait(0, t)
                    loaded(IN_AT[l] + c)
                    if proj_bank(c, t) == 7 and i < 4:
                        pe.wait_ge(mod_taken, l * MODC + MODN)
                    if i >= 4:
                        pc, pt = PROJ[i - 4]
                        if pc == 1:
                            pe.wait_ge(z_ready, l * 3 + pt + 1)
                        else:
                            pe.wait_ge(proj_taken, l * 9 + taken(pc, pt))
                    mm = accumulate(ps[:, proj_bank(c, t), 0:n], lambda k: hT[:, t, k, :],
                                    lambda k: slot_w(s, n)[:, k, :], KD)
                    mm.then_inc(*((proj_ps, 1) if t < 2 else (slot_used[s], 1)))

                def z_transposed(t):
                    pe.wait_ge(z_ready, l * 3 + t + 1)
                    for m in range(CM):
                        mm = pe.transpose(ps[:, t, m * P:(m + 1) * P], h[:, t, m * P:(m + 1) * P], ident)
                    mm.then_inc(zT_ps, 1)

                for i_, (c_, t_) in enumerate(PROJ):
                    project(c_, t_, 2 * KVW if c_ == 3 else SEG)
                    if i_ == 2:
                        hT_wait(0, 2)
                        pe.wait_ge(small_in, (l + 1) * 128)
                        for m in range(CM):
                            mm = pe.transpose(ps[:, 3, m * (TAPS + 1):(m + 1) * (TAPS + 1)], sg[0:TAPS + 1, m * P:(m + 1) * P],
                                              ident[0:TAPS + 1, 0:TAPS + 1])
                        mm.then_inc(convw_ps, 1)
                        z_transposed(0)
                    if i_ == 6:
                        z_transposed(1)
                        z_transposed(2)

                pe.wait_ge(zT_ready, l * 3 + 3)
                modulation(l, MODN, 0, KD // 2)
                pe.wait_ge(proj_taken, l * 9 + 9)
                pe.transpose(ps[:, 7, P:2 * P], ck, ident)
                for t in range(TILES):
                    pe.wait_ge(rope_ready, l * 3 + t + 1)
                    for j in range(PAIRS):
                        mm = pe.transpose(ps[:, 4 + t, j * P:(j + 1) * P], h[:, t, j * P:(j + 1) * P], ident)
                    mm.then_inc(qkT_ps, 1)
                    mm = pe.transpose(ps[:, 7, V_CHUNK[t] * P:(V_CHUNK[t] + 1) * P], qk[:, t, QW:QW + KVW], ident)
                    if t == 2:
                        mm.then_inc(qkT_ps, 1)
                    c, k0 = ((MODN, KD // 2), (MODN + 1, 0), (MODN + 1, KD // 2))[t]
                    modulation(l, c, k0, k0 + KD // 2)

                def scores(hd, t):
                    g_, j = hd // PAIRS, hd % PAIRS
                    ks = KEY_CHUNKS[t]
                    pe.matmul(ps[:, 4 + t, 0:P * len(ks)], qT[g_ * HD:(g_ + 1) * HD, t, j * P:(j + 1) * P],
                              kT[g_ * HD:(g_ + 1) * HD, ks[0] * P:(ks[-1] + 1) * P], start=True, stop=True).then_inc(s_ps, 1)

                def conv_back(t):
                    if t == 0:
                        for step_ in conv_step:
                            pe.wait_ge(step_, (l + 1) * (TAPS * CM))
                    if t == 2:
                        pe.wait_ge(attn_out, (l + 1) * HEADS)
                    for m in range(CM):
                        mm = pe.transpose(ps[:, BACK[t], m * P:(m + 1) * P], acc[:, m, t * P:(t + 1) * P], ident)
                    mm.then_inc(back_ps, 1)

                pe.wait_ge(qkT_ready, l * 4 + 4)
                for t in range(TILES):
                    scores(0, t)
                for hd in range(HEADS):
                    u = l * (HEADS * TILES) + hd * TILES
                    for t in range(TILES):
                        pe.wait_ge(exp_done, u + t + 1)
                        if hd == 0 and t == 0:
                            pe.wait_ge(mod_taken, l * MODC + 2 * MOD1)
                        for n in range(len(KEY_CHUNKS[t])):
                            mm = pe.transpose(ps[:, 1 + t, n * P:(n + 1) * P], prob[:, t, n * P:(n + 1) * P], ident)
                        mm.then_inc(t_ps, 1)
                        if hd + 1 < HEADS:
                            scores(hd + 1, t)
                    c, k0, k1 = HEAD_FILL[hd]
                    if k0 == 0 and c > 8:
                        pe.wait_ge(mod_taken, l * MODC + c)
                    modulation(l, c, k0, k1)
                    if hd:
                        pe.wait_ge(attn_out, l * HEADS + hd)
                    for t in range(TILES):
                        pe.wait_ge(probT_ready, u + t + 1)
                        g_ = hd // PAIRS
                        ks = KEY_CHUNKS[t]
                        mm = accumulate(ps[:, 7, t * HD:(t + 1) * HD], lambda n: probT[:, t, n * P:(n + 1) * P],
                                   lambda n: vall[:, ks[n], g_ * HD:(g_ + 1) * HD], len(ks))
                    mm.then_inc(o_ps, 1)

                for t in range(TILES):
                    conv_back(t)

                def mix_transposed(t, half):
                    n = 3 * half + t
                    if half:
                        pe.wait_ge(mix_ready, l * 3 + t + 1)
                    if n == 0:
                        pe.wait_ge(mod_taken, l * MODC + MOD2)
                    if n == 3:
                        pe.wait_ge(ln_norm, l * 3 + 2)
                    if n >= 4:
                        pe.wait_ge(hT_ready, l * 18 + 6 + n - 3)
                    for m in range(4):
                        k = 4 * half + m
                        mm = pe.transpose(ps[:, n % 4, m * P:(m + 1) * P], h[:, t, k * P:(k + 1) * P], ident)
                    mm.then_inc(hT_ps, 1)

                def project_out(t, n, half):
                    u = 2 * t + n
                    s = slot_of(OUT_AT[l] + n)
                    pe.wait_ge(hT_ready, l * 18 + 6 + 3 * half + t + 1)
                    if half == 0:
                        loaded(OUT_AT[l] + n)
                        if u in (2, 3):
                            pe.wait_ge(ln_norm, l * 3 + {2: 1, 3: 3}[u])
                        if u >= 4:
                            pe.wait_ge(resid, l * 6 + u - 3)
                    for k in range(4 * half, 4 * half + 4):
                        mm = pe.matmul(ps[:, out_bank(t, n), :], hT[:, t, k, :], slot_w(s)[:, k, :],
                                       start=(k == 0), stop=(k == KD - 1))
                    if half:
                        mm.then_inc(*((outp_ps, 1) if t < 2 else (slot_used[s], 1)))

                def h2_transposed(t):
                    pe.wait_ge(h_ready, l * 6 + 3 + t + 1)
                    transposed(2, t)

                def router(t):
                    hT_wait(2, t)
                    if t < 2:
                        pe.wait_ge(resid, l * 6 + 3 + t)
                    else:
                        pe.wait_ge(score_ready, l * 3 + 1)
                    accumulate(ps[:, LOGITS[t], 0:E], lambda k: hT[:, t, k, :], lambda k: wr[:, k, :], KD)\
                        .then_inc(logit_ps, 1)

                for t in range(TILES):
                    mix_transposed(t, 0)
                project_out(0, 0, 0)
                project_out(0, 1, 0)
                project_out(1, 0, 0)
                mix_transposed(0, 1)
                project_out(0, 0, 1)
                mix_transposed(1, 1)
                project_out(0, 1, 1)
                project_out(1, 0, 1)
                mix_transposed(2, 1)
                project_out(1, 1, 0)
                project_out(1, 1, 1)
                project_out(2, 0, 0)
                project_out(2, 0, 1)
                h2_transposed(0)
                project_out(2, 1, 0)
                project_out(2, 1, 1)
                router(0)
                h2_transposed(1)
                router(1)
                h2_transposed(2)
                router(2)

                modulation(l, MOD2, 0, KD // 2)
                pe.wait_ge(sel_ready, l + 1)
                for t in range(TILES):
                    accumulate(ps[:, 5, t * E:(t + 1) * E], lambda k: ones if k < t else tri,
                               lambda k: sel_all[:, k * E:(k + 1) * E], t + 1)
                accumulate(ps[:, 5, TILES * E:(TILES + 1) * E], lambda k: ones,
                           lambda k: sel_all[:, k * E:(k + 1) * E], TILES).then_inc(pos_ps, 1)
                modulation(l, MOD2, KD // 2, KD)
                if l + 1 < LAYERS:
                    modulation(l, MOD2 + 1)
                    modulation(l + 1, 0)
                else:
                    modulation(l, MOD2 + 1, 0, KD // 2)
                pe.wait_ge(slots_in, (l + 1) * 16)
                pe.transpose(ps[:, 6, 0:E * TILES], slot_rows_sb[:, :], ident[0:E * TILES, 0:E * TILES]).then_inc(slots_ps, 1)
                if l + 1 < LAYERS:
                    for c_ in range(1, MOD1):
                        pe.wait_ge(mod_taken, (l + 1) * MODC - 2 + c_)
                        modulation(l + 1, c_)
                else:
                    modulation(l, MOD2 + 1, KD // 2, KD)
                pe.wait_ge(pos_ready, l + 1)

                def expert_slot(j, m):
                    return slot_of(EXP_AT[l] + 3 * j + m)

                def expert_loaded(i, j, m):
                    pe.wait_ge(slot_loaded[expert_slot(j, m)], (i + uses(EXP_AT[l] + 3 * j + m)) * 16)

                def token_transposes(rows, s):
                    for n in range(2):
                        for m in range(4):
                            mm = pe.transpose(ps[:, XT + n, m * P:(m + 1) * P], rows[:, 4 * n + m::KD], ident)
                        mm.then_inc(s, 1)

                def xT(e, i, j):
                    pe.wait_ge(gathered[j], (l * (E // 2) + i + 1) * 16)
                    token_transposes(xs[:, j, :], xT_ps)

                def gate_up(bank, s, src):
                    return accumulate(ps[:, bank, :], lambda k: src[:, k * P:(k + 1) * P],
                                      lambda k: slot_w(s)[:, k, :], KD)

                def hidden_transposes(rows):
                    for k in range(KF):
                        mm = pe.transpose(ps[:, HT, k * P:(k + 1) * P], rows[:, k:FF:KF], ident)
                    return mm

                def down(s, src, n):
                    w = ring[:, s, 0:KF * D].rearrange("p (k n) -> p k n", k=KF)
                    return accumulate(ps[:, YB + n, :], lambda k: src[:, k * P:(k + 1) * P],
                                      lambda k: w[:, k, n * SEG:(n + 1) * SEG], KF)

                def down_main(k, i, j):
                    s = expert_slot(j, 2)
                    pe.wait_ge(hidT_ready, l * E + k + 1)
                    if past(l * E + k):
                        pe.wait_ge(y_taken, l * E + k)
                    expert_loaded(i, j, 2)
                    down(s, hidT, 0).then_inc(y0_ps, 1)
                    down(s, hidT, 1).then_inc(slot_used[s], 1)

                def release(s):
                    pe.matmul(ps[0:1, 7, 0:1], ones[:, 0:1], ones[:, 0:1], start=True, stop=True).then_inc(slot_used[s], 1)

                def expert(i, j, first, last):
                    e = i * 2 + j
                    g0 = l * E + e
                    pe.wait_ge(xsT_ready, g0 + 1)
                    if past(g0):
                        pe.wait_ge(hid_ready, g0)
                    expert_loaded(i, j, 0)
                    gate_up(GATE, expert_slot(j, 0), xsT).then_inc(gate_ps, 1)
                    expert_loaded(i, j, 1)
                    gate_up(UP, expert_slot(j, 1), xsT).then_inc(up_ps, 1)

                    def run(t, at):
                        pe.wait_ge(ov_gathered, at + 1)
                        token_transposes(ov_a, ov_xT)
                        pe.wait_ge(ov_xsT, at + 1)
                        pe.wait_ge(hid_ready, g0 + 1)
                        gate_up(GATE, expert_slot(j, 0), ov_b).then_inc(ov_gate, 1)
                        gate_up(UP, expert_slot(j, 1), ov_b).then_inc(ov_up, 1)
                        pe.wait_ge(ov_hid, at + 1)
                        if past(g0):
                            pe.wait_ge(hidT_ready, g0)
                        hidden_transposes(ov_a).then_inc(ov_hT, 1)
                        pe.wait_ge(ov_hidT_ready, at + 1)
                        if past(g0 if first else g0 - 1):
                            pe.wait_ge(y_taken, g0 if first else g0 - 1)
                        expert_loaded(i, j, 2)
                        down(expert_slot(j, 2), ov_hidT, 0)
                        down(expert_slot(j, 2), ov_hidT, 1).then_inc(ov_y, 1)
                        pe.wait_ge(ov_taken, at + 1)

                    overflow(pe, l, e, run, ((ov_xT, 2), (ov_gate, 1), (ov_up, 1), (ov_hT, 1), (ov_y, 1)))
                    release(expert_slot(j, 0))
                    release(expert_slot(j, 1))
                    if not last:
                        xT(e + 1, i + j, 1 - j)
                    if not first:
                        if j:
                            down_main(e - 1, i, 0)
                        else:
                            down_main(e - 1, i - 1, 1)
                    pe.wait_ge(hid_ready, g0 + 1)
                    hidden_transposes(hid).then_inc(hidT_ps, 1)

                pe.wait_ge(mod_taken, (l + 1) * MODC + (MOD1 if l + 1 < LAYERS else 0))
                xT(0, 0, 0)
                expert(0, 0, True, False)
                expert(0, 1, False, False)
                with pe.Fori(1, E // 2 - 1) as i:
                    expert(i, 0, False, False)
                    expert(i, 1, False, False)
                expert(E // 2 - 1, 0, False, False)
                expert(E // 2 - 1, 1, False, True)
                down_main(E - 1, E // 2 - 1, 1)


_INS = ['x_prompt', 'x_sample', 'cache_k', 'cache_v', 'c', 'c_ctx', 'w_mod', 'b_mod', 'norm1_g', 'norm2_g', 'w_in',
        'q_norm_g', 'k_norm_g', 'conv_dw_w', 'conv_dw_b', 'conv_ln_g', 'conv_ln_b', 'w_out', 'w_router', 'b_router',
        'w_gate', 'w_up', 'w_down']
_OUTS = [(1, 128, 1024), (1, 256, 1024), (1, 2, 128, 2, 64), (1, 2, 128, 2, 64)]


def _table():
    import numpy as np
    p = np.arange(P)
    freqs = (np.float32(10000.0) ** (-np.arange(16, dtype=np.float32) / 16)).astype(np.float32)
    cos, sin = [], []
    for t in range(2):
        n = t * P + p
        ang = np.stack([(n // 64).astype(np.float32)[:, None] * freqs, (n % 64).astype(np.float32)[:, None] * freqs], 1)
        cos.append(np.stack([np.cos(ang), np.cos(ang)], 2).reshape(P, HD))
        sin.append(np.stack([-np.sin(ang), np.sin(ang)], 2).reshape(P, HD))
    i4 = np.arange(4)
    tie = (i4[None, :] < i4[:, None]).astype(np.float32).reshape(1, 16)
    parts = [np.eye(P), (p[:, None] < p[None, :]), np.ones((P, P)), *cos, *sin, np.tile(tie, (P, 1)),
             np.tile(np.arange(E)[None] * CAP, (P, 1)), p[:, None] + P * np.arange(TILES)[None]]
    return np.ascontiguousarray(np.concatenate([a.astype(np.float32) for a in parts], 1))


def kernel(**inputs):
    import numpy as _np
    import concourse.bacc as _bacc
    from concourse.bass_utils import run_bass_kernel_spmd as _run

    nc = _bacc.Bacc("TRN2", target_bir_lowering=False, num_devices=1)
    arrays, args = {}, []
    for name in _INS + ['table']:
        a = _table() if name == 'table' else _np.ascontiguousarray(inputs[name])
        arrays[f"in_{name}_dram"] = a
        args.append(nc.dram_tensor(f"in_{name}_dram", a.shape, mybir.dt.from_np(a.dtype), kind="ExternalInput").ap())
    for i, shape in enumerate(_OUTS):
        args.append(nc.dram_tensor(f"out_{i}_dram", shape, F32, kind="ExternalOutput").ap())
    build(nc, *args)
    r = _run(nc, [arrays], core_ids=[0])
    return tuple(r.results[0][f"out_{i}_dram"] for i in range(len(_OUTS)))
```
